# Optimizing a Trainium2 kernel written in Bass

```python
import jax, jax.numpy as jnp
from jax import lax
import numpy as np
import math

D_MODEL = 1024
BATCH = 1
SEQ = 256
DEPTH = 1

GRID_W = 64
CTX_LEN = 256
EPS = 1e-6
N_MOD = 6
SGU_WIDTH = 1024
SGU_CHUNK = 128
SGU_GROUPS = 8
SGU_GROUP_DIM = SGU_WIDTH // SGU_GROUPS
GLA_HEADS = 4
GLA_KEY_DIM = D_MODEL // 2
GLA_VAL_DIM = D_MODEL
GLA_HEAD_K = GLA_KEY_DIM // GLA_HEADS
GLA_HEAD_V = GLA_VAL_DIM // GLA_HEADS
GLA_RANK = 16
GLA_GATE_NORMALIZER = 16.0
GLA_CHUNK = 64
D_FF = 2816
CONV_K = 3

IN_SPLITS = (SGU_WIDTH, SGU_WIDTH, GLA_KEY_DIM, GLA_VAL_DIM, D_MODEL, D_MODEL, GLA_KEY_DIM, GLA_VAL_DIM, 2 * GLA_RANK)
D_IN = sum(IN_SPLITS)
OFF_KVG = sum(IN_SPLITS[:6])


def _split(z, sizes):
    offs = [int(o) for o in np.cumsum(sizes)[:-1]]
    return jnp.split(z, offs, axis=-1)

def _rms_norm(x, g):
    xf = x.astype(jnp.float32)
    y = xf * lax.rsqrt(jnp.mean(xf * xf, axis=-1, keepdims=True) + EPS)
    return (y * g.astype(jnp.float32)).astype(x.dtype)

def _layer_norm(x, g, b):
    xf = x.astype(jnp.float32)
    mu = jnp.mean(xf, axis=-1, keepdims=True)
    var = jnp.mean(jnp.square(xf - mu), axis=-1, keepdims=True)
    y = (xf - mu) * lax.rsqrt(var + EPS)
    return (y * g.astype(jnp.float32) + b.astype(jnp.float32)).astype(x.dtype)

def _modulate(h, shift, scale):
    return h * (1 + scale) + shift

def _spatial_gating(u, vs, ln_g, ln_b, w_s, b_s):
    bsz, length, _ = u.shape
    n = length // SGU_CHUNK
    vn = _layer_norm(vs, ln_g, ln_b).reshape(bsz, n, SGU_CHUNK, SGU_GROUPS, SGU_GROUP_DIM)
    s = jnp.einsum('gpq,bnqgc->bnpgc', w_s, vn) + b_s.T[:, :, None]
    return u * s.reshape(bsz, length, SGU_WIDTH)

def _heads(a, hd):
    return a.reshape(a.shape[0], a.shape[1], GLA_HEADS, hd).astype(jnp.float32)

def _log_decay(lr, w2, b2):
    z = (lr @ w2 + b2).astype(jnp.float32)
    la = jax.nn.log_sigmoid(z) / GLA_GATE_NORMALIZER
    return la.reshape(lr.shape[0], lr.shape[1], GLA_HEADS, GLA_HEAD_K)

def _gla_direction(q, k, v, log_a, s0):
    bsz, t, h, _ = k.shape
    n = t // GLA_CHUNK

    def chunks(a):
        return a.reshape(bsz, n, GLA_CHUNK, h, a.shape[-1])

    k, v, log_a = chunks(k), chunks(v), chunks(log_a)
    b = jnp.cumsum(log_a, axis=2)
    b_last = b[:, :, -1:]
    k_dec = k * jnp.exp(b_last - b)
    cm = lambda a: jnp.moveaxis(a, 1, 0)
    xs_state = (cm(k_dec), cm(v), cm(jnp.exp(b_last[:, :, 0])))

    if q is None:
        def step_state(s, xs):
            kd, vv, dec = xs
            return dec[..., None] * s + jnp.einsum('bchk,bchv->bhkv', kd, vv), None
        s_final, _ = lax.scan(step_state, s0, xs_state)
        return None, s_final

    q = chunks(q)
    q_dec = q * jnp.exp(b)
    k_inv = k * jnp.exp(-b)
    mask = jnp.tril(jnp.ones((GLA_CHUNK, GLA_CHUNK), dtype=bool))
    scores = jnp.where(mask, jnp.einsum('bnchk,bnshk->bnhcs', q_dec, k_inv), 0.0)
    o_intra = jnp.einsum('bnhcs,bnshv->bnchv', scores, v)

    def step(s, xs):
        qd, kd, vv, dec = xs
        o = jnp.einsum('bchk,bhkv->bchv', qd, s)
        return dec[..., None] * s + jnp.einsum('bchk,bchv->bhkv', kd, vv), o

    s_final, o_inter = lax.scan(step, s0, (cm(q_dec),) + xs_state)
    o = o_intra + jnp.moveaxis(o_inter, 0, 1)
    return o.reshape(bsz, t, h, -1), s_final

def _gla_bidir(q, k, v, lr, w2, b2, s0f, s0b):
    la_f = _log_decay(lr[..., :GLA_RANK], w2[0], b2[0])
    la_b = _log_decay(lr[..., GLA_RANK:], w2[1], b2[1])
    flip = lambda a: None if a is None else a[:, ::-1]
    o_f, s_f = _gla_direction(q, k, v, la_f, s0f)
    o_b, s_b = _gla_direction(flip(q), flip(k), flip(v), flip(la_b), s0b)
    o = None if q is None else o_f + flip(o_b)
    return o, s_f, s_b

def _token_mixer(h, w_in, sgu_ln_g, sgu_ln_b, sgu_w, sgu_b, gla_w2, gla_b2, gla_norm_g,
                 w_br_a, w_br_b, w_o, s0f, s0b):
    z = h @ w_in
    u, vs, q, r, ga, gb, k, v, lr = _split(z, IN_SPLITS)
    a = _spatial_gating(jax.nn.gelu(u, approximate=False), jax.nn.gelu(vs, approximate=False),
                        sgu_ln_g, sgu_ln_b, sgu_w, sgu_b)
    qh = _heads(q, GLA_HEAD_K) * (GLA_HEAD_K ** -0.5)
    o, s_f, s_b = _gla_bidir(qh, _heads(k, GLA_HEAD_K), _heads(v, GLA_HEAD_V), lr, gla_w2, gla_b2, s0f, s0b)
    o = o * lax.rsqrt(jnp.mean(o * o, axis=-1, keepdims=True) + EPS)
    o = o.reshape(h.shape[0], h.shape[1], GLA_VAL_DIM) * gla_norm_g.astype(jnp.float32)
    ob = o.astype(h.dtype) * jax.nn.silu(r)
    merged = jax.nn.sigmoid(ga) * (a @ w_br_a) + jax.nn.sigmoid(gb) * (ob @ w_br_b)
    return merged @ w_o, s_f, s_b

def _context_states(hc, w_in, gla_w2, gla_b2, s0):
    k, v, lr = _split(hc @ w_in[:, OFF_KVG:], IN_SPLITS[6:])
    _, s_f, s_b = _gla_bidir(None, _heads(k, GLA_HEAD_K), _heads(v, GLA_HEAD_V), lr, gla_w2, gla_b2, s0, s0)
    return s_f, s_b

def _conv_ffn(h, rows, w_up, conv_w, conv_b, w_down):
    bsz, length, _ = h.shape
    a, val = _split(h @ w_up, (D_FF, D_FF))
    img = a.reshape(bsz, rows, length // rows, D_FF)
    a = lax.conv_general_dilated(img, conv_w[:, :, None, :], (1, 1), 'SAME',
                                 dimension_numbers=('NHWC', 'HWIO', 'NHWC'),
                                 feature_group_count=D_FF) + conv_b
    return (jax.nn.gelu(a.reshape(bsz, length, D_FF), approximate=False) * val) @ w_down

def first_inputs(seed: int = 0) -> dict:
    key = jax.random.key(seed)
    ks = jax.random.split(key, 32)

    def nrm(k, shape, scale):
        return jax.random.normal(k, shape, jnp.float32) * scale

    def gain(k, shape):
        return 1.0 + nrm(k, shape, 0.1)

    D = D_MODEL
    return {
        "x": nrm(ks[0], (BATCH, SEQ, D), 1.0),
        "c": nrm(ks[1], (BATCH, D), 1.0),
        "ctx": nrm(ks[2], (BATCH, CTX_LEN, D), 1.0),
        "c_ctx": nrm(ks[3], (D,), 1.0),
        "w_ada": nrm(ks[4], (DEPTH, D, N_MOD * D), 0.5 * D ** -0.5),
        "b_ada": nrm(ks[5], (DEPTH, N_MOD * D), 0.01),
        "norm1_g": gain(ks[6], (DEPTH, D)),
        "norm2_g": gain(ks[7], (DEPTH, D)),
        "w_in": nrm(ks[8], (DEPTH, D, D_IN), D ** -0.5),
        "sgu_ln_g": gain(ks[9], (DEPTH, SGU_WIDTH)),
        "sgu_ln_b": nrm(ks[10], (DEPTH, SGU_WIDTH), 0.01),
        "sgu_w": nrm(ks[11], (DEPTH, SGU_GROUPS, SGU_CHUNK, SGU_CHUNK), 0.5 * SGU_CHUNK ** -0.5),
        "sgu_b": gain(ks[12], (DEPTH, SGU_GROUPS, SGU_CHUNK)),
        "gla_w2": nrm(ks[13], (DEPTH, 2, GLA_RANK, GLA_KEY_DIM), GLA_RANK ** -0.5),
        "gla_b2": nrm(ks[14], (DEPTH, 2, GLA_KEY_DIM), 0.1),
        "gla_norm_g": gain(ks[15], (DEPTH, GLA_VAL_DIM)),
        "w_br_a": nrm(ks[16], (DEPTH, SGU_WIDTH, D), SGU_WIDTH ** -0.5),
        "w_br_b": nrm(ks[17], (DEPTH, GLA_VAL_DIM, D), GLA_VAL_DIM ** -0.5),
        "w_o": nrm(ks[18], (DEPTH, D, D), D ** -0.5),
        "ffn_w_up": nrm(ks[19], (DEPTH, D, 2 * D_FF), D ** -0.5),
        "ffn_conv_w": nrm(ks[20], (DEPTH, CONV_K, CONV_K, D_FF), 1.0 / CONV_K),
        "ffn_conv_b": nrm(ks[21], (DEPTH, D_FF), 0.01),
        "ffn_w_down": nrm(ks[22], (DEPTH, D_FF, D), D_FF ** -0.5),
        "final_norm_g": gain(ks[23], (D,)),
    }

def first_block(x, c, ctx, c_ctx, w_ada, b_ada, norm1_g, norm2_g, w_in, sgu_ln_g, sgu_ln_b, sgu_w, sgu_b,
              gla_w2, gla_b2, gla_norm_g, w_br_a, w_br_b, w_o, ffn_w_up, ffn_conv_w, ffn_conv_b,
              ffn_w_down, final_norm_g):
    bsz, seq, _ = x.shape
    rows = seq // GRID_W
    s0 = jnp.zeros((bsz, GLA_HEADS, GLA_HEAD_K, GLA_HEAD_V), jnp.float32)
    for l in range(DEPTH):
        last = l == DEPTH - 1
        sh1x, sc1x, g1x, sh2x, sc2x, g2x = jnp.split((jax.nn.silu(c) @ w_ada[l] + b_ada[l])[:, None, :], N_MOD, axis=-1)
        sh1c, sc1c, g1c, sh2c, sc2c, g2c = jnp.split(jax.nn.silu(c_ctx) @ w_ada[l] + b_ada[l], N_MOD, axis=-1)
        tm = (w_in[l], sgu_ln_g[l], sgu_ln_b[l], sgu_w[l], sgu_b[l], gla_w2[l], gla_b2[l], gla_norm_g[l],
              w_br_a[l], w_br_b[l], w_o[l])
        hc = _modulate(_rms_norm(ctx, norm1_g[l]), sh1c, sc1c)
        if last:
            s_f, s_b = _context_states(hc, w_in[l], gla_w2[l], gla_b2[l], s0)
        else:
            y_c, s_f, s_b = _token_mixer(hc, *tm, s0, s0)
        hx = _modulate(_rms_norm(x, norm1_g[l]), sh1x, sc1x)
        y_x, _, _ = _token_mixer(hx, *tm, s_f, s_b)
        x = x + g1x * y_x
        hx2 = _modulate(_rms_norm(x, norm2_g[l]), sh2x, sc2x)
        x = x + g2x * _conv_ffn(hx2, rows, ffn_w_up[l], ffn_conv_w[l], ffn_conv_b[l], ffn_w_down[l])
        if not last:
            ctx = ctx + g1c * y_c
            hc2 = _modulate(_rms_norm(ctx, norm2_g[l]), sh2c, sc2c)
            ctx = ctx + g2c * _conv_ffn(hc2, 1, ffn_w_up[l], ffn_conv_w[l], ffn_conv_b[l], ffn_w_down[l])
    return _rms_norm(x, final_norm_g)


DEPTH_2 = 2

N_MIXERS = 2
N_META = 16
GDN_HEADS = 8
GDN_HEAD_DIM = 128
GDN_WIDTH = GDN_HEADS * GDN_HEAD_DIM
GDN_CONV = 4
CHUNK = 64
META_PAD = (-N_META) % CHUNK
SC_WIDTH = D_MODEL
SC_CONV = 3
FFN_CONV = 3
N_LAYERS_A = (DEPTH_2 + 1) // 2
N_LAYERS_B = DEPTH_2 // 2
ALPHA = (2.0 * DEPTH_2) ** 0.25
BETA_INIT = (8.0 * DEPTH_2) ** -0.25
LN_EPS = 1e-5
RMS_EPS = 1e-6
L2_EPS = 1e-6


def causal_dwconv(x, w):
    width, ch = w.shape
    return lax.conv_general_dilated(
        x, w[:, None, :].astype(x.dtype), window_strides=(1,), padding=[(width - 1, 0)],
        dimension_numbers=("NWC", "WIO", "NWC"), feature_group_count=ch)

def layer_norm(x, g, b):
    xf = x.astype(jnp.float32)
    mu = jnp.mean(xf, axis=-1, keepdims=True)
    var = jnp.mean(jnp.square(xf - mu), axis=-1, keepdims=True)
    y = (xf - mu) * lax.rsqrt(var + LN_EPS) * g.astype(jnp.float32) + b.astype(jnp.float32)
    return y.astype(x.dtype)

def l2norm(x):
    return x * lax.rsqrt(jnp.sum(x * x, axis=-1, keepdims=True) + L2_EPS)

def chunk_gated_delta_rule(q, k, v, g, beta):
    bsz, t_len, h, dk = q.shape
    n = t_len // CHUNK

    def to_chunks(t):
        return jnp.transpose(t.reshape(bsz, n, CHUNK, h, -1), (0, 3, 1, 2, 4))

    q, k, v = to_chunks(q), to_chunks(k), to_chunks(v)
    g = jnp.transpose(g.reshape(bsz, n, CHUNK, h), (0, 3, 1, 2))
    beta = jnp.transpose(beta.reshape(bsz, n, CHUNK, h), (0, 3, 1, 2))
    g = jnp.cumsum(g, axis=-1)

    causal = jnp.tril(jnp.ones((CHUNK, CHUNK), dtype=bool))
    strict = jnp.tril(jnp.ones((CHUNK, CHUNK), dtype=bool), -1)
    decay = jnp.exp(jnp.where(causal, g[..., :, None] - g[..., None, :], -jnp.inf))

    k_beta = k * beta[..., None]
    v_beta = v * beta[..., None]
    m = jnp.where(strict, jnp.einsum("bhnid,bhnjd->bhnij", k_beta, k) * decay, 0.0)
    a_mat = jnp.eye(CHUNK, dtype=q.dtype) + m
    u = lax.linalg.triangular_solve(a_mat, v_beta, left_side=True, lower=True)
    w = lax.linalg.triangular_solve(a_mat, k_beta * jnp.exp(g)[..., None], left_side=True, lower=True)

    qk = jnp.einsum("bhnid,bhnjd->bhnij", q, k) * decay
    q_g = q * jnp.exp(g)[..., None]
    g_last = g[..., -1]
    k_dec = k * jnp.exp(g_last[..., None] - g)[..., None]

    def step(state, inp):
        qg_i, kd_i, u_i, w_i, qk_i, gl_i = inp
        v_new = u_i - jnp.einsum("bhcd,bhde->bhce", w_i, state)
        o_i = jnp.einsum("bhcd,bhde->bhce", qg_i, state) + jnp.einsum("bhij,bhje->bhie", qk_i, v_new)
        state = state * jnp.exp(gl_i)[..., None, None] + jnp.einsum("bhcd,bhce->bhde", kd_i, v_new)
        return state, o_i

    xs = tuple(jnp.moveaxis(t, 2, 0) for t in (q_g, k_dec, u, w, qk, g_last))
    state0 = jnp.zeros((bsz, h, dk, v.shape[-1]), dtype=q.dtype)
    _, o = lax.scan(step, state0, xs)
    return jnp.transpose(o, (1, 0, 3, 2, 4)).reshape(bsz, t_len, h, -1)

def gated_deltanet(h, w_in, conv_w, a_log, dt_bias, norm_w, w_out):
    bsz, seq_len, _ = h.shape
    proj = h @ w_in
    qkv, z, b_raw, a_raw = jnp.split(
        proj, [3 * GDN_WIDTH, 4 * GDN_WIDTH, 4 * GDN_WIDTH + GDN_HEADS], axis=-1)
    qkv = jax.nn.silu(causal_dwconv(qkv, conv_w))
    q, k, v = [t.reshape(bsz, seq_len, GDN_HEADS, GDN_HEAD_DIM).astype(jnp.float32)
               for t in jnp.split(qkv, 3, axis=-1)]
    q = l2norm(q) * (GDN_HEAD_DIM ** -0.5)
    k = l2norm(k)
    beta = jax.nn.sigmoid(b_raw.astype(jnp.float32))
    g = -jnp.exp(a_log.astype(jnp.float32)) * jax.nn.softplus(
        a_raw.astype(jnp.float32) + dt_bias.astype(jnp.float32))
    pad4 = ((0, 0), (META_PAD, 0), (0, 0), (0, 0))
    pad3 = ((0, 0), (META_PAD, 0), (0, 0))
    o = chunk_gated_delta_rule(jnp.pad(q, pad4), jnp.pad(k, pad4), jnp.pad(v, pad4),
                               jnp.pad(g, pad3), jnp.pad(beta, pad3))[:, META_PAD:]
    o = o * lax.rsqrt(jnp.mean(o * o, axis=-1, keepdims=True) + RMS_EPS) * norm_w.astype(jnp.float32)
    o = o * jax.nn.silu(z.reshape(bsz, seq_len, GDN_HEADS, GDN_HEAD_DIM).astype(jnp.float32))
    return o.reshape(bsz, seq_len, GDN_WIDTH).astype(h.dtype) @ w_out

def short_conv_mixer(h, w_in, conv_w, w_out):
    b_gate, c_gate, xv = jnp.split(h @ w_in, 3, axis=-1)
    u = causal_dwconv(c_gate * xv, conv_w)
    return (b_gate * u) @ w_out

def conv_ffn(h, w_up, conv_w, w_down):
    u, gate = jnp.split(h @ w_up, 2, axis=-1)
    u = causal_dwconv(u, conv_w)
    return (jax.nn.silu(u) * gate) @ w_down

def second_inputs(seed: int = 0) -> dict:
    key = jax.random.key(seed)
    ks = iter(jax.random.split(key, 32))
    f32 = jnp.float32

    def nrm(shape, scale):
        return jax.random.normal(next(ks), shape, f32) * scale

    a_in_cols = 4 * GDN_WIDTH + 2 * GDN_HEADS
    dt = jnp.exp(jax.random.uniform(next(ks), (N_LAYERS_A, GDN_HEADS), f32,
                                    math.log(1e-3), math.log(1e-1)))
    return {
        "x": nrm((BATCH, SEQ, D_MODEL), 1.0),
        "meta": nrm((N_META, D_MODEL), 1.0),
        "a_w_in": nrm((N_LAYERS_A, D_MODEL, a_in_cols), D_MODEL ** -0.5),
        "a_conv": nrm((N_LAYERS_A, GDN_CONV, 3 * GDN_WIDTH), GDN_CONV ** -0.5),
        "a_log": jnp.log(jax.random.uniform(next(ks), (N_LAYERS_A, GDN_HEADS), f32, 1.0, 16.0)),
        "a_dt_bias": dt + jnp.log(-jnp.expm1(-dt)),
        "a_norm": 1.0 + nrm((N_LAYERS_A, GDN_HEAD_DIM), 0.02),
        "a_w_out": nrm((N_LAYERS_A, GDN_WIDTH, D_MODEL), BETA_INIT * GDN_WIDTH ** -0.5),
        "b_w_in": nrm((N_LAYERS_B, D_MODEL, 3 * SC_WIDTH), D_MODEL ** -0.5),
        "b_conv": nrm((N_LAYERS_B, SC_CONV, SC_WIDTH), SC_CONV ** -0.5),
        "b_w_out": nrm((N_LAYERS_B, SC_WIDTH, D_MODEL), BETA_INIT * SC_WIDTH ** -0.5),
        "ln_mix_g": 1.0 + nrm((DEPTH_2, D_MODEL), 0.02),
        "ln_mix_b": nrm((DEPTH_2, D_MODEL), 0.02),
        "ffn_w_up": nrm((DEPTH_2, D_MODEL, 2 * D_FF), D_MODEL ** -0.5),
        "ffn_conv": nrm((DEPTH_2, FFN_CONV, D_FF), FFN_CONV ** -0.5),
        "ffn_w_down": nrm((DEPTH_2, D_FF, D_MODEL), BETA_INIT * D_FF ** -0.5),
        "ln_ffn_g": 1.0 + nrm((DEPTH_2, D_MODEL), 0.02),
        "ln_ffn_b": nrm((DEPTH_2, D_MODEL), 0.02),
    }

def second_block(x, meta, a_w_in, a_conv, a_log, a_dt_bias, a_norm, a_w_out,
              b_w_in, b_conv, b_w_out, ln_mix_g, ln_mix_b,
              ffn_w_up, ffn_conv, ffn_w_down, ln_ffn_g, ln_ffn_b):
    bsz = x.shape[0]
    h = jnp.concatenate(
        [jnp.broadcast_to(meta.astype(x.dtype)[None], (bsz, N_META, D_MODEL)), x], axis=1)
    for i in range(DEPTH_2):
        j = i // N_MIXERS
        if i % N_MIXERS == 0:
            mix = gated_deltanet(h, a_w_in[j], a_conv[j], a_log[j], a_dt_bias[j], a_norm[j], a_w_out[j])
        else:
            mix = short_conv_mixer(h, b_w_in[j], b_conv[j], b_w_out[j])
        h = layer_norm(ALPHA * h + mix, ln_mix_g[i], ln_mix_b[i])
        h = layer_norm(ALPHA * h + conv_ffn(h, ffn_w_up[i], ffn_conv[i], ffn_w_down[i]),
                       ln_ffn_g[i], ln_ffn_b[i])
    return h[:, N_META:]


def setup_inputs(seed=0):
    out = dict(first_inputs(seed))
    for name, value in second_inputs(seed + 1).items():
        if name != "x":
            out[name + "_2"] = value
    return out


def reference(
    x, c, ctx, c_ctx, w_ada, b_ada, norm1_g, norm2_g, w_in, sgu_ln_g, sgu_ln_b, sgu_w, sgu_b,
    gla_w2, gla_b2, gla_norm_g, w_br_a, w_br_b, w_o, ffn_w_up, ffn_conv_w, ffn_conv_b,
    ffn_w_down, final_norm_g, meta_2, a_w_in_2, a_conv_2, a_log_2, a_dt_bias_2, a_norm_2,
    a_w_out_2, b_w_in_2, b_conv_2, b_w_out_2, ln_mix_g_2, ln_mix_b_2, ffn_w_up_2, ffn_conv_2,
    ffn_w_down_2, ln_ffn_g_2, ln_ffn_b_2,
):
    x = first_block(
        x, c, ctx, c_ctx, w_ada, b_ada, norm1_g, norm2_g, w_in, sgu_ln_g, sgu_ln_b, sgu_w,
        sgu_b, gla_w2, gla_b2, gla_norm_g, w_br_a, w_br_b, w_o, ffn_w_up, ffn_conv_w,
        ffn_conv_b, ffn_w_down, final_norm_g,
    )
    return second_block(
        x, meta_2, a_w_in_2, a_conv_2, a_log_2, a_dt_bias_2, a_norm_2, a_w_out_2, b_w_in_2,
        b_conv_2, b_w_out_2, ln_mix_g_2, ln_mix_b_2, ffn_w_up_2, ffn_conv_2, ffn_w_down_2,
        ln_ffn_g_2, ln_ffn_b_2,
    )


_drawn_inputs = setup_inputs


def setup_inputs(seed=0):
    import zlib

    import numpy as np

    out = dict(_drawn_inputs(seed))
    spreads = {}
    factors = {'c_ctx': 3.712,
     'b_ada': 4.296,
     'sgu_ln_g': 7.745,
     'sgu_ln_b': 64.0,
     'sgu_b': 3.903,
     'gla_b2': 8.0,
     'gla_norm_g': 4.202,
     'ffn_conv_b': 8.0,
     'a_norm_2': 22.965}
    for name, (base, spread) in spreads.items():
        noise = np.random.default_rng([zlib.crc32(name.encode()), seed]).standard_normal(out[name].shape)
        drawn = base * np.exp(spread * noise) if base else spread * noise
        out[name] = __import__('jax').numpy.asarray(drawn.astype(out[name].dtype))
    for name, factor in factors.items():
        out[name] = (out[name] * factor).astype(out[name].dtype)
    return out
```

```python
from contextlib import ExitStack

import numpy as np

import concourse.bass as bass
from concourse import mybir

F32 = mybir.dt.float32
F32R = mybir.dt.float32r
I32 = mybir.dt.int32
ALU = mybir.AluOpType
ACT = mybir.ActivationFunctionType
ds = bass.ds

P = 128
D = 1024
KD = D // P
N1 = 256
META = 16
N2 = META + N1
FF = 2816
KF = FF // P
HG, DK, DV = 4, 128, 256
RANK = 16
GC = 64
GRID = 64
HN = 8
ALPHA = 4.0 ** 0.25
SLOTS = 4
UB = 8
CHUNKS = [(0, 128), (128, 128), (256, 16)]

PV_PARTS = [("b_ada", 48), ("norm1_g", 8), ("norm2_g", 8), ("gla_b2", 8), ("gla_norm_g", 8),
            ("conv1_w", 9 * KF), ("conv1_b", KF), ("final_g", 8), ("a_conv", 4 * 24), ("a_norm", 1),
            ("b_conv", 3 * 8), ("ln_mix_g", 16), ("ln_mix_b", 16), ("conv2_w", 2 * 3 * KF),
            ("ln_ffn_g", 16), ("ln_ffn_b", 16)]
PV = {}
PV_N = 0
for _name, _n in PV_PARTS:
    PV[_name] = PV_N
    PV_N += _n

LINEARS = [("w_k", 4, 4), ("w_q", 4, 4), ("w_v", 8, 8), ("w_u", 8, 8), ("w_vs", 8, 8), ("w_r", 8, 8),
           ("w_ga", 8, 8), ("w_gb", 8, 8), ("w_br_a", 8, 8), ("w_br_b", 8, 8), ("w_o", 8, 8),
           ("up0", 44, 44), ("down0", 8, 24), ("a_in", 32, 32), ("a_out", 8, 8), ("up1", 44, 44),
           ("down1", 8, 24), ("b_cx", 16, 16), ("b_b", 8, 8), ("b_out", 8, 8), ("up2", 44, 44),
           ("down2", 8, 24)]
UNIT0, TILE0 = {}, {}
_u = _t = 0
for _name, _tiles, _units in LINEARS:
    UNIT0[_name], TILE0[_name] = _u, _t
    _u += _units
    _t += _tiles
UNITS = _u
TILES_OF = {n: t for n, t, _ in LINEARS}
STREAMS = [("s0", ["w_k", "w_q", "w_v", "w_u", "w_vs", "w_r", "w_ga", "w_gb"]),
           ("s1", ["w_br_a", "w_br_b", "w_o", "up0"]), ("down0", None), ("s2", ["a_in", "a_out", "up1"]),
           ("down1", None), ("s3", ["b_cx", "b_b", "b_out", "up2"]), ("down2", None)]
DOWN_SPLIT = [(0, 8), (8, 8), (16, 6)]
LOG2P = 7


def bass_two_blocks(nc, a, out):
    ctx = ExitStack()
    with ctx:
        base = nc.sbuf_base + (-nc.sbuf_base) % 64
        where = [base]

        def at(name, shape, offset, dt=F32):
            return nc.alloc_sbuf_tensor_at(name, shape, dt, offset=offset)

        def sb(name, shape, dt=F32):
            n = 4 * int(np.prod(shape[1:]))
            t = at(name, shape, where[0], dt)
            where[0] += n + (-n) % 32
            return t

        def sem(name):
            return ctx.enter_context(nc.semaphore(name))

        w_raw = sb("w_raw", [P, SLOTS, UB, P])
        w_hi = sb("w_hi", [P, SLOTS, UB, P], F32R)
        w_lo = sb("w_lo", [P, SLOTS, UB, P], F32R)
        area_a = where[0]
        a_hi = sb("a_hi", [P, KD, 2 * N1], F32R)
        a_lo = sb("a_lo", [P, KD, 2 * N1], F32R)
        ident = sb("ident", [P, P])
        averages = sb("averages", [P, 4, P])
        over_d, over_dv, over_dh, ones = (averages[:, i] for i in range(4))
        levels = sb("levels", [P, LOG2P + 1, P])
        gla_masks = sb("gla_masks", [P, 2, P], I32)
        pv = sb("pv", [P, PV_N])
        mod = sb("mod", [P, 2, 48])
        gain = sb("gain", [P, 3, KD])
        eps6 = sb("eps6", [P, 2])
        csil = sb("csil", [P, D])
        stats = sb("stats", [P, 2, 2, 6])
        mv = sb("mv", [P, 2, 4])
        x = sb("x", [P, KD, N1])
        area_r = where[0]
        rstd = sb("rstd", [P, 2 * N1])
        area_h = where[0]
        h = sb("h", [P, KD, N2])
        area_s = where[0]
        sq = sb("sq", [P, KD, N2])
        arena = where[0]
        assert arena + 86016 <= nc.sbuf_usable_end, (arena, nc.sbuf_usable_end)

        q1 = at("q1", [P, HG, N1], arena)
        k1 = at("k1", [P, HG, 2 * N1], arena + 4096)
        vx = at("vx", [P, 2, D], arena + 12288)
        vc = at("vc", [P, 2, D], arena + 20480)
        ctxt = at("ctxt", [P, KD, N1], arena + 20480)
        sr = at("sr", [P, KD, N1], arena + 28672)
        ga = at("ga", [P, KD, N1], arena + 36864)
        gb = at("gb", [P, KD, N1], arena + 45056)
        hfull = at("hfull", [P, KD, 2 * N1], arena + 53248)
        ebuf = at("ebuf", [P, 2, HG, 2 * N1], arena + 53248)
        la = at("la", [P, 2, HG, 2 * N1], arena + 69632)
        adaw = at("adaw", [P, 2, 2, D], arena + 69632)
        rows = at("rows", [P, 3, D], arena + 69632)
        mixed = at("mixed", [P, 4, P], area_r)
        sguw = at("sguw", [P, 8, P], arena + 69632 + 12288)
        csil2 = at("csil2", [P, D], arena + 36864)
        wlr = at("wlr", [P, KD, 2 * RANK], arena + 28672)
        w2p = at("w2p", [2 * RANK, 2, HG * DK], arena + 28672 + 1024)
        lrt = at("lrt", [2 * RANK, 2 * N1], arena)
        reset = at("reset", [P, HG * 2 * N1], arena + 45056)
        gu = at("gu", [P, KD, N1], area_s)
        vs = at("vs", [P, 2, D], area_h)
        kdec = at("kdec", [P, HG, 2 * N1], arena + 69632)
        eq = at("eq", [P, HG, N1], arena + 77824)
        ek = at("ek", [P, HG, N1], arena + 81920)
        qd = at("qd", [P, HG, N1], area_a)
        ki = at("ki", [P, HG, N1], area_a + 4096)
        kt = at("kt", [P, 4, HG, DK], area_a + 8192)
        st = at("st", [P, HG, DV], area_a + 16384)
        sc = at("sc", [P, 2, HG, P], area_a + 20480)
        dec = at("dec", [P, HG * 8], area_a + 24576)
        o1 = at("o1", [P, HG, 2, N1], area_s)
        osq = at("osq", [P, HG, 2, N1], area_h)
        orstd = at("orstd", [P, HG, N1], arena + 69632)

        g_hi = at("g_hi", [P, KF, N2], arena, F32R)
        g_lo = at("g_lo", [P, KF, N2], arena + 23936, F32R)
        off = arena + 47872
        abuf = at("abuf", [P, 2, N2], off)
        cbuf = at("cbuf", [P, 2, N2], off + 2176)
        vbuf = at("vbuf", [P, 2, N2], off + 4352)
        gbuf = at("gbuf", [P, 2, N2], off + 6528)
        gfull = at("gfull", [P, 2, N2], off + 8704)
        ucv = at("ucv", [P, KD, N2], arena)
        pbuf = at("pbuf", [P, 2, N2], off + 8704)

        qkv = at("qkv", [P, 24, N2], arena)
        kb = at("kb", [P, HN, N2], arena + 26112)
        qg = at("qg", [P, HN, N2], arena + 34816)
        sz = at("sz", [P, HN, N2], arena + 43520)
        on = at("on", [P, HN, N2], arena + 52224)
        s2 = at("s2", [P, HN, P], arena + 60928)
        sel = at("sel", [HN, HN, P], arena + 65024)
        tok = at("tok", [HN, 6, N2], arena + 69120)
        tokm = at("tokm", [HN, N2], arena + 75648)
        toks = at("toks", [P, 3, 4, HN], arena + 76736)
        glast = at("glast", [HN, 4], arena + 77120)
        glb = at("glb", [P, HN, 3], arena + 77152)
        hb = at("hb", [HN, 4], arena + 77248)
        wba = at("wba", [P, KD, 2 * HN], arena + 77312)
        conva = at("conva", [P, 4, N2], arena + 77824)
        convc = at("convc", [P, 4, N2], arena + 43520)
        junk = at("junk", [P, D], arena + 53248)
        grp = []
        slot = [area_a + 2048 * i for i in range(16)] + [arena + 77824 + 2048 * i for i in range(2)]
        for g in range(2):
            names = ("kbeg", "kdc", "vb", "dd", "mt", "qkd", "tt", "uu", "ml")
            grp.append({n: at(f"{n}{g}", [P, 4, P], slot[9 * g + i]) for i, n in enumerate(names)})

        banks = [ctx.enter_context(nc.psum_tensor(f"bank{i}", [P, 512], F32)) for i in range(8)]

        def sems(names):
            return [sem(n) for n in names.split()]

        landed = [sem(f"landed{i}") for i in range(SLOTS)]
        hi_ready, lo_ready, unit_used, banks_free = sems("hi_ready lo_ready unit_used banks_free")
        small_in, w2_in, c_in, ctx_in, sgu_in, h_in, gdn_in, fills = sems("small_in w2_in c_in ctx_in sgu_in h_in gdn_in fills")
        ada_in = sems("ada_in0 ada_in1")
        ada_seq, ada_used, csil_ready, ada_done = sems("ada_seq ada_used csil_ready ada_done")
        act_seq, dve_seq = sems("act_seq dve_seq")
        sq_ready, ms_ready, std_ready, mean_ready, cent_ready, normed = sems(
            "sq_ready ms_ready std_ready mean_ready cent_ready normed")
        split_hi, split_ready = sems("split_hi split_ready")
        lr_done, lr_ready, z_done, t_ready, log_ready, decay_ready = sems(
            "lr_done lr_ready z_done t_ready log_ready decay_ready")
        vs_var, vs_std, vn_ready, sgu_done, gated = sems("vs_var vs_std vn_ready sgu_done gated")
        diff_ready, exps_ready, kdec_ready, qk_ready = sems("diff_ready exps_ready kdec_ready qk_ready")
        kt_done, kt_ready, sc_done, sc_ready, o_done, o_taken, up_done, st_ready = sems(
            "kt_done kt_ready sc_done sc_ready o_done o_taken up_done st_ready")
        osq_ready, oms_done, ostd_ready, ob_ready, merged = sems("osq_ready oms_done ostd_ready ob_ready merged")
        conv_seq, conv_done, act_done, glu_done, g_rounded, g_ready = sems(
            "conv_seq conv_done act_done glu_done g_rounded g_ready")
        p_used, u_seq = sems("p_used u_seq")
        conv4_seq, conv4_done, conv4_act = sems("conv4_seq conv4_done conv4_act")
        ba_done, tok_act, gcum_ready, tok_ready, tokx_done, toks_ready = sems(
            "ba_done tok_act gcum_ready tok_ready tokx_done toks_ready")
        qsq_ready, qss_done, qstd_ready, qk_norm, bc_done, bc_used = sems(
            "qsq_ready qss_done qstd_ready qk_norm bc_done bc_used")
        ktok_done, ktok_used, gm_done, gm_used, dcy_done, dcy_used, dcy_exp, mtu_ready, tt_done, tt_ready = sems(
            "ktok_done ktok_used gm_done gm_used dcy_done dcy_used dcy_exp mtu_ready tt_done tt_ready")
        ml_ready, y_done, y_ready, ty_done, ty_used = sems("ml_ready y_done y_ready ty_done ty_used")
        wt_done, wt_ready, vn_done, vnew_ready, ov_done, ov_taken, s2_done, s2_ready, on_used = sems(
            "wt_done wt_ready vn_done vnew_ready ov_done ov_taken s2_done s2_ready on_used")
        stored = sem("stored")

        RMS_CTX, RMS_X, RMS_F, RMS_END, LN0 = 0, 1, 2, 3, 4

        def out_of(name):
            return TILE0[name] + TILES_OF[name] + 4

        def quad(bank, cols, rows=None):
            return bank[0:rows or cols, :].rearrange("p (h m) -> p h m", h=4)[:, :, 0:cols]

        block = ctx.enter_context(nc.Block())

        @block.sync
        def _(sp):
            def small(dst, src, s):
                sp.dma_start(dst, src).then_inc(s, 16)

            small(csil[:], a["c"].partition_broadcast(P), c_in)
            small(csil2[:], a["c_ctx"].partition_broadcast(P), c_in)
            small(ctxt[:], a["ctx"], ctx_in)
            small(x[:], a["x"], ctx_in)
            small(averages[:], a["averages"], small_in)
            small(pv[:], a["pv"], small_in)
            small(ident[:], a["ident"], small_in)
            small(levels[:], a["levels"], small_in)
            small(gla_masks[:], a["gla_masks"], small_in)
            small(wlr[:], a["w_lr"], small_in)

            def ada(pair, s):
                sp.dma_start(adaw[:, s], a["w_ada"][ds(pair, 1)].rearrange("o p t d -> (o p) t d")) \
                    .then_inc(ada_in[s], 16)

            for i in range(2):
                ada(i, i)
            with sp.Fori(1, 4) as it:
                for s in range(2):
                    sp.wait_ge(ada_seq, it * 8 + (4 * s - 3))
                    ada(it * 2 + s, s)

            def unit(src, s):
                sp.dma_start(w_raw[:, s], src).then_inc(landed[s], 16)

            def stream_unit(name, i, s):
                unit(a[name][ds(i, 1)].rearrange("o p k m -> (o p) k m"), s)

            u0 = 0
            for name, parts in STREAMS:
                if parts is None:
                    with sp.Fori(0, 2) as it:
                        for j in range(4):
                            for b, (k0, kn) in enumerate(DOWN_SPLIT):
                                n = 3 * j + b
                                sp.wait_ge(lo_ready, it * 12 + (u0 + n - 3))
                                unit_src = a[name][ds(it * 4 + j, 1), :, k0:k0 + kn] \
                                    .rearrange("o p k m -> (o p) k m")
                                sp.dma_start(w_raw[:, n % 4, 0:kn], unit_src).then_inc(landed[n % 4], 16)
                    if name == "down0":
                        sp.wait_ge(normed, 2)
                        small(h[:, :, 0:META], a["meta"], h_in)
                        small(wba[:], a["w_ba"], gdn_in)
                        small(sel[:], a["sel"], gdn_in)
                        small(hb[:, 0:1], a["a_log"], gdn_in)
                        small(hb[:, 1:2], a["dt_bias"], gdn_in)
                    u0 += 24
                    continue
                n = sum(TILES_OF[x_] for x_ in parts)
                first = 0
                if u0 == 0:
                    for s in range(SLOTS):
                        stream_unit(name, s, s)
                    first = 1
                    with sp.Fori(1, 4) as it:
                        for s in range(SLOTS):
                            sp.wait_ge(lo_ready, it * 4 + (s - 3))
                            stream_unit(name, it * 4 + s, s)
                    sp.wait_ge(decay_ready, 2)
                    with sp.Fori(4, 12) as it:
                        for s in range(SLOTS):
                            sp.wait_ge(lo_ready, it * 4 + (s - 3))
                            stream_unit(name, it * 4 + s, s)
                        for s in range(2):
                            sp.wait_ge(ada_used, it * 2 + (s - 1))
                            ada(it * 2 + s, s)
                    sp.wait_ge(ada_used, 24)
                    small(rows[:, 0], a["sgu_ln_g"].partition_broadcast(P), sgu_in)
                    small(rows[:, 1], a["sgu_ln_b"].partition_broadcast(P), sgu_in)
                    small(rows[:, 2], a["sgu_b"].partition_broadcast(P), sgu_in)
                    small(sguw[:], a["sgu_w"], sgu_in)
                    first = 12
                if u0 + first * 4 > 0:
                    with sp.Fori(first, n // 4) as it:
                        for s in range(SLOTS):
                            sp.wait_ge(lo_ready, it * 4 + (u0 + s - 3))
                            stream_unit(name, it * 4 + s, s)
                u0 += n
            sp.wait_ge(normed, 7)
            sp.dma_start(out, h[:, :, META:N2]).then_inc(stored, 16)
            sp.wait_ge(stored, 16)

        @block.gpsimd
        def _(pool):
            pool.memset(w2p[:], 0.0).then_inc(fills, 1)
            pool.memset(eps6[:, 0:1], 1e-6).then_inc(fills, 1)
            pool.memset(eps6[:, 1:2], 1e-5).then_inc(fills, 1)
            pool.sem_inc(banks_free, SLOTS)
            pool.sem_inc(u_seq, 2)
            pool.sem_inc(p_used, 2)
            pool.wait_ge(fills, 3)
            pool.dma_start(w2p[0:RANK, 0], a["gla_w2"][0]).then_inc(w2_in, 16)
            pool.dma_start(w2p[RANK:2 * RANK, 1], a["gla_w2"][1]).then_inc(w2_in, 16)
            with pool.Fori(0, UNITS // 4) as it:
                for s in range(SLOTS):
                    pool.wait_ge(hi_ready, it * 4 + (s + 1))
                    pool.tensor_tensor(w_lo[:, s], w_raw[:, s], w_hi[:, s].bitcast(F32), ALU.subtract) \
                        .then_inc(lo_ready, 1)

        @block.tensor
        def _(pe):
            mm = nc.tensor.matmul

            def three(dst, pairs):
                n = 0
                last = 3 * len(pairs) - 1
                for (wh, wl), (xh, xl) in pairs:
                    for w_, x_ in ((wh, xh), (wh, xl), (wl, xh)):
                        ins = mm(dst, w_, x_, start=(n == 0), stop=(n == last))
                        n += 1
                return ins

            def lin(name, n):
                u0, t0 = UNIT0[name], TILE0[name]
                with pe.Fori(0, TILES_OF[name] // 4) as it:
                    for s in range(SLOTS):
                        pe.wait_ge(lo_ready, it * 4 + (u0 + s + 1))
                        pe.wait_ge(banks_free, it * 4 + (t0 + s + 1))
                        three(banks[s][:, 0:n], [((w_hi[:, s, k], w_lo[:, s, k]),
                                                  (a_hi[:, k, 0:n], a_lo[:, k, 0:n])) for k in range(KD)]) \
                            .then_inc(unit_used, 1)

            def lin_tokens(name, tiles):
                u0, t0 = UNIT0[name], TILE0[name]
                with pe.Fori(0, TILES_OF[name] // 4) as it:
                    for s in (0, 2):
                        pe.wait_ge(lo_ready, it * 4 + (u0 + s + 2))
                        pe.wait_ge(banks_free, it * 4 + (t0 + s + 2))
                        for t in range(tiles):
                            dst = banks[s + t * 2 // tiles][:, 256 * (t % (tiles // 2)):][:, 0:256] \
                                .rearrange("p (u m) -> p u m", u=2)
                            tk = slice(t * P, t * P + P)
                            n = 0
                            for k in range(KD):
                                wh, wl = w_hi[:, s:s + 2, k], w_lo[:, s:s + 2, k]
                                for x_, w_ in ((a_hi, wh), (a_lo, wh), (a_hi, wl)):
                                    ins = mm(dst, x_[:, k, tk], w_, start=(n == 0), stop=(n == 3 * KD - 1))
                                    n += 1
                        ins.then_inc(unit_used, 2)

            def down(name, n):
                u0, t0 = UNIT0[name], TILE0[name]
                with pe.Fori(0, 2) as it:
                    for j in range(4):
                        pe.wait_ge(banks_free, it * 4 + (t0 + j + 1))
                        m = 0
                        for b, (k0, kn) in enumerate(DOWN_SPLIT):
                            s = (3 * j + b) % 4
                            pe.wait_ge(lo_ready, it * 12 + (u0 + 3 * j + b + 1))
                            for k in range(kn):
                                for w_, x_ in ((w_hi, g_hi), (w_hi, g_lo), (w_lo, g_hi)):
                                    ins = mm(banks[j][:, 0:n], w_[:, s, k], x_[:, k0 + k, 0:n],
                                             start=(m == 0), stop=(m == 3 * KF - 1))
                                    m += 1
                            ins.then_inc(unit_used, 1)

            def mean_of(src, n, bank):
                for k in range(KD):
                    ins = mm(banks[bank][:, 0:n], over_d, src[:, k, 0:n], start=(k == 0), stop=(k == KD - 1))
                return ins

            def norm_ms(i, n):
                pe.wait_ge(sq_ready, i + 1)
                mean_of(sq, n, 4 if i == RMS_CTX else 5).then_inc(ms_ready, 1)

            def ln_norm(i):
                j = i - LN0
                name = ("a_out", "down1", "b_out", "down2")[j]
                pe.wait_ge(banks_free, out_of(name))
                mean_of(h, N2, 4).then_inc(mean_ready, 1)
                norm_ms(i, N2)

            pe.wait_ge(small_in, 16 * 6)
            norm_ms(RMS_CTX, N1)
            norm_ms(RMS_X, N1)
            pe.wait_ge(normed, 1)
            for k in range(KD):
                ins = mm(banks[6][0:2 * RANK, :], wlr[:, k], hfull[:, k], start=(k == 0), stop=(k == KD - 1))
            ins.then_inc(lr_done, 1)
            pe.wait_ge(split_ready, 1)
            lin("w_k", 2 * N1)
            pe.wait_ge(lr_ready, 1)
            pe.wait_ge(w2_in, 32)
            for i in range(2 * HG):
                d, hh = divmod(i, HG)
                if i >= 4:
                    pe.wait_ge(t_ready, i - 3)
                mm(banks[4 + i % 4][:, :], w2p[:, d, hh * DK:(hh + 1) * DK], lrt[:], start=True, stop=True) \
                    .then_inc(z_done, 1)
            lin("w_q", N1)
            lin_tokens("w_v", 4)
            lin("w_u", N1)
            lin_tokens("w_vs", 2)
            lin("w_r", N1)
            lin("w_ga", N1)
            lin("w_gb", N1)

            pe.wait_ge(sgu_in, 64)
            pe.wait_ge(t_ready, 8)
            for n in range(2):
                pe.wait_ge(vn_ready, n + 1)
                for half in range(2):
                    for g in range(4):
                        gg = 4 * half + g
                        ins = mm(banks[4 + 2 * n + half][:, g * P:(g + 1) * P], vs[:, n, gg * P:(gg + 1) * P],
                                 sguw[:, gg], start=True, stop=True)
                    ins.then_inc(sgu_done, 1)
            pe.wait_ge(split_ready, 2)
            lin("w_br_a", N1)

            for d in range(2):
                pe.wait_ge(kdec_ready, d + 1)
                for blk in range(4):
                    if blk >= 2 or d:
                        pe.wait_ge(kt_ready, 4 * d + blk - 1)
                    for hh in range(HG):
                        ins = nc.tensor.transpose(banks[4 + blk % 2][:, hh * DK:(hh + 1) * DK],
                                                  kdec[:, hh, blk * P:(blk + 1) * P], ident[:])
                    ins.then_inc(kt_done, 1)
                pe.wait_ge(qk_ready, 2 * d + 2)
                for blk in range(2):
                    if d:
                        pe.wait_ge(sc_ready, 2)
                    for hh in range(HG):
                        tk = slice(blk * P, (blk + 1) * P)
                        ins = mm(banks[6 + blk][:, hh * P:(hh + 1) * P], ki[:, hh, tk], qd[:, hh, tk],
                                 start=True, stop=True)
                    ins.then_inc(sc_done, 1)

                def state(step, chunk):
                    blk, rw = chunk // 2, slice(GC * (chunk % 2), GC * (chunk % 2) + GC)
                    src = vx if blk < 2 else vc
                    if 7 * d + step >= 1:
                        pe.wait_ge(st_ready, 7 * d + step)
                    for hh in range(HG):
                        ins = mm(banks[hh // 2][:, (hh % 2) * DV:(hh % 2 + 1) * DV], kt[rw, blk, hh],
                                 src[rw, blk % 2, hh * DV:(hh + 1) * DV], start=True, stop=True)
                    ins.then_inc(up_done, 1)

                pe.wait_ge(kt_ready, 4 * d + 4)
                order = [0, 1, 2, 3] if d == 0 else [3, 2, 1, 0]
                for step, c in enumerate(order):
                    state(step, 4 + c)
                pe.wait_ge(sc_ready, 2 * d + 2)
                for step, c in enumerate(order):
                    blk, rw = c // 2, slice(GC * (c % 2), GC * (c % 2) + GC)
                    if 4 * d + step >= 2:
                        pe.wait_ge(o_taken, 4 * d + step - 1)
                    pe.wait_ge(st_ready, 7 * d + 4 + step)
                    o_bank = banks[2 + step % 2]
                    for hh in range(HG):
                        for half in range(2):
                            dst = o_bank[:, (2 * hh + half) * GC:(2 * hh + half + 1) * GC]
                            col = hh * DV + half * P
                            mm(dst, vx[rw, blk, col:col + P], sc[rw, blk, hh, rw], start=True, stop=False)
                            ins = mm(dst, st[:, hh, half * P:(half + 1) * P], qd[:, hh, c * GC:(c + 1) * GC],
                                     start=False, stop=True)
                    ins.then_inc(o_done, 1)
                    if step < 3:
                        state(4 + step, c)
            pe.wait_ge(osq_ready, 1)
            for hh in range(HG):
                for half in range(2):
                    ins = mm(banks[4 + hh // 2][:, (hh % 2) * N1:(hh % 2 + 1) * N1], over_dv, osq[:, hh, half],
                             start=(half == 0), stop=(half == 1))
            ins.then_inc(oms_done, 1)
            pe.wait_ge(split_ready, 3)
            lin("w_br_b", N1)
            pe.wait_ge(split_ready, 4)
            lin("w_o", N1)
            norm_ms(RMS_F, N1)
            pe.wait_ge(split_ready, 5)
            lin("up0", N1)
            pe.wait_ge(g_ready, KF)
            down("down0", N1)
            norm_ms(RMS_END, N1)

            pe.wait_ge(split_ready, 6)
            lin("a_in", N2)
            pe.wait_ge(gdn_in, 64)
            for j in range(2):
                for k in range(KD):
                    ins = mm(banks[4 + j][0:HN, 0:N2], wba[:, k, j * HN:(j + 1) * HN], h[:, k],
                             start=(k == 0), stop=(k == KD - 1))
                ins.then_inc(ba_done, 1)
            pe.wait_ge(qsq_ready, 2)
            for i in range(16):
                if i >= 2:
                    pe.wait_ge(qstd_ready, i - 1)
                mm(banks[6 + i % 2][:, 0:N2], ones, (sq if i < 8 else kb)[:, i % 8], start=True, stop=True) \
                    .then_inc(qss_done, 1)
            pe.wait_ge(tok_ready, 1)
            for ci, (c0, cn) in enumerate(CHUNKS):
                for j, r in enumerate((0, 1, 4, 3)):
                    ins = nc.tensor.transpose(banks[0][0:cn, (4 * ci + j) * HN:(4 * ci + j + 1) * HN],
                                              tok[:, r, c0:c0 + cn], ident[0:HN, 0:HN])
            ins.then_inc(tokx_done, 1)
            for hh in range(HN):
                ins = mm(banks[1][:, 3 * hh:3 * hh + 3], sel[:, hh], glast[:, 0:3], start=True, stop=True)
            ins.then_inc(tokx_done, 1)
            for i in range(2 * HN):
                j, hh = divmod(i, HN)
                if i >= 2:
                    pe.wait_ge(bc_used, i - 1)
                mm(banks[2 + i % 2][:, 0:N2], sel[:, hh], tok[:, 2 * j], start=True, stop=True).then_inc(bc_done, 1)

            pe.wait_ge(bc_used, 16)
            pe.wait_ge(toks_ready, 2)
            n_lv = 0
            for ci, (c0, cn) in enumerate(CHUNKS):
                tk = slice(c0, c0 + cn)
                nlev = cn.bit_length() - 1
                for g in range(2):
                    b0 = 4 * g
                    if ci:
                        pe.wait_ge(vnew_ready, 2 * (ci - 1) + g + 1)
                        pe.wait_ge(ov_taken, 2 * (ci - 1) + g + 1)
                        pe.wait_ge(s2_ready, 2 * (ci - 1) + g + 1)
                    for j in range(2):
                        for hh in range(4):
                            ins = nc.tensor.transpose(banks[b0 + j][0:cn, hh * P:(hh + 1) * P],
                                                      qkv[:, 8 + 8 * j + 4 * g + hh, tk], ident[:])
                        ins.then_inc(ktok_done, 1)
                    for hh in range(4):
                        ins = mm(banks[b0 + 2][0:cn, hh * P:hh * P + cn], sel[:, 4 * g + hh, 0:cn], tok[:, 1, tk],
                                 start=True, stop=True)
                    ins.then_inc(dcy_done, 1)
                    for hh in range(4):
                        ins = mm(banks[b0 + 3][0:cn, hh * P:hh * P + cn], qkv[:, 8 + 4 * g + hh, tk],
                                 kb[:, 4 * g + hh, tk], start=True, stop=True)
                    ins.then_inc(gm_done, 1)
                for g in range(2):
                    b0 = 4 * g
                    pe.wait_ge(ktok_used, 3 * (2 * ci + g) + 3)
                    for hh in range(4):
                        ins = mm(banks[b0][0:cn, hh * P:hh * P + cn], qkv[:, 8 + 4 * g + hh, tk],
                                 qkv[:, 4 * g + hh, tk], start=True, stop=True)
                    ins.then_inc(gm_done, 1)
                for g in range(2):
                    b0, G = 4 * g, grp[g]
                    pe.wait_ge(mtu_ready, 2 * ci + g + 1)
                    for hh in range(4):
                        ins = nc.tensor.transpose(banks[b0 + 1][0:cn, hh * P:hh * P + cn], G["uu"][0:cn, hh, 0:cn],
                                                  ident[0:cn, 0:cn])
                    ins.then_inc(tt_done, 1)
                for lv in range(1, nlev):
                    for g in range(2):
                        b0, G = 4 * g, grp[g]
                        pe.wait_ge(ml_ready, n_lv + g + 1)
                        if lv == 1:
                            pe.wait_ge(tt_ready, 2 * ci + g + 1)
                            pe.wait_ge(gm_used, 4 * ci + 3 + g)
                        else:
                            pe.wait_ge(ty_used, n_lv - 2 + g + 1)
                        for hh in range(4):
                            ins = mm(banks[b0][0:cn, hh * P:hh * P + cn], G["ml"][0:cn, hh, 0:cn],
                                     G["tt"][0:cn, hh, 0:cn], start=True, stop=True)
                        ins.then_inc(y_done, 1)
                    for g in range(2):
                        b0, G = 4 * g, grp[g]
                        pe.wait_ge(y_ready, n_lv + g + 1)
                        for hh in range(4):
                            ins = mm(banks[b0 + 2][0:cn, hh * P:hh * P + cn], G["dd"][0:cn, hh, 0:cn],
                                     G["uu"][0:cn, hh, 0:cn], start=True, stop=True)
                        if lv < nlev - 1:
                            for hh in range(4):
                                ins = mm(banks[b0 + 3][0:cn, hh * P:hh * P + cn], G["uu"][0:cn, hh, 0:cn],
                                         G["dd"][0:cn, hh, 0:cn], start=True, stop=True)
                        ins.then_inc(ty_done, 1)
                    n_lv += 2
                if ci:
                    for g in range(2):
                        b0, G = 4 * g, grp[g]
                        pe.wait_ge(ty_used, n_lv - 2 + g + 1)
                        for hh in range(4):
                            ins = mm(banks[b0 + 1][:, hh * P:hh * P + cn], G["kbeg"][0:cn, hh],
                                     G["uu"][0:cn, hh, 0:cn], start=True, stop=True)
                        ins.then_inc(wt_done, 1)
                for g in range(2):
                    b0, G = 4 * g, grp[g]
                    pe.wait_ge(ty_used, n_lv - 2 + g + 1)
                    if ci:
                        pe.wait_ge(wt_ready, 2 * (ci - 1) + g + 1)
                        pe.wait_ge(s2_ready, 2 * (ci - 1) + g + 1)
                    for hh in range(4):
                        dst = banks[b0][0:cn, hh * P:(hh + 1) * P]
                        ins = mm(dst, G["uu"][0:cn, hh, 0:cn], G["vb"][0:cn, hh], start=True, stop=(ci == 0))
                        if ci:
                            ins = mm(dst, G["tt"][:, hh, 0:cn], s2[:, 4 * g + hh], start=False, stop=True)
                    ins.then_inc(vn_done, 1)
                for g in range(2):
                    b0, G = 4 * g, grp[g]
                    pe.wait_ge(vnew_ready, 2 * ci + g + 1)
                    for hh in range(4):
                        dst = banks[b0 + 2][:, hh * P:hh * P + cn]
                        ins = mm(dst, G["ml"][0:cn, hh], G["qkd"][0:cn, hh, 0:cn], start=True, stop=(ci == 0))
                        if ci:
                            ins = mm(dst, s2[:, 4 * g + hh], qg[:, 4 * g + hh, tk], start=False, stop=True)
                    ins.then_inc(ov_done, 1)
                    if ci < 2:
                        for hh in range(4):
                            ins = mm(banks[b0 + 3][:, hh * P:(hh + 1) * P], G["kdc"][0:cn, hh], G["ml"][0:cn, hh],
                                     start=True, stop=True)
                        ins.then_inc(s2_done, 1)
            pe.wait_ge(osq_ready, 2)
            for hh in range(HN):
                if hh >= 2:
                    pe.wait_ge(ostd_ready, 1 + hh - 1)
                mm(banks[6 + hh % 2][:, 0:N2], over_dh, sq[:, hh], start=True, stop=True).then_inc(oms_done, 1)
            pe.wait_ge(split_ready, 7)
            lin("a_out", N2)
            ln_norm(LN0)
            pe.wait_ge(split_ready, 8)
            lin("up1", N2)
            pe.wait_ge(g_ready, 2 * KF)
            down("down1", N2)
            ln_norm(LN0 + 1)
            pe.wait_ge(split_ready, 9)
            lin("b_cx", N2)
            lin("b_b", N2)
            pe.wait_ge(split_ready, 10)
            lin("b_out", N2)
            ln_norm(LN0 + 2)
            pe.wait_ge(split_ready, 11)
            lin("up2", N2)
            pe.wait_ge(g_ready, 3 * KF)
            down("down2", N2)
            ln_norm(LN0 + 3)

        @block.scalar
        def _(act):
            act_n = [0]

            def link(ins):
                act_n[0] += 1
                ins.then_inc(act_seq, 1)
                act.wait_ge(act_seq, act_n[0])

            def fn(out_, in_, f, **kw):
                return nc.scalar.activation(out_, in_, f, **kw)

            def round_unit(u, s):
                act.wait_ge(landed[s], u * 4 + 16 - 4 * s)
                fn(w_hi[:, s], w_raw[:, s], ACT.Copy).then_inc(hi_ready, 1)

            def lin(name, evac, units=None, ahead=True):
                u0 = UNIT0[name]
                with act.Fori(0, TILES_OF[name] // 4) as it:
                    for s in range(SLOTS):
                        act.wait_ge(unit_used, it * 4 + (u0 + s + 1))
                        if evac is not None:
                            evac(it * 4 + s, s)
                        round_unit(it * 4 + (u0 + s + 4), s)

            def down(name, last=False):
                u0 = UNIT0[name]
                if last:
                    with act.Fori(0, 5) as it:
                        for s in range(SLOTS):
                            act.wait_ge(unit_used, it * 4 + (u0 + s + 1))
                            round_unit(it * 4 + (u0 + s + 4), s)
                    return
                with act.Fori(0, 6) as it:
                    for s in range(SLOTS):
                        act.wait_ge(unit_used, it * 4 + (u0 + s + 1))
                        round_unit(it * 4 + (u0 + s + 4), s)

            def split(src, n, ready, count):
                act.wait_ge(ready, count)
                fn(a_hi[:, :, 0:n], src, ACT.Copy).then_inc(split_hi, 1)

            def square(i, src, n):
                fn(sq[:, :, 0:n], src, ACT.Square).then_inc(sq_ready, 1)

            def root(i, n, e):
                act.wait_ge(ms_ready, i + 1)
                c0, bank = (N1, 4) if i == RMS_CTX else (0, 5)
                fn(rstd[:, c0:c0 + n], banks[bank][:, 0:n], ACT.Sqrt, bias=eps6[:, e:e + 1]).then_inc(std_ready, 1)

            act.wait_ge(fills, 3)
            act.wait_ge(c_in, 32)
            fn(csil[:], csil[:], ACT.Silu).then_inc(csil_ready, 1)
            fn(csil2[:], csil2[:], ACT.Silu).then_inc(csil_ready, 1)
            act.wait_ge(ctx_in, 32)
            square(RMS_CTX, ctxt[:], N1)
            root(RMS_CTX, N1, 0)
            square(RMS_X, x[:], N1)
            root(RMS_X, N1, 0)
            for s in range(SLOTS):
                round_unit(s, s)
            split(hfull[:], 2 * N1, normed, 1)
            act.wait_ge(lr_done, 1)
            fn(lrt[:], banks[6][0:2 * RANK, :], ACT.Copy).then_inc(lr_ready, 1)
            lin("w_k", lambda t, s: fn(k1[:, ds(t, 1)], banks[s][:, :].unsqueeze(1), ACT.Copy).then_inc(banks_free, 1))
            act.wait_ge(z_done, 8)
            lin("w_q", lambda t, s: fn(q1[:, ds(t, 1)], banks[s][:, 0:N1].unsqueeze(1), ACT.Copy, scale=DK ** -0.5)
                .then_inc(banks_free, 1))
            act.wait_ge(t_ready, 8)
            link(fn(ebuf[:], la[:], ACT.Abs))
            link(fn(ebuf[:], ebuf[:], ACT.Exp, scale=-1.0))
            fn(ebuf[:], ebuf[:], ACT.Ln, bias=1.0).then_inc(log_ready, 1)

            def evac_v(t, s):
                if s % 2 == 0:
                    return
                for b, dst in ((s - 1, vx), (s, vc)):
                    fn(dst[:, :, ds((t - 1) * P, 2 * P)], banks[b][:, :].rearrange("p (t m) -> p t m", t=2), ACT.Copy) \
                        .then_inc(banks_free, 1)

            lin("w_v", evac_v)
            lin("w_u", lambda t, s: fn(gu[:, ds(t, 1)], banks[s][:, 0:N1].unsqueeze(1), ACT.Gelu).then_inc(banks_free, 1))

            def evac_vs(t, s):
                if s % 2 == 0:
                    return
                for b in range(2):
                    fn(vs[:, b, ds((t - 1) * P, 2 * P)], banks[s - 1 + b][:, 0:2 * P], ACT.Gelu).then_inc(banks_free, 1)

            lin("w_vs", evac_vs)
            act.wait_ge(decay_ready, 2)
            nc.scalar.preload_act_table(ACT.Silu)
            lin("w_r", lambda t, s: fn(sr[:, ds(t, 1)], banks[s][:, 0:N1].unsqueeze(1), ACT.Silu).then_inc(banks_free, 1))
            nc.scalar.preload_act_table(ACT.Sigmoid)
            act.wait_ge(ada_used, 8)
            lin("w_ga", lambda t, s: fn(ga[:, ds(t, 1)], banks[s][:, 0:N1].unsqueeze(1), ACT.Sigmoid).then_inc(banks_free, 1))
            act.wait_ge(vs_var, 2)
            for n in range(2):
                fn(mv[:, n, 2:3], mv[:, n, 1:2], ACT.Sqrt, bias=eps6[:, 0:1]).then_inc(vs_std, 1)
            nc.scalar.preload_act_table(ACT.Sigmoid)
            lin("w_gb", lambda t, s: fn(gb[:, ds(t, 1)], banks[s][:, 0:N1].unsqueeze(1), ACT.Sigmoid).then_inc(banks_free, 1))
            split(gu[:], N1, gated, 8)
            lin("w_br_a", None)
            for d in range(2):
                if d == 0:
                    act.wait_ge(banks_free, out_of("w_br_a"))
                else:
                    act.wait_ge(qk_ready, 2)
                    act.wait_ge(st_ready, 7)
                fn(eq[:], ebuf[:, d, :, 0:N1], ACT.Exp, scale=1 / 16).then_inc(exps_ready, 1)
                fn(ek[:], ebuf[:, d, :, 0:N1], ACT.Exp, scale=-1 / 16).then_inc(exps_ready, 1)
                flat = ebuf[:, d].rearrange("p h (c t) -> p (h c) t", t=GC)
                last = flat[:, :, GC - 1] if d == 0 else flat[:, :, 0]
                fn(dec[:], last, ACT.Exp, scale=1 / 16).then_inc(exps_ready, 1)
                act.wait_ge(diff_ready, d + 1)
                fn(kdec[:], kdec[:], ACT.Exp, scale=1 / 16).then_inc(exps_ready, 1)
                for blk in range(4):
                    act.wait_ge(kt_done, 4 * d + blk + 1)
                    if d and blk == 0:
                        act.wait_ge(up_done, 7)
                    fn(kt[:, blk], banks[4 + blk % 2][:, :].rearrange("p (h k) -> p h k", h=HG), ACT.Copy) \
                        .then_inc(kt_ready, 1)
            act.wait_ge(o_taken, 8)
            fn(osq[:], o1[:], ACT.Square).then_inc(osq_ready, 1)
            act.wait_ge(oms_done, 1)
            for b in range(2):
                ins = fn(orstd[:, 2 * b:2 * b + 2], banks[4 + b][:, :].rearrange("p (h t) -> p h t", h=2), ACT.Sqrt,
                         bias=eps6[:, 0:1])
            ins.then_inc(ostd_ready, 1)
            split(o1[:].rearrange("p h v t -> p (h v) t"), N1, ob_ready, 8)
            lin("w_br_b", None)
            split(gb[:], N1, merged, 8)
            lin("w_o", None)
            act.wait_ge(banks_free, out_of("w_o"))
            square(RMS_F, x[:], N1)
            root(RMS_F, N1, 0)
            split(sq[:, :, 0:N1], N1, normed, 2)

            def ffn(i, n, f, w_center, bias):
                name = f"up{i}"
                u0, j0 = UNIT0[name], KF * i
                nc.scalar.preload_act_table(f)

                def activate(j, p):
                    act.wait_ge(conv_done, j + (j0 + p + 1))
                    fn(gbuf[:, p, 0:n], cbuf[:, p, 0:n], f).then_inc(act_done, 1)

                def tiles(it, first):
                    for p in range(2):
                        s = 2 * p
                        u = it * 4 + (u0 + s)
                        act.wait_ge(unit_used, u + 1)
                        if not first:
                            act.wait_ge(act_done, it * 2 + (j0 + p - 1))
                        fn(abuf[:, p, 0:n], banks[s][:, 0:n], ACT.Copy)
                        kw = {"scale": pv[:, ds(it * 2 + (w_center + p), 1)]}
                        if bias is not None:
                            kw["bias"] = pv[:, ds(it * 2 + (bias + p), 1)]
                        fn(cbuf[:, p, 0:n], banks[s][:, 0:n], ACT.Identity, **kw).then_inc(banks_free, 1)
                        round_unit(u + 4, s)
                        act.wait_ge(unit_used, u + 2)
                        if not first:
                            act.wait_ge(glu_done, it * 2 + (j0 + p - 1))
                        fn(vbuf[:, p, 0:n], banks[s + 1][:, 0:n], ACT.Copy).then_inc(banks_free, 1)
                        round_unit(u + 5, s + 1)

                tiles(0, True)
                with act.Fori(1, KF // 2) as it:
                    for p in range(2):
                        activate(it * 2 - 2, p)
                    tiles(it, False)
                for p in range(2):
                    activate(KF - 2, p)

            ffn(0, N1, ACT.Gelu, PV["conv1_w"] + 4 * KF, PV["conv1_b"])
            down("down0")
            act.wait_ge(banks_free, out_of("down0"))
            square(RMS_END, x[:], N1)
            root(RMS_END, N1, 0)
            act.wait_ge(h_in, 16)
            split(h[:], N2, normed, 3)

            u0 = UNIT0["a_in"]

            def qkv_tiles(it, first):
                for s in range(SLOTS):
                    act.wait_ge(unit_used, it * 4 + (u0 + s + 1))
                    if not first:
                        act.wait_ge(conv4_act, it * 4 + (s - 3))
                    fn(conva[:, s], banks[s][:, 0:N2], ACT.Copy)
                    fn(convc[:, s], banks[s][:, 0:N2], ACT.Copy, scale=pv[:, ds(it * 4 + (PV["a_conv"] + 3 * 24 + s), 1)]) \
                        .then_inc(banks_free, 1)
                    round_unit(it * 4 + (u0 + s + 4), s)

            def qkv_activate(it):
                for s in range(SLOTS):
                    act.wait_ge(conv4_done, it * 4 + (s + 1))
                    fn(qkv[:, ds(it * 4 + s, 1)], convc[:, s].unsqueeze(1), ACT.Silu).then_inc(conv4_act, 1)

            nc.scalar.preload_act_table(ACT.Silu)
            qkv_tiles(0, True)
            with act.Fori(1, 6) as it:
                qkv_activate(it - 1)
                qkv_tiles(it, False)
            qkv_activate(5)
            act.wait_ge(conv4_act, 24)
            with act.Fori(0, 2) as it:
                for s in range(SLOTS):
                    act.wait_ge(unit_used, it * 4 + (u0 + 24 + s + 1))
                    fn(sz[:, ds(it * 4 + s, 1)], banks[s][:, 0:N2].unsqueeze(1), ACT.Silu).then_inc(banks_free, 1)
                    round_unit(it * 4 + (u0 + 24 + s + 4), s)
            fn(sq[:], qkv[:, 0:8], ACT.Square).then_inc(qsq_ready, 1)
            fn(kb[:], qkv[:, 8:16], ACT.Square).then_inc(qsq_ready, 1)
            act.wait_ge(gdn_in, 64)
            act.wait_ge(ba_done, 2)
            fn(tok[:, 0], banks[4][0:HN, 0:N2], ACT.Sigmoid).then_inc(tok_act, 1)
            fn(hb[:, 2:3], hb[:, 0:1], ACT.Exp).then_inc(tok_act, 1)
            act.wait_ge(tok_act, 2)
            fn(tok[:, 1], banks[5][0:HN, 0:N2], ACT.Identity, bias=hb[:, 1:2]).then_inc(tok_act, 1)
            act.wait_ge(tok_act, 3)
            link(fn(tok[:, 5], tok[:, 1], ACT.Abs))
            link(fn(tok[:, 5], tok[:, 5], ACT.Exp, scale=-1.0))
            fn(tok[:, 5], tok[:, 5], ACT.Ln, bias=1.0).then_inc(tok_act, 1)
            act.wait_ge(gcum_ready, 1)
            fn(tok[:, 2], tok[:, 1], ACT.Exp).then_inc(tok_act, 1)
            fn(tok[:, 3], tok[:, 3], ACT.Exp).then_inc(tok_act, 1)
            fn(glast[:, 0:3], glast[:, 0:3], ACT.Exp).then_inc(tok_act, 1)
            for i in range(16):
                act.wait_ge(qss_done, i + 1)
                if i >= 2:
                    act.wait_ge(qk_norm, i - 1)
                fn(conva[:, i % 2], banks[6 + i % 2][:, 0:N2], ACT.Sqrt,
                   bias=eps6[:, 0:1]).then_inc(qstd_ready, 1)
            act.wait_ge(tokx_done, 2)
            for ci, (c0, cn) in enumerate(CHUNKS):
                ins = fn(toks[0:cn, ci], banks[0][0:cn, ci * 4 * HN:(ci + 1) * 4 * HN]
                         .rearrange("p (j h) -> p j h", j=4), ACT.Copy)
            ins.then_inc(toks_ready, 1)
            fn(glb[:], banks[1][:, 0:3 * HN].rearrange("p (h c) -> p h c", h=HN), ACT.Copy).then_inc(toks_ready, 1)
            n_lv = 0
            nc.scalar.preload_act_table(ACT.Exp)
            for ci, (c0, cn) in enumerate(CHUNKS):
                for g in range(2):
                    act.wait_ge(dcy_used, 2 * ci + g + 1)
                    dd = grp[g]["dd"][0:cn, :, 0:cn]
                    fn(dd, dd, ACT.Exp).then_inc(dcy_exp, 1)
                for g in range(2):
                    act.wait_ge(tt_done, 2 * ci + g + 1)
                    fn(grp[g]["tt"][0:cn, :, 0:cn], quad(banks[4 * g + 1], cn), ACT.Copy).then_inc(tt_ready, 1)
                for lv in range(1, cn.bit_length() - 1):
                    for g in range(2):
                        act.wait_ge(y_done, n_lv + g + 1)
                        fn(grp[g]["dd"][0:cn, :, 0:cn], quad(banks[4 * g], cn), ACT.Copy).then_inc(y_ready, 1)
                    n_lv += 2
                if ci:
                    for g in range(2):
                        act.wait_ge(wt_done, 2 * (ci - 1) + g + 1)
                        fn(grp[g]["tt"][:, :, 0:cn], quad(banks[4 * g + 1], cn, P), ACT.Copy, scale=-1.0) \
                            .then_inc(wt_ready, 1)
                for g in range(2):
                    act.wait_ge(vn_done, 2 * ci + g + 1)
                    fn(grp[g]["ml"][0:cn], quad(banks[4 * g], P, cn), ACT.Copy).then_inc(vnew_ready, 1)
                for g in range(2):
                    act.wait_ge(ov_done, 2 * ci + g + 1)
                    fn(on[:, 4 * g:4 * g + 4, c0:c0 + cn], quad(banks[4 * g + 2], cn, P), ACT.Copy).then_inc(ov_taken, 1)
            act.wait_ge(ov_taken, 6)
            fn(sq[:], on[:], ACT.Square).then_inc(osq_ready, 1)
            for hh in range(HN):
                act.wait_ge(oms_done, 1 + hh + 1)
                if hh >= 2:
                    act.wait_ge(on_used, hh - 1)
                fn(kb[:, hh % 2], banks[6 + hh % 2][:, 0:N2], ACT.Sqrt, bias=eps6[:, 0:1]).then_inc(ostd_ready, 1)
            split(on[:], N2, on_used, 8)
            lin("a_out", None)

            def ln(i):
                act.wait_ge(cent_ready, i - LN0 + 1)
                square(i, h[:], N2)
                root(i, N2, 1)

            ln(LN0)
            split(h[:], N2, normed, 4)
            ffn(1, N2, ACT.Silu, PV["conv2_w"] + 2 * KF, None)
            down("down1")
            ln(LN0 + 1)
            split(h[:], N2, normed, 5)
            u0 = UNIT0["b_cx"]

            with act.Fori(0, 4) as it:
                for s in range(SLOTS):
                    act.wait_ge(unit_used, it * 4 + (u0 + s + 1))
                    act.wait_ge(p_used, it * 2 + (s // 2 + 1))
                    fn((abuf if s % 2 == 0 else vbuf)[:, s // 2], banks[s][:, 0:N2], ACT.Copy).then_inc(banks_free, 1)
                    round_unit(it * 4 + (u0 + s + 4), s)
            lin("b_b", None)
            split(ucv[:], N2, banks_free, out_of("b_b"))
            lin("b_out", None)
            ln(LN0 + 2)
            split(h[:], N2, normed, 6)
            ffn(2, N2, ACT.Silu, PV["conv2_w"] + 5 * KF, None)
            down("down2", last=True)
            ln(LN0 + 3)

        @block.vector
        def _(dve):
            v = nc.vector
            dve_n = [0]

            def link(ins):
                dve_n[0] += 1
                ins.then_inc(dve_seq, 1)
                dve.wait_ge(dve_seq, dve_n[0])

            def lanes(ap, k):
                return ap.unsqueeze(1).broadcast_to([ap.shape[0], k, ap.shape[-1]])

            def col(name, i):
                return pv[:, PV[name] + i:PV[name] + i + 1]

            def remainder(i, src, n):
                dve.wait_ge(split_hi, i + 1)
                v.tensor_tensor(a_lo[:, :, 0:n], src, a_hi[:, :, 0:n].bitcast(F32), ALU.subtract) \
                    .then_inc(split_ready, 1)

            def affine(dst, gains, shifts, signal):
                for k in range(KD):
                    if shifts is None:
                        ins = v.tensor_scalar(dst[:, k], dst[:, k], gains(k), None, ALU.mult)
                    else:
                        ins = v.tensor_scalar(dst[:, k], dst[:, k], gains(k), shifts(k), ALU.mult, ALU.add)
                if signal:
                    ins.then_inc(normed, 1)
                return ins

            def scaled(i, dst, src, n):
                c0 = N1 if i == RMS_CTX else 0
                r = rstd[:, c0:c0 + n]
                dve.wait_ge(std_ready, i + 1)
                link(v.reciprocal(r, r))
                link(v.tensor_tensor(dst, src, lanes(r, KD), ALU.mult))

            dve.wait_ge(csil_ready, 2)
            v.memset(junk[:, 0:1], 0.0).then_inc(ada_seq, 1)
            with dve.Fori(0, 4) as it:
                for s in range(2):
                    dve.wait_ge(ada_in[s], it * 16 + 16)
                    for t in range(2):
                        for j, cs in enumerate((csil, csil2)):
                            dve.wait_ge(ada_seq, it * 8 + (4 * s + 2 * t + j + 1))
                            ins = v.scalar_tensor_tensor(junk[:], adaw[:, s, t], 1.0, cs[:], ALU.mult, ALU.mult,
                                                         accum_out=mod[:, j, ds(it * 4 + (2 * s + t), 1)])
                            ins.then_inc(ada_seq, 1)
            dve.wait_ge(ada_seq, 33)
            dve.sem_inc(ada_used, 8)
            dve.wait_ge(small_in, 96)
            for j in range(2):
                ins = v.tensor_tensor(mod[:, j, 0:16], mod[:, j, 0:16], pv[:, PV["b_ada"]:PV["b_ada"] + 16], ALU.add)
            link(ins)
            norm1 = pv[:, PV["norm1_g"]:PV["norm1_g"] + KD]
            for j in range(2):
                ins = v.scalar_tensor_tensor(gain[:, j], mod[:, j, 8:16], 1.0, norm1, ALU.add, ALU.mult)
            link(ins)
            scaled(RMS_CTX, hfull[:, :, N1:], ctxt[:], N1)
            affine(hfull[:, :, N1:], lambda k: gain[:, 1, k:k + 1], lambda k: mod[:, 1, k:k + 1], False)
            scaled(RMS_X, hfull[:, :, 0:N1], x[:], N1)
            affine(hfull[:, :, 0:N1], lambda k: gain[:, 0, k:k + 1], lambda k: mod[:, 0, k:k + 1], True)
            remainder(0, hfull[:], 2 * N1)

            v.memset(reset[:], 1.0).then_inc(ada_done, 1)
            dve.wait_ge(ada_done, 1)
            link(v.memset(reset[:].rearrange("p (c t) -> p c t", t=GC)[:, :, 0:1], 0.0))
            for i in range(2 * HG):
                d, hh = divmod(i, HG)
                dve.wait_ge(z_done, i + 1)
                v.tensor_scalar(la[:, d, hh], banks[4 + i % 4][:, :], col("gla_b2", i), None, ALU.add).then_inc(t_ready, 1)
            dve.wait_ge(log_ready, 1)
            link(v.scalar_tensor_tensor(la[:], la[:], 0.0, ebuf[:], ALU.min, ALU.subtract))
            for d in range(2):
                src = la[:, d].rearrange("p h t -> p (h t)")
                dst = ebuf[:, d].rearrange("p h t -> p (h t)")
                if d:
                    src, dst = src[:, ::-1], dst[:, ::-1]
                v.tensor_tensor_scan(dst, reset[:], src, 0.0, ALU.mult, ALU.add).then_inc(decay_ready, 1)

            with dve.Fori(4, 12) as it:
                for s in range(2):
                    dve.wait_ge(ada_in[s], it * 16 + 16)
                    for t in range(2):
                        ins = v.scalar_tensor_tensor(adaw[:, s, t], adaw[:, s, t], 1.0, csil[:], ALU.mult, ALU.mult,
                                                     accum_out=mod[:, 0, ds(it * 4 + (2 * s + t), 1)])
                    ins.then_inc(ada_used, 1)
            dve.wait_ge(ada_used, 24)
            link(v.tensor_tensor(mod[:, 0, 16:48], mod[:, 0, 16:48], pv[:, PV["b_ada"] + 16:PV["b_ada"] + 48], ALU.add))
            link(v.scalar_tensor_tensor(gain[:, 2], mod[:, 0, 32:40], 1.0, pv[:, PV["norm2_g"]:PV["norm2_g"] + KD],
                                        ALU.add, ALU.mult))

            dve.wait_ge(banks_free, out_of("w_vs"))
            for n in range(2):
                for c in range(2):
                    ins = v.bn_stats(stats[:, n, c], vs[:, n, c * 512:(c + 1) * 512])
                link(ins)
                v.bn_aggr(mv[:, n, 0:2], stats[:, n]).then_inc(vs_var, 1)
            dve.wait_ge(vs_std, 2)
            for n in range(2):
                ins = v.reciprocal(mv[:, n, 3:4], mv[:, n, 2:3])
            link(ins)
            dve.wait_ge(sgu_in, 64)
            for n in range(2):
                link(v.tensor_scalar(vs[:, n], vs[:, n], mv[:, n, 0:1], mv[:, n, 3:4], ALU.subtract, ALU.mult))
                link(v.tensor_tensor(vs[:, n], vs[:, n], rows[:, 0], ALU.mult))
                v.tensor_tensor(vs[:, n], vs[:, n], rows[:, 1], ALU.add).then_inc(vn_ready, 1)
            for n in range(2):
                for half in range(2):
                    dve.wait_ge(sgu_done, 2 * n + half + 1)
                    gs = slice(4 * half, 4 * half + 4)
                    buf = mixed[:]
                    if n or half:
                        dve.wait_ge(gated, 2 * (2 * n + half))
                    link(v.tensor_tensor(buf, quad(banks[4 + 2 * n + half], P),
                                         rows[:, 2].rearrange("p (g t) -> p g t", g=8)[:, gs], ALU.add))
                    v.tensor_tensor(gu[:, gs, n * P:(n + 1) * P], gu[:, gs, n * P:(n + 1) * P], buf, ALU.mult) \
                        .then_inc(gated, 2)
            remainder(1, gu[:], N1)

            def lin(name, take):
                u0 = UNIT0[name]
                with dve.Fori(0, TILES_OF[name] // 4) as it:
                    for s in range(SLOTS):
                        dve.wait_ge(unit_used, it * 4 + (u0 + s + 1))
                        take(it * 4 + s, s)

            def down(name, take):
                u0 = UNIT0[name]
                with dve.Fori(0, 2) as it:
                    for j in range(4):
                        dve.wait_ge(unit_used, it * 12 + (u0 + 3 * j + 3))
                        take(it * 4 + j, j)

            lin("w_br_a", lambda t, s: v.tensor_tensor(ga[:, ds(t, 1)], banks[s][:, 0:N1].unsqueeze(1), ga[:, ds(t, 1)],
                                                       ALU.mult).then_inc(banks_free, 1))

            for d in range(2):
                flat = ebuf[:, d].rearrange("p h (c t) -> p (h c) t", t=GC)
                last = (flat[:, :, GC - 1:GC] if d == 0 else flat[:, :, 0:1]).broadcast_to([P, HG * 8, GC])
                if d:
                    dve.wait_ge(kt_ready, 4)
                else:
                    dve.wait_ge(banks_free, out_of("w_br_a"))
                v.tensor_tensor(kdec[:].rearrange("p h (c t) -> p (h c) t", t=GC), last, flat, ALU.subtract) \
                    .then_inc(diff_ready, 1)
                if d:
                    dve.wait_ge(o_done, 4)
                v.memset(sc[:], 0.0).then_inc(ada_done, 1)
                dve.wait_ge(exps_ready, 4 * d + 1)
                v.tensor_tensor(qd[:], q1[:], eq[:], ALU.mult).then_inc(qk_ready, 1)
                dve.wait_ge(exps_ready, 4 * d + 2)
                v.tensor_tensor(ki[:], k1[:, :, 0:N1], ek[:], ALU.mult).then_inc(qk_ready, 1)
                dve.wait_ge(exps_ready, 4 * d + 4)
                v.tensor_tensor(kdec[:], kdec[:], k1[:], ALU.mult).then_inc(kdec_ready, 1)
                dve.wait_ge(ada_done, 2 + d)
                for blk in range(2):
                    dve.wait_ge(sc_done, 2 * d + blk + 1)
                    for hh in range(HG):
                        ins = v.copy_predicated(sc[:, blk, hh], gla_masks[:, d], banks[6 + blk][:, hh * P:(hh + 1) * P])
                    ins.then_inc(sc_ready, 1)

                def state(step, chunk):
                    dve.wait_ge(up_done, 7 * d + step + 1)
                    if step:
                        dve.wait_ge(st_ready, 7 * d + step)
                    for hh in range(HG):
                        src = banks[hh // 2][:, (hh % 2) * DV:(hh % 2 + 1) * DV]
                        if step == 0:
                            ins = v.tensor_copy(st[:, hh], src)
                        else:
                            c = hh * 8 + chunk
                            ins = v.scalar_tensor_tensor(st[:, hh], st[:, hh], dec[:, c:c + 1], src, ALU.mult, ALU.add)
                    ins.then_inc(st_ready, 1)

                order = [0, 1, 2, 3] if d == 0 else [3, 2, 1, 0]
                if d:
                    dve.wait_ge(o_done, 4)
                for step, c in enumerate(order):
                    state(step, 4 + c)
                for step, c in enumerate(order):
                    dve.wait_ge(o_done, 4 * d + step + 1)
                    dst = o1[:].rearrange("p h v t -> p (h v) t")[:, :, c * GC:(c + 1) * GC]
                    src = banks[2 + step % 2][:, :].rearrange("p (h t) -> p h t", t=GC)
                    if d == 0:
                        ins = v.tensor_copy(dst, src)
                    else:
                        ins = v.tensor_tensor(dst, dst, src, ALU.add)
                    ins.then_inc(o_taken, 1)
                    if step < 3:
                        state(4 + step, c)
            dve.wait_ge(ostd_ready, 1)
            link(v.reciprocal(orstd[:], orstd[:]))
            for half in range(2):
                ins = v.tensor_tensor(o1[:, :, half], o1[:, :, half], orstd[:], ALU.mult)
            link(ins)
            of = o1[:].rearrange("p h v t -> p (h v) t")
            for k in range(KD):
                v.scalar_tensor_tensor(of[:, k], of[:, k], col("gla_norm_g", k), sr[:, k], ALU.mult, ALU.mult) \
                    .then_inc(ob_ready, 1)
            remainder(2, of, N1)

            def merge(t, s):
                v.tensor_tensor(gb[:, ds(t, 1)], banks[s][:, 0:N1].unsqueeze(1), gb[:, ds(t, 1)], ALU.mult) \
                    .then_inc(banks_free, 1)
                dve.wait_ge(banks_free, t + (TILE0["w_br_b"] + 5))
                v.tensor_tensor(gb[:, ds(t, 1)], gb[:, ds(t, 1)], ga[:, ds(t, 1)], ALU.add).then_inc(merged, 1)

            lin("w_br_b", merge)
            remainder(3, gb[:], N1)

            def residual(j):
                def take(t, s):
                    v.scalar_tensor_tensor(x[:, ds(t, 1)], banks[s][:, 0:N1].unsqueeze(1), mod[:, 0, ds(t + j * KD, 1)],
                                           x[:, ds(t, 1)], ALU.mult, ALU.add).then_inc(banks_free, 1)
                return take

            lin("w_o", residual(2))
            scaled(RMS_F, sq[:, :, 0:N1], x[:], N1)
            affine(sq[:, :, 0:N1], lambda k: gain[:, 2, k:k + 1], lambda k: mod[:, 0, 24 + k:25 + k], True)
            remainder(4, sq[:, :, 0:N1], N1)

            def ffn(i, n, taps):
                t0, j0, nt = TILE0[f"up{i}"], KF * i, len(taps)
                c0 = conv_links[0]
                conv_links[0] += KF * (nt - 1)
                with dve.Fori(0, KF // 2) as it:
                    for m, (w, to, frm) in enumerate(taps):
                        for p in range(2):
                            if m == 0:
                                dve.wait_ge(banks_free, it * 4 + (t0 + 2 * p + 5))
                            else:
                                dve.wait_ge(conv_seq, it * (2 * (nt - 1)) + (c0 + 2 * (m - 1) + p + 1))
                            dst = to(cbuf[:, p, 0:n])
                            v.scalar_tensor_tensor(dst, frm(abuf[:, p, 0:n]), pv[:, ds(it * 2 + (w + p), 1)], dst,
                                                   ALU.mult, ALU.add) \
                                .then_inc(conv_done if m == nt - 1 else conv_seq, 1)
                    for p in range(2):
                        dve.wait_ge(act_done, it * 2 + (j0 + p + 1))
                        v.tensor_tensor(gfull[:, p, 0:n], gbuf[:, p, 0:n], vbuf[:, p, 0:n], ALU.mult).then_inc(glu_done, 1)
                    for p in range(2):
                        dve.wait_ge(glu_done, it * 2 + (j0 + p + 1))
                        v.tensor_copy(g_hi[:, ds(it * 2 + p, 1), 0:n], gfull[:, p:p + 1, 0:n]).then_inc(g_rounded, 1)
                    for p in range(2):
                        dve.wait_ge(g_rounded, it * 2 + (j0 + p + 1))
                        jj = ds(it * 2 + p, 1)
                        v.tensor_tensor(g_lo[:, jj, 0:n], gfull[:, p:p + 1, 0:n], g_hi[:, jj, 0:n].bitcast(F32),
                                        ALU.subtract).then_inc(g_ready, 1)

            conv_links = [0]

            def image_tap(dy, dx):
                rows_, w = N1 // GRID, GRID
                y0, y1 = max(0, 1 - dy), rows_ - max(0, dy - 1)
                x0, x1 = max(0, 1 - dx), w - max(0, dx - 1)

                def view(ap, sy, sx):
                    return ap.rearrange("p (y x) -> p y x", x=w)[:, y0 + sy:y1 + sy, x0 + sx:x1 + sx]

                return (PV["conv1_w"] + (3 * dy + dx) * KF, lambda ap: view(ap, 0, 0),
                        lambda ap: view(ap, dy - 1, dx - 1))

            ffn(0, N1, [image_tap(dy, dx) for dy in range(3) for dx in range(3) if (dy, dx) != (1, 1)])
            down("down0", residual(5))
            scaled(RMS_END, h[:, :, META:], x[:], N1)
            affine(h[:, :, META:], lambda k: col("final_g", k), None, True)
            dve.wait_ge(h_in, 16)
            remainder(5, h[:], N2)

            def causal(w, shift, n=N2):
                return (w, lambda ap: ap[:, shift:n], lambda ap: ap[:, 0:n - shift])

            t0 = TILE0["a_in"]
            with dve.Fori(0, 6) as it:
                for m in range(3):
                    for s in range(SLOTS):
                        if m == 0:
                            dve.wait_ge(banks_free, it * 4 + (t0 + s + 5))
                        else:
                            dve.wait_ge(conv4_seq, it * 8 + (4 * (m - 1) + s + 1))
                        dst = convc[:, s, 3 - m:N2]
                        v.scalar_tensor_tensor(dst, conva[:, s, 0:N2 - 3 + m],
                                               pv[:, ds(it * 4 + (PV["a_conv"] + 24 * m + s), 1)], dst, ALU.mult, ALU.add) \
                            .then_inc(conv4_done if m == 2 else conv4_seq, 1)
            link(v.memset(tokm[:], 1.0))
            for c0, _ in CHUNKS:
                ins = v.memset(tokm[:, c0:c0 + 1], 0.0)
            link(ins)
            dve.wait_ge(tok_act, 4)
            link(v.scalar_tensor_tensor(tok[:, 5], tok[:, 1], 0.0, tok[:, 5], ALU.max, ALU.add))
            link(v.tensor_scalar(tok[:, 5], tok[:, 5], hb[:, 2:3], -1.0, ALU.mult, ALU.mult))
            link(v.tensor_tensor_scan(tok[:, 1], tokm[:], tok[:, 5], 0.0, ALU.mult, ALU.add))
            for ci, (c0, cn) in enumerate(CHUNKS):
                ins = v.tensor_copy(glast[:, ci:ci + 1], tok[:, 1, c0 + cn - 1:c0 + cn])
            link(ins)
            for ci, (c0, cn) in enumerate(CHUNKS):
                ins = v.tensor_scalar(tok[:, 3, c0:c0 + cn], tok[:, 1, c0:c0 + cn], glast[:, ci:ci + 1], -1.0,
                                      ALU.subtract, ALU.mult)
            ins.then_inc(gcum_ready, 1)
            dve.wait_ge(tok_act, 7)
            v.tensor_tensor(tok[:, 4], tok[:, 0], tok[:, 2], ALU.mult).then_inc(tok_ready, 1)
            for i in range(16):
                dve.wait_ge(qstd_ready, i + 1)
                link(v.reciprocal(conva[:, i % 2], conva[:, i % 2]))
                if i < 8:
                    ins = v.scalar_tensor_tensor(qkv[:, i], qkv[:, i], 128 ** -0.5, conva[:, i % 2], ALU.mult, ALU.mult)
                else:
                    ins = v.tensor_tensor(qkv[:, i], qkv[:, i], conva[:, i % 2], ALU.mult)
                ins.then_inc(qk_norm, 1)
            dve.wait_ge(qk_norm, 16)
            for i in range(2 * HN):
                j, hh = divmod(i, HN)
                dve.wait_ge(bc_done, i + 1)
                dst, src = (kb, qkv[:, 8 + hh]) if j == 0 else (qg, qkv[:, hh])
                v.tensor_tensor(dst[:, hh], src, banks[2 + i % 2][:, 0:N2], ALU.mult).then_inc(bc_used, 1)
            dve.wait_ge(toks_ready, 2)
            n_lv = 0
            for ci, (c0, cn) in enumerate(CHUNKS):
                def per_token(j, g, n):
                    return toks[0:cn, ci, j, 4 * g:4 * g + 4].unsqueeze(2).broadcast_to([cn, 4, n])

                def mask(lv):
                    return levels[0:cn, lv, 0:cn].unsqueeze(1).broadcast_to([cn, 4, cn])

                eye = ident[0:cn, 0:cn].unsqueeze(1).broadcast_to([cn, 4, cn])
                sub = {(g, n): grp[g][n][0:cn, :, 0:cn] for g in range(2) for n in ("dd", "mt", "qkd", "tt", "uu", "ml")}
                for g in range(2):
                    b0, G = 4 * g, grp[g]
                    dve.wait_ge(ktok_done, 2 * (2 * ci + g) + 1)
                    v.tensor_tensor(G["kbeg"][0:cn], quad(banks[b0], P, cn), per_token(2, g, P), ALU.mult) \
                        .then_inc(ktok_used, 1)
                    v.tensor_tensor(G["kdc"][0:cn], quad(banks[b0], P, cn), per_token(3, g, P), ALU.mult) \
                        .then_inc(ktok_used, 1)
                    dve.wait_ge(ktok_done, 2 * (2 * ci + g) + 2)
                    v.tensor_tensor(G["vb"][0:cn], quad(banks[b0 + 1], P, cn), per_token(0, g, P), ALU.mult) \
                        .then_inc(ktok_used, 1)
                    dve.wait_ge(dcy_done, 2 * ci + g + 1)
                    link(v.tensor_tensor(sub[g, "dd"], quad(banks[b0 + 2], cn), per_token(1, g, cn), ALU.subtract))
                    v.tensor_scalar(sub[g, "dd"], sub[g, "dd"], 0.0, None, ALU.min).then_inc(dcy_used, 1)
                for g in range(2):
                    dve.wait_ge(dcy_exp, 2 * ci + g + 1)
                    dve.wait_ge(gm_done, 4 * ci + g + 1)
                    v.tensor_tensor(sub[g, "mt"], quad(banks[4 * g + 3], cn), sub[g, "dd"], ALU.mult).then_inc(gm_used, 1)
                for g in range(2):
                    dve.wait_ge(gm_done, 4 * ci + 2 + g + 1)
                    link(v.tensor_tensor(sub[g, "qkd"], quad(banks[4 * g], cn), sub[g, "dd"], ALU.mult))
                    v.tensor_tensor(sub[g, "qkd"], sub[g, "qkd"], mask(LOG2P), ALU.mult).then_inc(gm_used, 1)
                for g in range(2):
                    dve.wait_ge(gm_used, 4 * ci + g + 1)
                    link(v.tensor_tensor(sub[g, "uu"], sub[g, "mt"], mask(0), ALU.mult))
                    v.tensor_tensor(sub[g, "uu"], eye, sub[g, "uu"], ALU.subtract).then_inc(mtu_ready, 1)
                nlev = cn.bit_length() - 1
                for lv in range(1, nlev):
                    for g in range(2):
                        if lv > 1:
                            dve.wait_ge(y_done, n_lv - 2 + g + 1)
                        v.tensor_tensor(sub[g, "ml"], sub[g, "mt"], mask(lv), ALU.mult).then_inc(ml_ready, 1)
                    for g in range(2):
                        dve.wait_ge(ty_done, n_lv + g + 1)
                        ins = v.tensor_tensor(sub[g, "uu"], sub[g, "uu"], quad(banks[4 * g + 2], cn), ALU.subtract)
                        if lv < nlev - 1:
                            ins = v.tensor_tensor(sub[g, "tt"], sub[g, "tt"], quad(banks[4 * g + 3], cn), ALU.subtract)
                        ins.then_inc(ty_used, 1)
                    n_lv += 2
                if ci < 2:
                    for g in range(2):
                        dve.wait_ge(s2_done, 2 * ci + g + 1)
                        for hh in range(4):
                            src = banks[4 * g + 3][:, hh * P:(hh + 1) * P]
                            n = 4 * g + hh
                            if ci == 0:
                                ins = v.tensor_copy(s2[:, n], src)
                            else:
                                ins = v.scalar_tensor_tensor(s2[:, n], s2[:, n], glb[:, n, ci:ci + 1], src, ALU.mult, ALU.add)
                        ins.then_inc(s2_ready, 1)
            for hh in range(HN):
                dve.wait_ge(ostd_ready, 1 + hh + 1)
                link(v.reciprocal(kb[:, hh % 2], kb[:, hh % 2]))
                link(v.scalar_tensor_tensor(on[:, hh], on[:, hh], col("a_norm", 0), kb[:, hh % 2], ALU.mult, ALU.mult))
                v.tensor_tensor(on[:, hh], on[:, hh], sz[:, hh], ALU.mult).then_inc(on_used, 1)
            remainder(6, on[:], N2)

            def add_to_h(t, s):
                v.scalar_tensor_tensor(h[:, ds(t, 1)], h[:, ds(t, 1)], ALPHA, banks[s][:, 0:N2].unsqueeze(1), ALU.mult,
                                       ALU.add).then_inc(banks_free, 1)

            def ln(i, gains, shifts, first):
                dve.wait_ge(mean_ready, i - LN0 + 1)
                v.tensor_tensor(h[:], h[:], lanes(banks[4][:, 0:N2], KD), ALU.subtract).then_inc(cent_ready, 1)
                dve.wait_ge(cent_ready, i - LN0 + 1)
                scaled(i, h[:], h[:], N2)
                affine(h[:], lambda k: col(gains, first + k), lambda k: col(shifts, first + k), True)

            lin("a_out", add_to_h)
            ln(LN0, "ln_mix_g", "ln_mix_b", 0)
            remainder(7, h[:], N2)
            conv2 = PV["conv2_w"]
            ffn(1, N2, [causal(conv2 + KF, 1), causal(conv2, 2)])
            down("down1", add_to_h)
            ln(LN0 + 1, "ln_ffn_g", "ln_ffn_b", 0)
            remainder(8, h[:], N2)
            t0 = TILE0["b_cx"]
            with dve.Fori(0, 4) as it:
                for p in range(2):
                    dve.wait_ge(banks_free, it * 4 + (t0 + 2 * p + 6))
                    dve.wait_ge(u_seq, it * 6 + (p + 1))
                    v.tensor_tensor(pbuf[:, p], abuf[:, p], vbuf[:, p], ALU.mult).then_inc(p_used, 1)
                for m, shift in enumerate((0, 1, 2)):
                    for p in range(2):
                        w = pv[:, ds(it * 2 + (PV["b_conv"] + 8 * (2 - shift) + p), 1)]
                        dst = ucv[:, ds(it * 2 + p, 1), shift:N2]
                        src = pbuf[:, p:p + 1, 0:N2 - shift]
                        if m == 0:
                            dve.wait_ge(p_used, it * 2 + (p + 3))
                            ins = v.tensor_scalar(dst, src, w, None, ALU.mult)
                        else:
                            dve.wait_ge(u_seq, it * 6 + (2 * (m - 1) + p + 3))
                            ins = v.scalar_tensor_tensor(dst, src, w, dst, ALU.mult, ALU.add)
                        ins.then_inc(u_seq, 1)
            dve.wait_ge(u_seq, 26)
            lin("b_b", lambda t, s: v.tensor_tensor(ucv[:, ds(t, 1)], banks[s][:, 0:N2].unsqueeze(1), ucv[:, ds(t, 1)],
                                                    ALU.mult).then_inc(banks_free, 1))
            remainder(9, ucv[:], N2)
            lin("b_out", add_to_h)
            ln(LN0 + 2, "ln_mix_g", "ln_mix_b", 8)
            remainder(10, h[:], N2)
            conv2 = PV["conv2_w"] + 3 * KF
            ffn(2, N2, [causal(conv2 + KF, 1), causal(conv2, 2)])
            down("down2", add_to_h)
            ln(LN0 + 3, "ln_ffn_g", "ln_ffn_b", 8)

    return nc


def _units(w, cols):
    k, m = w.shape
    t = w.reshape(k // P, P, m // P, P).transpose(2, 1, 0, 3)
    return t[list(cols)]


def _features(v):
    return v.reshape(-1, P).T


def _tokens(t):
    return t.T.reshape(KD, P, -1).transpose(1, 0, 2)


def _layout(i):
    f = np.asarray
    w_in = f(i["w_in"])[0]
    w_main = w_in[:, :7168]
    edge = {"w_u": 0, "w_vs": 8, "w_q": 16, "w_r": 20, "w_ga": 28, "w_gb": 36, "w_k": 44, "w_v": 48}
    tiles = {"w_u": 8, "w_vs": 8, "w_q": 4, "w_r": 8, "w_ga": 8, "w_gb": 8, "w_k": 4, "w_v": 8}
    parts = {n: _units(w_main, range(edge[n], edge[n] + tiles[n])) for n in edge}
    for n in ("w_br_a", "w_br_b", "w_o"):
        parts[n] = _units(f(i[n])[0], range(8))
    pair = [t for j in range(KF) for t in (j, KF + j)]
    parts["up0"] = _units(f(i["ffn_w_up"])[0], pair)
    a_in = f(i["a_w_in_2"])[0]
    parts["a_in"] = _units(a_in[:, :4096], range(32))
    parts["a_out"] = _units(f(i["a_w_out_2"])[0], range(8))
    b_in = f(i["b_w_in_2"])[0]
    parts["b_cx"] = _units(b_in, [t for j in range(8) for t in (8 + j, 16 + j)])
    parts["b_b"] = _units(b_in, range(8))
    parts["b_out"] = _units(f(i["b_w_out_2"])[0], range(8))
    for j in range(2):
        parts[f"up{j + 1}"] = _units(f(i["ffn_w_up_2"])[j], pair)
    d = {name: np.concatenate([parts[n] for n in names]) for name, names in STREAMS if names}
    d["down0"] = _units(f(i["ffn_w_down"])[0], range(8))
    for j in range(2):
        d[f"down{j + 1}"] = _units(f(i["ffn_w_down_2"])[j], range(8))
    d["x"], d["ctx"], d["meta"] = _tokens(f(i["x"])[0]), _tokens(f(i["ctx"])[0]), _tokens(f(i["meta_2"]))
    d["c"], d["c_ctx"] = f(i["c"]).reshape(D), f(i["c_ctx"]).reshape(D)
    d["w_ada"] = f(i["w_ada"])[0].T.reshape(24, 2, P, D).transpose(0, 2, 1, 3)
    d["w_lr"] = w_in[:, 7168:].reshape(KD, P, 2 * RANK).transpose(1, 0, 2)
    d["gla_w2"] = f(i["gla_w2"])[0]
    d["sgu_w"] = f(i["sgu_w"])[0].transpose(2, 0, 1)
    d["sgu_ln_g"], d["sgu_ln_b"] = f(i["sgu_ln_g"]).reshape(D), f(i["sgu_ln_b"]).reshape(D)
    d["sgu_b"] = f(i["sgu_b"]).reshape(D)
    d["w_ba"] = a_in[:, 4096:].reshape(KD, P, 2 * HN).transpose(1, 0, 2)
    d["a_log"], d["dt_bias"] = f(i["a_log_2"]).reshape(HN, 1), f(i["a_dt_bias_2"]).reshape(HN, 1)
    vectors = {"b_ada": i["b_ada"], "norm1_g": i["norm1_g"], "norm2_g": i["norm2_g"], "gla_b2": i["gla_b2"],
               "gla_norm_g": i["gla_norm_g"], "conv1_w": i["ffn_conv_w"], "conv1_b": i["ffn_conv_b"],
               "final_g": i["final_norm_g"], "a_conv": i["a_conv_2"], "a_norm": i["a_norm_2"], "b_conv": i["b_conv_2"],
               "ln_mix_g": i["ln_mix_g_2"], "ln_mix_b": i["ln_mix_b_2"], "conv2_w": i["ffn_conv_2"],
               "ln_ffn_g": i["ln_ffn_g_2"], "ln_ffn_b": i["ln_ffn_b_2"]}
    d["pv"] = np.concatenate([_features(f(vectors[n])) for n, _ in PV_PARTS], axis=1)
    t = np.arange(P)
    d["ident"] = np.eye(P, dtype=np.float32)
    d["averages"] = np.stack([np.full((P, P), 1 / n, np.float32) for n in (D, DV, P, 1)], axis=1)
    masks = []
    for lv in range(LOG2P):
        b = 2 ** lv
        same = (t[:, None] // (2 * b)) == (t[None, :] // (2 * b))
        masks.append(same & ((t[:, None] // b) % 2 == 0) & ((t[None, :] // b) % 2 == 1))
    masks.append(t[:, None] <= t[None, :])
    d["levels"] = np.stack(masks, axis=1).astype(np.float32)
    same = (t[:, None] // GC) == (t[None, :] // GC)
    d["gla_masks"] = np.stack([same & (t[:, None] <= t[None, :]), same & (t[:, None] >= t[None, :])], axis=1) \
        .astype(np.int32)
    d["sel"] = np.repeat(np.eye(HN, dtype=np.float32)[:, :, None], P, axis=2)
    return {n: np.ascontiguousarray(a) for n, a in d.items()}


def kernel(**inputs):
    import concourse.bacc as bacc
    from concourse.bass_utils import run_bass_kernel_spmd

    nc = bacc.Bacc("TRN2", target_bir_lowering=False, num_devices=1)
    arrays = {f"in_{n}": a for n, a in _layout(inputs).items()}
    args = {n[3:]: nc.dram_tensor(n, a.shape, mybir.dt.from_np(a.dtype), kind="ExternalInput").ap()
            for n, a in arrays.items()}
    out = nc.dram_tensor("out_h", (P, KD, N1), F32, kind="ExternalOutput").ap()
    bass_two_blocks(nc, args, out)
    r = run_bass_kernel_spmd(nc, [arrays], core_ids=[0])
    h = np.asarray(r.results[0]["out_h"])
    return np.ascontiguousarray(h.transpose(2, 1, 0).reshape(1, N1, D))
```

```python
from contextlib import ExitStack

import numpy as np

import concourse.bass as bass
from concourse import mybir

F32 = mybir.dt.float32
F32R = mybir.dt.float32r
I32 = mybir.dt.int32
ALU = mybir.AluOpType
ACT = mybir.ActivationFunctionType
ds = bass.ds

P = 128
D = 1024
KD = D // P
N1 = 256
META = 16
N2 = META + N1
FF = 2816
KF = FF // P
HG, DK, DV = 4, 128, 256
RANK = 16
GC = 64
GRID = 64
HN = 8
ALPHA = 4.0 ** 0.25
SLOTS = 4
UB = 8
CHUNKS = [(0, 128), (128, 128), (256, 16)]

PV_PARTS = [("b_ada", 48), ("norm1_g", 8), ("norm2_g", 8), ("gla_b2", 8), ("gla_norm_g", 8),
            ("conv1_w", 9 * KF), ("conv1_b", KF), ("final_g", 8), ("a_conv", 4 * 24), ("a_norm", 1),
            ("b_conv", 3 * 8), ("ln_mix_g", 16), ("ln_mix_b", 16), ("conv2_w", 2 * 3 * KF),
            ("ln_ffn_g", 16), ("ln_ffn_b", 16)]
PV = {}
PV_N = 0
for _name, _n in PV_PARTS:
    PV[_name] = PV_N
    PV_N += _n

LINEARS = [("w_k", 4, 4), ("w_q", 4, 4), ("w_v", 8, 8), ("w_u", 8, 8), ("w_vs", 8, 8), ("w_r", 8, 8),
           ("w_ga", 8, 8), ("w_gb", 8, 8), ("w_br_a", 8, 8), ("w_br_b", 8, 8), ("w_o", 8, 8),
           ("up0", 44, 44), ("down0", 8, 24), ("a_in", 32, 32), ("a_out", 8, 8), ("up1", 44, 44),
           ("down1", 8, 24), ("b_cx", 16, 16), ("b_b", 8, 8), ("b_out", 8, 8), ("up2", 44, 44),
           ("down2", 8, 24)]
UNIT0, TILE0 = {}, {}
_u = _t = 0
for _name, _tiles, _units in LINEARS:
    UNIT0[_name], TILE0[_name] = _u, _t
    _u += _units
    _t += _tiles
UNITS = _u
TILES_OF = {n: t for n, t, _ in LINEARS}
STREAMS = [("s0", ["w_k", "w_q", "w_v", "w_u", "w_vs", "w_r", "w_ga", "w_gb"]),
           ("s1", ["w_br_a", "w_br_b", "w_o", "up0"]), ("down0", None), ("s2", ["a_in", "a_out", "up1"]),
           ("down1", None), ("s3", ["b_cx", "b_b", "b_out", "up2"]), ("down2", None)]
DOWN_SPLIT = [(0, 8), (8, 8), (16, 6)]
LOG2P = 7


def bass_two_blocks(nc, a, out):
    ctx = ExitStack()
    with ctx:
        base = nc.sbuf_base + (-nc.sbuf_base) % 64
        where = [base]

        def at(name, shape, offset, dt=F32):
            return nc.alloc_sbuf_tensor_at(name, shape, dt, offset=offset)

        def sb(name, shape, dt=F32):
            n = 4 * int(np.prod(shape[1:]))
            t = at(name, shape, where[0], dt)
            where[0] += n + (-n) % 32
            return t

        def sem(name):
            return ctx.enter_context(nc.semaphore(name))

        w_raw = sb("w_raw", [P, SLOTS, UB, P])
        w_hi = sb("w_hi", [P, SLOTS, UB, P], F32R)
        w_lo = sb("w_lo", [P, SLOTS, UB, P], F32R)
        area_a = where[0]
        a_hi = sb("a_hi", [P, KD, 2 * N1], F32R)
        a_lo = sb("a_lo", [P, KD, 2 * N1], F32R)
        ident = sb("ident", [P, P])
        averages = sb("averages", [P, 4, P])
        over_d, over_dv, over_dh, ones = (averages[:, i] for i in range(4))
        levels = sb("levels", [P, LOG2P + 1, P])
        gla_masks = sb("gla_masks", [P, 2, P], I32)
        pv = sb("pv", [P, PV_N])
        mod = sb("mod", [P, 2, 48])
        dec = sb("dec", [P, 2, HG, 8])
        kmul = sb("kmul", [P, 2, HG, 8])
        qmul = sb("qmul", [P, 2, HG, 4])
        bdec = sb("bdec", [P, 2, HG, 2])
        gain = sb("gain", [P, 3, KD])
        eps6 = sb("eps6", [P, 2])
        area_c = where[0]
        csil = sb("csil", [P, D])
        stats = sb("stats", [P, 2, 2, 6])
        mv = sb("mv", [P, 2, 4])
        area_x = where[0]
        x = sb("x", [P, KD, N1])
        area_r = where[0]
        rstd = sb("rstd", [P, 2 * N1])
        area_h = where[0]
        h = sb("h", [P, KD, N2])
        area_s = where[0]
        sq = sb("sq", [P, KD, N2])
        arena = where[0]
        assert arena + 86016 <= nc.sbuf_usable_end, (arena, nc.sbuf_usable_end)

        q1 = at("q1", [P, HG, N1], arena)
        k1 = at("k1", [P, HG, 2 * N1], arena + 4096)
        vx = at("vx", [P, 2, D], arena + 12288)
        vc = at("vc", [P, 2, D], arena + 20480)
        ctxt = at("ctxt", [P, KD, N1], arena + 20480)
        sr = at("sr", [P, KD, N1], arena + 28672)
        ga = at("ga", [P, KD, N1], arena + 36864)
        gb = at("gb", [P, KD, N1], arena + 45056)
        hfull = at("hfull", [P, KD, 2 * N1], arena + 53248)
        ebuf = at("ebuf", [P, 2, HG, 2 * N1], arena + 53248)
        la = at("la", [P, 2, HG, 2 * N1], arena + 69632)
        adaw = at("adaw", [P, 2, 2, D], arena + 69632)
        rows = at("rows", [P, 3, D], arena + 69632)
        mixed = at("mixed", [P, 4, P], area_r)
        sguw = at("sguw", [P, 8, P], arena + 69632 + 12288)
        csil2 = at("csil2", [P, D], arena + 36864)
        wlr = at("wlr", [P, KD, 2 * RANK], arena + 28672)
        w2p = at("w2p", [2 * RANK, 2, HG * DK], arena + 28672 + 1024)
        lrt = at("lrt", [2 * RANK, 2 * N1], arena)
        reset = at("reset", [P, HG * 2 * N1], arena + 45056)
        gu = at("gu", [P, KD, N1], area_s)
        vs = at("vs", [P, 2, D], area_h)
        kd = at("kd", [P, HG, 2 * N1], arena + 69632)
        ks = at("ks", [P, HG, 2 * N1], arena + 77824)
        kt = at("kt", [P, 4, HG, DK], area_h)
        qd, qs, ki, sc, st0, st1 = [], [], [], [], [], []
        for d in range(2):
            o_ = area_a + 16384 * d
            qd.append(at(f"qd{d}", [P, HG, N1], o_))
            qs.append(at(f"qs{d}", [P, HG, N1], o_ + 4096))
            ki.append(at(f"ki{d}", [P, HG, N1], o_ + 8192))
            sc.append(at(f"sc{d}", [P, 2, HG, P], o_ + 12288))
            st0.append(at(f"st0{d}", [P, HG, DV], arena + 53248 + 8192 * d))
            st1.append(at(f"st1{d}", [P, HG, DV], arena + 53248 + 8192 * d + 4096))
        o1 = at("o1", [P, HG, 2, N1], area_s)
        osq = at("osq", [P, HG, 2, N1], area_h)
        orstd = at("orstd", [P, HG, N1], arena + 69632)

        junk = at("junk", [P, D], arena + 53248)

        g_hi = at("g_hi", [P, KF, N2], arena, F32R)
        g_lo = at("g_lo", [P, KF, N2], arena + 23936, F32R)
        off = arena + 47872
        abuf = at("abuf", [P, 2, N2], off)
        cbuf = at("cbuf", [P, 2, N2], off + 2176)
        vbuf = at("vbuf", [P, 2, N2], off + 4352)
        gbuf = at("gbuf", [P, 2, N2], off + 6528)
        gfull = at("gfull", [P, 2, N2], off + 8704)
        ucv = at("ucv", [P, KD, N2], arena)
        pbuf = at("pbuf", [P, 2, N2], off + 8704)

        qkv = at("qkv", [P, 24, N2], arena)
        kb = at("kb", [P, HN, N2], arena + 26112)
        qg = at("qg", [P, HN, N2], arena + 34816)
        sz = at("sz", [P, HN, N2], arena + 43520)
        convc = at("convc", [P, 4, N2], arena + 43520)
        on = at("on", [P, HN, N2], arena + 52224)
        conva = at("conva", [P, 4, N2], arena + 52224)
        s2 = at("s2", [P, HN, P], arena + 60928)
        sel = at("sel", [HN, HN, P], arena + 65024)
        tok = at("tok", [HN, 10, N2], arena + 69120)
        tokm = at("tokm", [HN, N2], arena + 80000)
        toks = at("toks", [P, 3, 5, HN], arena + 81088)
        glast = at("glast", [HN, 4], arena + 81568)
        glb = at("glb", [P, HN, 3], arena + 81600)
        hb = at("hb", [HN, 4], arena + 81696)
        wba = at("wba", [P, KD, 2 * HN], arena + 81728)
        pick = at("pick", [P, HN, HN], arena + 82240)
        cb = []
        for c, (_, cn) in enumerate(CHUNKS):
            B = {}
            if c < 2:
                for i, n in enumerate(("kbeg", "kdc", "vb", "mt")):
                    B[n] = at(f"{n}{c}", [P, HN, P], area_a + 16384 * c + 4096 * i)
                B["qkd"] = at(f"qkd{c}", [P, HN, P], area_x + 4096 * c)
                for i, n in enumerate(("tt", "uu", "ml0", "ml1")):
                    B[n] = at(f"{n}_{c}", [P, HN, P], arena + 16384 * c + 4096 * i)
                B["dd"] = at(f"dd{c}", [P, HN, P], arena + 52224 + 4096 * c)
                B["yy"] = at(f"yy{c}", [P, HN, P // 2], arena + 52224 + 2048 * c)
            else:
                B["kbeg"] = at("kbeg2", [P, HN, P], area_s)
                B["vb"] = at("vb2", [P, HN, P], area_s + 4096)
                for i, n in enumerate(("mt", "qkd", "tt", "uu", "ml0", "ml1", "dd")):
                    B[n] = at(f"{n}_2", [P, HN, cn], area_c + 512 * i)
                B["yy"] = at("yy2", [P, HN, cn // 2], area_c + 3584)
            cb.append(B)
        vnew2 = at("vnew2", [P, HN, P], area_x)

        banks = [ctx.enter_context(nc.psum_tensor(f"bank{i}", [P, 512], F32)) for i in range(8)]

        def sems(names):
            return [sem(n) for n in names.split()]

        landed = [sem(f"landed{i}") for i in range(SLOTS)]
        hi_ready, lo_ready, unit_used, banks_free = sems("hi_ready lo_ready unit_used banks_free")
        small_in, w2_in, c_in, ctx_in, sgu_in, h_in, gdn_in, fills = sems("small_in w2_in c_in ctx_in sgu_in h_in gdn_in fills")
        ada_in = sems("ada_in0 ada_in1")
        ada_seq, ada_used, csil_ready, ada_done = sems("ada_seq ada_used csil_ready ada_done")
        act_seq, dve_seq = sems("act_seq dve_seq")
        sq_ready, ms_ready, std_ready, mean_ready, cent_ready, normed = sems(
            "sq_ready ms_ready std_ready mean_ready cent_ready normed")
        split_hi, split_ready = sems("split_hi split_ready")
        lr_done, lr_ready, z_done, t_ready, log_ready, decay_ready = sems(
            "lr_done lr_ready z_done t_ready log_ready decay_ready")
        vs_var, vs_std, vn_ready, sgu_done, gated = sems("vs_var vs_std vn_ready sgu_done gated")
        diff_ready, exps_ready, kd_ready, ks_ready, qk_ready = sems("diff_ready exps_ready kd_ready ks_ready qk_ready")
        kt_done, kt_ready, sc_done, sc_ready, o_done, o_taken, up_done, st0_ready, st1_ready = sems(
            "kt_done kt_ready sc_done sc_ready o_done o_taken up_done st0_ready st1_ready")
        osq_ready, oms_done, ostd_ready, ob_ready, merged = sems("osq_ready oms_done ostd_ready ob_ready merged")
        conv_seq, conv_done, act_done, glu_done, g_rounded, g_ready = sems(
            "conv_seq conv_done act_done glu_done g_rounded g_ready")
        p_used, u_seq = sems("p_used u_seq")
        conv4_seq, conv4_done, conv4_act = sems("conv4_seq conv4_done conv4_act")
        ba_done, tok_act, gcum_ready, tok_ready, tokx_done, toks_ready = sems(
            "ba_done tok_act gcum_ready tok_ready tokx_done toks_ready")
        qsq_ready, qss_done, qstd_ready, bc_done, bc_used = sems("qsq_ready qss_done qstd_ready bc_done bc_used")
        pre_done, pre_used, dcy_used, dcy_exp, mt_ready, uu_init = sems(
            "pre_done pre_used dcy_used dcy_exp mt_ready uu_init")
        ml_ready, y_done, y_ready, ty_done, ty_used, ut_done = sems("ml_ready y_done y_ready ty_done ty_used ut_done")
        u_ready_act, u_ready_dve, vnew_act, vnew_dve = sems("u_ready_act u_ready_dve vnew_act vnew_dve")
        wt_done, wt_ready, vn_done, ov_done, ov_taken, s2_ready = sems(
            "wt_done wt_ready vn_done ov_done ov_taken s2_ready")
        onorm_sq, onorm_done, onorm_std, onorm_r, ob2_done, on_used, sz_ready = sems(
            "onorm_sq onorm_done onorm_std onorm_r ob2_done on_used sz_ready")
        stored = sem("stored")

        RMS_CTX, RMS_X, RMS_F, RMS_END, LN0 = 0, 1, 2, 3, 4

        def out_of(name):
            return TILE0[name] + TILES_OF[name] + 4

        STEPS = [(lv, c) for lv in range(1, LOG2P) for c, (_, cn) in enumerate(CHUNKS) if 2 ** lv < cn]
        STEP = {step: i for i, step in enumerate(STEPS)}
        FLIPS = list(range(len(CHUNKS))) + [c for _, c in STEPS]

        INV = [(0, (1, 2)), (3, (4, 5)), (6, (7,))]

        def firsts(ap, lv):
            return ap.rearrange("p h (n two b) -> p h n two b", two=2, b=2 ** lv)[:, :, :, 0]

        vnews = [cb[0]["ml0"], cb[1]["ml0"], vnew2]

        def octet(bs, cols, rows):
            per = HN // len(bs)
            return [(slice(per * i, per * i + per),
                     banks[b][0:rows, 0:per * cols].rearrange("p (h m) -> p h m", h=per)) for i, b in enumerate(bs)]

        def quad(bank, cols, rows=None):
            return bank[0:rows or cols, :].rearrange("p (h m) -> p h m", h=4)[:, :, 0:cols]

        block = ctx.enter_context(nc.Block())

        @block.sync
        def _(sp):
            def small(dst, src, s):
                sp.dma_start(dst, src).then_inc(s, 16)

            small(csil[:], a["c"].partition_broadcast(P), c_in)
            small(csil2[:], a["c_ctx"].partition_broadcast(P), c_in)
            small(ctxt[:], a["ctx"], ctx_in)
            small(x[:], a["x"], ctx_in)
            small(averages[:], a["averages"], small_in)
            small(pv[:], a["pv"], small_in)
            small(ident[:], a["ident"], small_in)
            small(levels[:], a["levels"], small_in)
            small(gla_masks[:], a["gla_masks"], small_in)
            small(wlr[:], a["w_lr"], small_in)

            def ada(pair, s):
                sp.dma_start(adaw[:, s], a["w_ada"][ds(pair, 1)].rearrange("o p t d -> (o p) t d")) \
                    .then_inc(ada_in[s], 16)

            for i in range(2):
                ada(i, i)
            with sp.Fori(1, 4) as it:
                for s in range(2):
                    sp.wait_ge(ada_seq, it * 8 + (4 * s - 3))
                    ada(it * 2 + s, s)

            def unit(src, s):
                sp.dma_start(w_raw[:, s], src).then_inc(landed[s], 16)

            def stream_unit(name, i, s):
                unit(a[name][ds(i, 1)].rearrange("o p k m -> (o p) k m"), s)

            u0 = 0
            for name, parts in STREAMS:
                if parts is None:
                    with sp.Fori(0, 2) as it:
                        for j in range(4):
                            for b, (k0, kn) in enumerate(DOWN_SPLIT):
                                n = 3 * j + b
                                sp.wait_ge(lo_ready, it * 12 + (u0 + n - 3))
                                unit_src = a[name][ds(it * 4 + j, 1), :, k0:k0 + kn] \
                                    .rearrange("o p k m -> (o p) k m")
                                sp.dma_start(w_raw[:, n % 4, 0:kn], unit_src).then_inc(landed[n % 4], 16)
                    if name == "down0":
                        sp.wait_ge(normed, 2)
                        small(h[:, :, 0:META], a["meta"], h_in)
                        small(wba[:], a["w_ba"], gdn_in)
                        small(sel[:], a["sel"], gdn_in)
                        small(pick[:], a["pick"], gdn_in)
                        small(hb[:, 0:1], a["a_log"], gdn_in)
                        small(hb[:, 1:2], a["dt_bias"], gdn_in)
                    u0 += 24
                    continue
                n = sum(TILES_OF[x_] for x_ in parts)
                first = 0
                if u0 == 0:
                    for s in range(SLOTS):
                        stream_unit(name, s, s)
                    first = 1
                    with sp.Fori(1, 4) as it:
                        for s in range(SLOTS):
                            sp.wait_ge(lo_ready, it * 4 + (s - 3))
                            stream_unit(name, it * 4 + s, s)
                    sp.wait_ge(decay_ready, 2)
                    with sp.Fori(4, 12) as it:
                        for s in range(SLOTS):
                            sp.wait_ge(lo_ready, it * 4 + (s - 3))
                            stream_unit(name, it * 4 + s, s)
                        for s in range(2):
                            sp.wait_ge(ada_used, it * 2 + (s - 1))
                            ada(it * 2 + s, s)
                    sp.wait_ge(ada_used, 24)
                    small(rows[:, 0], a["sgu_ln_g"].partition_broadcast(P), sgu_in)
                    small(rows[:, 1], a["sgu_ln_b"].partition_broadcast(P), sgu_in)
                    small(rows[:, 2], a["sgu_b"].partition_broadcast(P), sgu_in)
                    small(sguw[:], a["sgu_w"], sgu_in)
                    first = 12
                if u0 + first * 4 > 0:
                    with sp.Fori(first, n // 4) as it:
                        for s in range(SLOTS):
                            sp.wait_ge(lo_ready, it * 4 + (u0 + s - 3))
                            stream_unit(name, it * 4 + s, s)
                u0 += n
            sp.wait_ge(normed, 7)
            sp.dma_start(out, h[:, :, META:N2]).then_inc(stored, 16)
            sp.wait_ge(stored, 16)

        @block.gpsimd
        def _(pool):
            pool.memset(w2p[:], 0.0).then_inc(fills, 1)
            pool.memset(eps6[:, 0:1], 1e-6).then_inc(fills, 1)
            pool.memset(eps6[:, 1:2], 1e-5).then_inc(fills, 1)
            pool.sem_inc(banks_free, SLOTS)
            pool.sem_inc(u_seq, 2)
            pool.sem_inc(p_used, 2)
            pool.wait_ge(fills, 3)
            pool.dma_start(w2p[0:RANK, 0], a["gla_w2"][0]).then_inc(w2_in, 16)
            pool.dma_start(w2p[RANK:2 * RANK, 1], a["gla_w2"][1]).then_inc(w2_in, 16)
            def remainders(u0, u1):
                with pool.Fori(u0 // 4, u1 // 4) as it:
                    for s in range(SLOTS):
                        pool.wait_ge(hi_ready, it * 4 + (s + 1))
                        pool.tensor_tensor(w_lo[:, s], w_raw[:, s], w_hi[:, s].bitcast(F32), ALU.subtract) \
                            .then_inc(lo_ready, 1)

            ahead = UNIT0["a_out"] + SLOTS
            remainders(0, ahead)
            for c, (_, cn) in enumerate(CHUNKS):
                B = cb[c]
                uu, mt = B["uu"][0:cn], B["mt"][0:cn]
                pool.wait_ge(mt_ready, c + 1)
                if c < 2:
                    pool.wait_ge(pre_used, 15)
                pool.tensor_tensor(uu, mt, levels[0:cn, 0, 0:cn].unsqueeze(1).broadcast_to([cn, HN, cn]), ALU.mult) \
                    .then_inc(uu_init, 1)
                pool.wait_ge(uu_init, 2 * c + 1)
                pool.tensor_tensor(uu, ident[0:cn, 0:cn].unsqueeze(1).broadcast_to([cn, HN, cn]), uu, ALU.subtract) \
                    .then_inc(uu_init, 1)
            for i, (lv, c) in enumerate(STEPS):
                cn = CHUNKS[c][1]
                if lv > 2:
                    pool.wait_ge(y_done, STEP[lv - 2, c] + 1)
                pool.tensor_tensor(cb[c][f"ml{lv % 2}"][0:cn], cb[c]["mt"][0:cn],
                                   levels[0:cn, lv, 0:cn].unsqueeze(1).broadcast_to([cn, HN, cn]), ALU.mult) \
                    .then_inc(ml_ready, 1)
            remainders(ahead, UNITS)

        @block.tensor
        def _(pe):
            mm = nc.tensor.matmul

            def three(dst, pairs):
                n = 0
                last = 3 * len(pairs) - 1
                for (wh, wl), (xh, xl) in pairs:
                    for w_, x_ in ((wh, xh), (wh, xl), (wl, xh)):
                        ins = mm(dst, w_, x_, start=(n == 0), stop=(n == last))
                        n += 1
                return ins

            def lin(name, n):
                u0, t0 = UNIT0[name], TILE0[name]
                with pe.Fori(0, TILES_OF[name] // 4) as it:
                    for s in range(SLOTS):
                        pe.wait_ge(lo_ready, it * 4 + (u0 + s + 1))
                        pe.wait_ge(banks_free, it * 4 + (t0 + s + 1))
                        three(banks[s][:, 0:n], [((w_hi[:, s, k], w_lo[:, s, k]),
                                                  (a_hi[:, k, 0:n], a_lo[:, k, 0:n])) for k in range(KD)]) \
                            .then_inc(unit_used, 1)

            def lin_tokens(name, tiles):
                u0, t0 = UNIT0[name], TILE0[name]
                with pe.Fori(0, TILES_OF[name] // 4) as it:
                    for s in (0, 2):
                        pe.wait_ge(lo_ready, it * 4 + (u0 + s + 2))
                        pe.wait_ge(banks_free, it * 4 + (t0 + s + 2))
                        for t in range(tiles):
                            dst = banks[s + t * 2 // tiles][:, 256 * (t % (tiles // 2)):][:, 0:256] \
                                .rearrange("p (u m) -> p u m", u=2)
                            tk = slice(t * P, t * P + P)
                            n = 0
                            for k in range(KD):
                                wh, wl = w_hi[:, s:s + 2, k], w_lo[:, s:s + 2, k]
                                for x_, w_ in ((a_hi, wh), (a_lo, wh), (a_hi, wl)):
                                    ins = mm(dst, x_[:, k, tk], w_, start=(n == 0), stop=(n == 3 * KD - 1))
                                    n += 1
                        ins.then_inc(unit_used, 2)

            def down(name, n):
                u0, t0 = UNIT0[name], TILE0[name]
                with pe.Fori(0, 2) as it:
                    for j in range(4):
                        pe.wait_ge(banks_free, it * 4 + (t0 + j + 1))
                        m = 0
                        for b, (k0, kn) in enumerate(DOWN_SPLIT):
                            s = (3 * j + b) % 4
                            pe.wait_ge(lo_ready, it * 12 + (u0 + 3 * j + b + 1))
                            for k in range(kn):
                                for w_, x_ in ((w_hi, g_hi), (w_hi, g_lo), (w_lo, g_hi)):
                                    ins = mm(banks[j][:, 0:n], w_[:, s, k], x_[:, k0 + k, 0:n],
                                             start=(m == 0), stop=(m == 3 * KF - 1))
                                    m += 1
                            ins.then_inc(unit_used, 1)

            def mean_of(src, n, bank):
                for k in range(KD):
                    ins = mm(banks[bank][:, 0:n], over_d, src[:, k, 0:n], start=(k == 0), stop=(k == KD - 1))
                return ins

            def norm_ms(i, n):
                pe.wait_ge(sq_ready, i + 1)
                mean_of(sq, n, 4 if i == RMS_CTX else 5).then_inc(ms_ready, 1)

            def ln_norm(i):
                j = i - LN0
                name = ("a_out", "down1", "b_out", "down2")[j]
                pe.wait_ge(banks_free, out_of(name))
                mean_of(h, N2, 4).then_inc(mean_ready, 1)
                norm_ms(i, N2)

            pe.wait_ge(small_in, 16 * 6)
            norm_ms(RMS_CTX, N1)
            norm_ms(RMS_X, N1)
            pe.wait_ge(normed, 1)
            for k in range(KD):
                ins = mm(banks[6][0:2 * RANK, :], wlr[:, k], hfull[:, k], start=(k == 0), stop=(k == KD - 1))
            ins.then_inc(lr_done, 1)
            pe.wait_ge(split_ready, 1)
            lin("w_k", 2 * N1)
            pe.wait_ge(lr_ready, 1)
            pe.wait_ge(w2_in, 32)
            for i in range(2 * HG):
                d, hh = divmod(i, HG)
                if i >= 4:
                    pe.wait_ge(t_ready, i - 3)
                mm(banks[4 + i % 4][:, :], w2p[:, d, hh * DK:(hh + 1) * DK], lrt[:], start=True, stop=True) \
                    .then_inc(z_done, 1)
            lin("w_q", N1)
            lin_tokens("w_v", 4)
            lin("w_u", N1)
            lin_tokens("w_vs", 2)
            lin("w_r", N1)
            lin("w_ga", N1)
            lin("w_gb", N1)

            pe.wait_ge(sgu_in, 64)
            pe.wait_ge(t_ready, 8)
            for n in range(2):
                pe.wait_ge(vn_ready, n + 1)
                for half in range(2):
                    for g in range(4):
                        gg = 4 * half + g
                        ins = mm(banks[4 + 2 * n + half][:, g * P:(g + 1) * P], vs[:, n, gg * P:(gg + 1) * P],
                                 sguw[:, gg], start=True, stop=True)
                    ins.then_inc(sgu_done, 1)
            pe.wait_ge(split_ready, 2)
            lin("w_br_a", N1)

            for d in range(2):
                pe.wait_ge(qk_ready, 2 * d + 2)
                pe.wait_ge(kd_ready, d + 1)
                for blk in range(2):
                    if d:
                        pe.wait_ge(sc_ready, 2)
                    e, l = GC * d, GC * (1 - d)
                    tk = slice(blk * P, (blk + 1) * P)
                    for hh in range(HG):
                        mm(banks[6 + blk][:, hh * P:(hh + 1) * P], ki[d][:, hh, tk], qd[d][:, hh, tk],
                           start=True, stop=True)
                        ins = mm(banks[6 + blk][e:e + GC, hh * P + l:hh * P + l + GC],
                                 kd[:, hh, blk * P + e:blk * P + e + GC], qd[d][:, hh, blk * P + l:blk * P + l + GC],
                                 start=True, stop=True)
                    ins.then_inc(sc_done, 1)
                pe.wait_ge(ks_ready, d + 1)
                for blk in range(4):
                    if blk >= 2 or d:
                        pe.wait_ge(kt_ready, 4 * d + blk - 1)
                    for hh in range(HG):
                        ins = nc.tensor.transpose(banks[4 + blk % 2][:, hh * DK:(hh + 1) * DK],
                                                  ks[:, hh, blk * P:(blk + 1) * P], ident[:])
                    ins.then_inc(kt_done, 1)
                pe.wait_ge(kt_ready, 4 * d + 4)
                if d:
                    pe.wait_ge(st0_ready, 1)
                    pe.wait_ge(st1_ready, 1)
                for hh in range(HG):
                    for blk in range(2):
                        ins = mm(banks[hh // 2][:, (hh % 2) * DV:(hh % 2 + 1) * DV], kt[:, 2 + blk, hh],
                                 vc[:, blk, hh * DV:(hh + 1) * DV], start=(blk == 0), stop=(blk == 1))
                ins.then_inc(up_done, 1)
                for hh in range(HG):
                    ins = mm(banks[2 + hh // 2][:, (hh % 2) * DV:(hh % 2 + 1) * DV], kt[:, d, hh],
                             vx[:, d, hh * DV:(hh + 1) * DV], start=True, stop=True)
                ins.then_inc(up_done, 1)
            pe.wait_ge(sc_ready, 4)
            pe.wait_ge(st0_ready, 2)
            pe.wait_ge(st1_ready, 2)
            for blk in range(2):
                for hh in range(HG):
                    for half in range(2):
                        c0, col = ((hh % 2) * 2 + half) * P, hh * DV + half * P
                        dst = banks[4 + 2 * blk + hh // 2][:, c0:c0 + P]
                        for d in range(2):
                            state = (st0 if blk == d else st1)[d]
                            mm(dst, vx[:, blk, col:col + P], sc[d][:, blk, hh], start=(d == 0), stop=False)
                            ins = mm(dst, state[:, hh, half * P:(half + 1) * P], qs[d][:, hh, blk * P:(blk + 1) * P],
                                     start=False, stop=(d == 1))
                    if hh % 2:
                        ins.then_inc(o_done, 1)
            for b in range(2):
                pe.wait_ge(osq_ready, b + 1)
                for hh in (2 * b, 2 * b + 1):
                    for half in range(2):
                        ins = mm(banks[b][:, (hh % 2) * N1:(hh % 2 + 1) * N1], over_dv, osq[:, hh, half],
                                 start=(half == 0), stop=(half == 1))
                ins.then_inc(oms_done, 1)
            pe.wait_ge(split_ready, 3)
            lin("w_br_b", N1)
            pe.wait_ge(split_ready, 4)
            lin("w_o", N1)
            norm_ms(RMS_F, N1)
            pe.wait_ge(split_ready, 5)
            lin("up0", N1)
            pe.wait_ge(g_ready, KF)
            down("down0", N1)
            norm_ms(RMS_END, N1)

            pe.wait_ge(gdn_in, 80)
            pe.wait_ge(h_in, 16)
            pe.wait_ge(normed, 3)
            for j in range(2):
                for k in range(KD):
                    ins = mm(banks[6 + j][0:HN, 0:N2], wba[:, k, j * HN:(j + 1) * HN], h[:, k],
                             start=(k == 0), stop=(k == KD - 1))
                ins.then_inc(ba_done, 1)
            pe.wait_ge(split_ready, 6)
            lin("a_in", N2)
            pe.wait_ge(qsq_ready, 2)
            for j, src in enumerate((sq, kb)):
                for hh in range(HN):
                    ins = mm(banks[4 + j][0:HN, 0:N2], pick[:, hh], src[:, hh], start=(hh == 0), stop=(hh == HN - 1))
                ins.then_inc(qss_done, 1)
            pe.wait_ge(tok_ready, 1)
            for ci, (c0, cn) in enumerate(CHUNKS):
                for j, r in enumerate((0, 1, 4, 3, 7)):
                    ins = nc.tensor.transpose(banks[6][0:cn, (5 * ci + j) * HN:(5 * ci + j + 1) * HN],
                                              tok[:, r, c0:c0 + cn], ident[0:HN, 0:HN])
            ins.then_inc(tokx_done, 1)
            for hh in range(HN):
                ins = mm(banks[7][:, 3 * hh:3 * hh + 3], sel[:, hh], glast[:, 0:3], start=True, stop=True)
            ins.then_inc(tokx_done, 1)
            for i in range(3 * HN):
                j, hh = divmod(i, HN)
                if i >= 4:
                    pe.wait_ge(bc_used, i - 3)
                mm(banks[i % 4][:, 0:N2], sel[:, hh], tok[:, (9, 8, 6)[j]], start=True, stop=True).then_inc(bc_done, 1)
            pe.wait_ge(toks_ready, 2)
            n = 0
            for ci, (c0, cn) in enumerate(CHUNKS):
                tk = slice(c0, c0 + cn)
                for stage in range(5):
                    if n < 4:
                        pe.wait_ge(bc_used, 24)
                    else:
                        pe.wait_ge(pre_used, n - 3)
                    pair = (2 * (n % 4), 2 * (n % 4) + 1)
                    width = P if stage in (1, 2) else cn
                    for heads, dst in octet(pair, width, cn):
                        for i in range(4):
                            hh = heads.start + i
                            if stage == 0:
                                ins = mm(dst[:, i], sel[:, hh, 0:cn], tok[:, 1, tk], start=True, stop=True)
                            elif stage in (1, 2):
                                ins = nc.tensor.transpose(dst[:, i], qkv[:, 8 * stage + hh, tk], ident[:])
                            else:
                                src = kb if stage == 3 else qkv
                                ins = mm(dst[:, i], qkv[:, 8 + hh, tk], src[:, hh, tk], start=True, stop=True)
                    ins.then_inc(pre_done, 1)
                    n += 1
            pe.wait_ge(pre_used, 15)

            def flip(c, src, dst_sem):
                cn = CHUNKS[c][1]
                for heads, dst in octet(INV[c][1], cn, cn):
                    for i in range(heads.stop - heads.start):
                        ins = nc.tensor.transpose(dst[:, i], cb[c][src][0:cn, heads.start + i], ident[0:cn, 0:cn])
                ins.then_inc(dst_sem, 1)

            def wait_flip(n):
                pe.wait_ge(u_ready_act, n + 1)
                pe.wait_ge(u_ready_dve, sum(c < 2 for c in FLIPS[:n + 1]))

            for c in range(3):
                pe.wait_ge(uu_init, 2 * c + 2)
                flip(c, "uu", ut_done)
            for lv in range(1, LOG2P):
                now = [c for c in range(3) if (lv, c) in STEP]
                before = {c: STEP[lv - 1, c] if lv > 1 else None for c in now}
                for c in now:
                    cn, B, i = CHUNKS[c][1], cb[c], STEP[lv, c]
                    pe.wait_ge(ml_ready, i + 1)
                    if lv > 1:
                        pe.wait_ge(ty_used, before[c] + 1)
                    else:
                        wait_flip(c)
                    for heads, dst in octet((INV[c][0],), cn // 2, cn):
                        for hh in range(HN):
                            ins = mm(dst[:, hh].rearrange("p (n b) -> p n b", b=2 ** lv), B[f"ml{lv % 2}"][0:cn, hh],
                                     firsts(B["tt"][0:cn], lv)[:, hh], start=True, stop=True)
                    ins.then_inc(y_done, 1)
                for c in now:
                    cn, B, i = CHUNKS[c][1], cb[c], STEP[lv, c]
                    pe.wait_ge(y_ready, i + 1)
                    if lv > 1:
                        wait_flip(3 + before[c])
                    for heads, dst in octet((INV[c][0],), cn // 2, cn):
                        for hh in range(HN):
                            ins = mm(dst[:, hh], B["uu"][0:cn, hh], B["yy"][0:cn, hh], start=True, stop=True)
                    ins.then_inc(ty_done, 1)
                for c in now:
                    pe.wait_ge(ty_used, STEP[lv, c] + 1)
                    flip(c, "tt", ut_done)
            wait_flip(len(FLIPS) - 1)

            def w_t(c):
                cn, B = CHUNKS[c][1], cb[c]
                if c == 2:
                    pe.wait_ge(wt_ready, 1)
                for heads, dst in octet((4, 5), cn, P):
                    for i in range(4):
                        hh = heads.start + i
                        ins = mm(dst[:, i], B["kbeg"][0:cn, hh], B["uu"][0:cn, hh], start=True, stop=True)
                ins.then_inc(wt_done, 1)

            for c, (c0, cn) in enumerate(CHUNKS):
                B, tk = cb[c], slice(c0, c0 + cn)
                vnew = vnews[c]
                if c:
                    pe.wait_ge(wt_ready, c)
                    pe.wait_ge(s2_ready, c)
                for heads, dst in octet((0, 1), P, cn):
                    for i in range(4):
                        hh = heads.start + i
                        ins = mm(dst[:, i], B["uu"][0:cn, hh], B["vb"][0:cn, hh], start=True, stop=(c == 0))
                        if c:
                            ins = mm(dst[:, i], B["tt"][:, hh], s2[:, hh], start=False, stop=True)
                ins.then_inc(vn_done, 1)
                if c < 2:
                    w_t(c + 1)
                pe.wait_ge(vnew_act, c + 1)
                pe.wait_ge(vnew_dve, c + 1)
                if c:
                    pe.wait_ge(ov_taken, c)
                if c < 2:
                    for heads, dst in octet((6, 7), P, P):
                        for i in range(4):
                            hh = heads.start + i
                            ins = mm(dst[:, i], B["kdc"][0:cn, hh], vnew[0:cn, hh], start=True, stop=True)
                for heads, dst in octet((2, 3), cn, P):
                    for i in range(4):
                        hh = heads.start + i
                        ins = mm(dst[:, i], vnew[0:cn, hh], B["qkd"][0:cn, hh], start=True, stop=(c == 0))
                        if c:
                            ins = mm(dst[:, i], s2[:, hh], qg[:, hh, tk], start=False, stop=True)
                ins.then_inc(ov_done, 1)
            pe.wait_ge(onorm_sq, 1)
            for hh in range(HN):
                ins = mm(banks[4][0:HN, 0:N2], pick[:, hh], sq[:, hh], start=(hh == 0), stop=(hh == HN - 1))
            ins.then_inc(onorm_done, 1)
            pe.wait_ge(onorm_r, 1)
            for hh in range(HN):
                if hh >= 4:
                    pe.wait_ge(on_used, hh - 3)
                mm(banks[hh % 4][:, 0:N2], sel[:, hh], tok[:, 5], start=True, stop=True).then_inc(ob2_done, 1)
            pe.wait_ge(split_ready, 7)
            lin("a_out", N2)
            ln_norm(LN0)
            pe.wait_ge(split_ready, 8)
            lin("up1", N2)
            pe.wait_ge(g_ready, 2 * KF)
            down("down1", N2)
            ln_norm(LN0 + 1)
            pe.wait_ge(split_ready, 9)
            lin("b_cx", N2)
            lin("b_b", N2)
            pe.wait_ge(split_ready, 10)
            lin("b_out", N2)
            ln_norm(LN0 + 2)
            pe.wait_ge(split_ready, 11)
            lin("up2", N2)
            pe.wait_ge(g_ready, 3 * KF)
            down("down2", N2)
            ln_norm(LN0 + 3)

        @block.scalar
        def _(act):
            act_n = [0]

            def link(ins):
                act_n[0] += 1
                ins.then_inc(act_seq, 1)
                act.wait_ge(act_seq, act_n[0])

            def fn(out_, in_, f, **kw):
                return nc.scalar.activation(out_, in_, f, **kw)

            def round_unit(u, s):
                act.wait_ge(landed[s], u * 4 + 16 - 4 * s)
                fn(w_hi[:, s], w_raw[:, s], ACT.Copy).then_inc(hi_ready, 1)

            def lin(name, evac, units=None, ahead=True):
                u0 = UNIT0[name]
                with act.Fori(0, TILES_OF[name] // 4) as it:
                    for s in range(SLOTS):
                        act.wait_ge(unit_used, it * 4 + (u0 + s + 1))
                        if evac is not None:
                            evac(it * 4 + s, s)
                        round_unit(it * 4 + (u0 + s + 4), s)

            def down(name, last=False):
                u0 = UNIT0[name]
                if last:
                    with act.Fori(0, 5) as it:
                        for s in range(SLOTS):
                            act.wait_ge(unit_used, it * 4 + (u0 + s + 1))
                            round_unit(it * 4 + (u0 + s + 4), s)
                    return
                with act.Fori(0, 6) as it:
                    for s in range(SLOTS):
                        act.wait_ge(unit_used, it * 4 + (u0 + s + 1))
                        round_unit(it * 4 + (u0 + s + 4), s)

            def split(src, n, ready, count):
                act.wait_ge(ready, count)
                fn(a_hi[:, :, 0:n], src, ACT.Copy).then_inc(split_hi, 1)

            def square(i, src, n):
                fn(sq[:, :, 0:n], src, ACT.Square).then_inc(sq_ready, 1)

            def root(i, n, e):
                act.wait_ge(ms_ready, i + 1)
                c0, bank = (N1, 4) if i == RMS_CTX else (0, 5)
                fn(rstd[:, c0:c0 + n], banks[bank][:, 0:n], ACT.Sqrt, bias=eps6[:, e:e + 1]).then_inc(std_ready, 1)

            act.wait_ge(fills, 3)
            act.wait_ge(c_in, 32)
            fn(csil[:], csil[:], ACT.Silu).then_inc(csil_ready, 1)
            fn(csil2[:], csil2[:], ACT.Silu).then_inc(csil_ready, 1)
            act.wait_ge(ctx_in, 32)
            square(RMS_CTX, ctxt[:], N1)
            root(RMS_CTX, N1, 0)
            square(RMS_X, x[:], N1)
            root(RMS_X, N1, 0)
            for s in range(SLOTS):
                round_unit(s, s)
            split(hfull[:], 2 * N1, normed, 1)
            act.wait_ge(lr_done, 1)
            fn(lrt[:], banks[6][0:2 * RANK, :], ACT.Copy).then_inc(lr_ready, 1)
            lin("w_k", lambda t, s: fn(k1[:, ds(t, 1)], banks[s][:, :].unsqueeze(1), ACT.Copy).then_inc(banks_free, 1))
            act.wait_ge(z_done, 8)
            lin("w_q", lambda t, s: fn(q1[:, ds(t, 1)], banks[s][:, 0:N1].unsqueeze(1), ACT.Copy, scale=DK ** -0.5)
                .then_inc(banks_free, 1))
            act.wait_ge(t_ready, 8)
            link(fn(ebuf[:], la[:], ACT.Abs))
            link(fn(ebuf[:], ebuf[:], ACT.Exp, scale=-1.0))
            fn(ebuf[:], ebuf[:], ACT.Ln, bias=1.0).then_inc(log_ready, 1)

            def evac_v(t, s):
                if s % 2 == 0:
                    return
                for b, dst in ((s - 1, vx), (s, vc)):
                    fn(dst[:, :, ds((t - 1) * P, 2 * P)], banks[b][:, :].rearrange("p (t m) -> p t m", t=2), ACT.Copy) \
                        .then_inc(banks_free, 1)

            lin("w_v", evac_v)
            lin("w_u", lambda t, s: fn(gu[:, ds(t, 1)], banks[s][:, 0:N1].unsqueeze(1), ACT.Gelu).then_inc(banks_free, 1))

            def evac_vs(t, s):
                if s % 2 == 0:
                    return
                for b in range(2):
                    fn(vs[:, b, ds((t - 1) * P, 2 * P)], banks[s - 1 + b][:, 0:2 * P], ACT.Gelu).then_inc(banks_free, 1)

            lin("w_vs", evac_vs)
            act.wait_ge(decay_ready, 2)
            nc.scalar.preload_act_table(ACT.Silu)
            lin("w_r", lambda t, s: fn(sr[:, ds(t, 1)], banks[s][:, 0:N1].unsqueeze(1), ACT.Silu).then_inc(banks_free, 1))
            nc.scalar.preload_act_table(ACT.Sigmoid)
            act.wait_ge(ada_used, 8)
            lin("w_ga", lambda t, s: fn(ga[:, ds(t, 1)], banks[s][:, 0:N1].unsqueeze(1), ACT.Sigmoid).then_inc(banks_free, 1))
            act.wait_ge(vs_var, 2)
            for n in range(2):
                fn(mv[:, n, 2:3], mv[:, n, 1:2], ACT.Sqrt, bias=eps6[:, 0:1]).then_inc(vs_std, 1)
            nc.scalar.preload_act_table(ACT.Sigmoid)
            lin("w_gb", lambda t, s: fn(gb[:, ds(t, 1)], banks[s][:, 0:N1].unsqueeze(1), ACT.Sigmoid).then_inc(banks_free, 1))
            split(gu[:], N1, gated, 8)
            lin("w_br_a", None)
            act.wait_ge(banks_free, out_of("w_br_a"))

            def powers(d):
                fn(qd[d][:], ebuf[:, d, :, 0:N1], ACT.Exp, scale=1 / 16).then_inc(exps_ready, 1)
                fn(ki[d][:], ebuf[:, d, :, 0:N1], ACT.Exp, scale=-1 / 16).then_inc(exps_ready, 1)
                flat = ebuf[:, d].rearrange("p h (c t) -> p h c t", t=GC)
                last = flat[:, :, :, GC - 1] if d == 0 else flat[:, :, :, 0]
                fn(dec[:, d], last, ACT.Exp, scale=1 / 16).then_inc(exps_ready, 1)

            def key_powers(d):
                act.wait_ge(diff_ready, d + 1)
                fn(kd[:], kd[:], ACT.Exp, scale=1 / 16).then_inc(exps_ready, 1)

            def states(d):
                for blk in range(4):
                    act.wait_ge(kt_done, 4 * d + blk + 1)
                    if d and blk == 0:
                        act.wait_ge(up_done, 2)
                    fn(kt[:, blk], banks[4 + blk % 2][:, :].rearrange("p (h k) -> p h k", h=HG), ACT.Copy) \
                        .then_inc(kt_ready, 1)
                act.wait_ge(up_done, 2 * d + 1)
                for b in range(2):
                    ins = fn(st0[d][:, 2 * b:2 * b + 2], banks[b][:, :].rearrange("p (h v) -> p h v", h=2), ACT.Copy)
                ins.then_inc(st0_ready, 1)

            powers(0)
            key_powers(0)
            powers(1)
            act.wait_ge(exps_ready, 7)
            states(0)
            key_powers(1)
            act.wait_ge(exps_ready, 8)
            states(1)
            for b in range(2):
                act.wait_ge(o_taken, 3 + b)
                if b == 0:
                    act.wait_ge(up_done, 4)
                fn(osq[:, 2 * b:2 * b + 2], o1[:, 2 * b:2 * b + 2], ACT.Square).then_inc(osq_ready, 1)
            for b in range(2):
                act.wait_ge(oms_done, b + 1)
                fn(orstd[:, 2 * b:2 * b + 2], banks[b][:, :].rearrange("p (h t) -> p h t", h=2), ACT.Sqrt,
                   bias=eps6[:, 0:1]).then_inc(ostd_ready, 1)
            split(o1[:].rearrange("p h v t -> p (h v) t"), N1, ob_ready, 8)
            lin("w_br_b", None)
            split(gb[:], N1, merged, 8)
            lin("w_o", None)
            act.wait_ge(banks_free, out_of("w_o"))
            square(RMS_F, x[:], N1)
            root(RMS_F, N1, 0)
            split(sq[:, :, 0:N1], N1, normed, 2)

            def ffn(i, n, f, w_center, bias):
                name = f"up{i}"
                u0, j0 = UNIT0[name], KF * i
                nc.scalar.preload_act_table(f)

                def activate(j, p):
                    act.wait_ge(conv_done, j + (j0 + p + 1))
                    fn(gbuf[:, p, 0:n], cbuf[:, p, 0:n], f).then_inc(act_done, 1)

                def tiles(it, first):
                    for p in range(2):
                        s = 2 * p
                        u = it * 4 + (u0 + s)
                        act.wait_ge(unit_used, u + 1)
                        if not first:
                            act.wait_ge(act_done, it * 2 + (j0 + p - 1))
                        fn(abuf[:, p, 0:n], banks[s][:, 0:n], ACT.Copy)
                        kw = {"scale": pv[:, ds(it * 2 + (w_center + p), 1)]}
                        if bias is not None:
                            kw["bias"] = pv[:, ds(it * 2 + (bias + p), 1)]
                        fn(cbuf[:, p, 0:n], banks[s][:, 0:n], ACT.Identity, **kw).then_inc(banks_free, 1)
                        round_unit(u + 4, s)
                        act.wait_ge(unit_used, u + 2)
                        if not first:
                            act.wait_ge(glu_done, it * 2 + (j0 + p - 1))
                        fn(vbuf[:, p, 0:n], banks[s + 1][:, 0:n], ACT.Copy).then_inc(banks_free, 1)
                        round_unit(u + 5, s + 1)

                tiles(0, True)
                with act.Fori(1, KF // 2) as it:
                    for p in range(2):
                        activate(it * 2 - 2, p)
                    tiles(it, False)
                for p in range(2):
                    activate(KF - 2, p)

            ffn(0, N1, ACT.Gelu, PV["conv1_w"] + 4 * KF, PV["conv1_b"])
            down("down0")
            act.wait_ge(banks_free, out_of("down0"))
            square(RMS_END, x[:], N1)
            root(RMS_END, N1, 0)
            act.wait_ge(h_in, 16)
            split(h[:], N2, normed, 3)
            act.wait_ge(gdn_in, 80)
            act.wait_ge(ba_done, 2)
            fn(tok[:, 0], banks[6][0:HN, 0:N2], ACT.Sigmoid).then_inc(tok_act, 1)
            fn(tok[:, 1], banks[7][0:HN, 0:N2], ACT.Identity, bias=hb[:, 1:2]).then_inc(tok_act, 1)
            fn(hb[:, 2:3], hb[:, 0:1], ACT.Exp).then_inc(tok_act, 1)
            act.wait_ge(tok_act, 2)
            link(fn(tok[:, 5], tok[:, 1], ACT.Abs))
            link(fn(tok[:, 5], tok[:, 5], ACT.Exp, scale=-1.0))
            fn(tok[:, 5], tok[:, 5], ACT.Ln, bias=1.0).then_inc(tok_act, 1)
            act.wait_ge(gcum_ready, 1)
            fn(tok[:, 2], tok[:, 1], ACT.Exp).then_inc(tok_act, 1)
            fn(tok[:, 3], tok[:, 3], ACT.Exp).then_inc(tok_act, 1)
            fn(glast[:, 0:3], glast[:, 0:3], ACT.Exp).then_inc(tok_act, 1)

            u0 = UNIT0["a_in"]

            def qkv_tiles(it, first):
                for s in range(SLOTS):
                    act.wait_ge(unit_used, it * 4 + (u0 + s + 1))
                    if not first:
                        act.wait_ge(conv4_act, it * 4 + (s - 3))
                    fn(conva[:, s], banks[s][:, 0:N2], ACT.Copy)
                    fn(convc[:, s], banks[s][:, 0:N2], ACT.Copy, scale=pv[:, ds(it * 4 + (PV["a_conv"] + 3 * 24 + s), 1)]) \
                        .then_inc(banks_free, 1)
                    round_unit(it * 4 + (u0 + s + 4), s)

            def qkv_activate(it):
                for s in range(SLOTS):
                    act.wait_ge(conv4_done, it * 4 + (s + 1))
                    fn(qkv[:, ds(it * 4 + s, 1)], convc[:, s].unsqueeze(1), ACT.Silu).then_inc(conv4_act, 1)

            nc.scalar.preload_act_table(ACT.Silu)
            qkv_tiles(0, True)
            with act.Fori(1, 6) as it:
                qkv_activate(it - 1)
                qkv_tiles(it, False)
            qkv_activate(5)
            act.wait_ge(conv4_act, 24)
            fn(sq[:], qkv[:, 0:8], ACT.Square).then_inc(qsq_ready, 1)
            fn(kb[:], qkv[:, 8:16], ACT.Square).then_inc(qsq_ready, 1)
            with act.Fori(0, 2) as it:
                for s in range(SLOTS):
                    act.wait_ge(unit_used, it * 4 + (u0 + 24 + s + 1))
                    fn(sz[:, ds(it * 4 + s, 1)], banks[s][:, 0:N2].unsqueeze(1), ACT.Silu).then_inc(banks_free, 1)
                    round_unit(it * 4 + (u0 + 24 + s + 4), s)
            for j in range(2):
                act.wait_ge(qss_done, j + 1)
                fn(tok[:, 6 + j], banks[4 + j][0:HN, 0:N2], ACT.Sqrt, bias=eps6[0:HN, 0:1]).then_inc(qstd_ready, 1)
            act.wait_ge(tokx_done, 2)
            for ci, (c0, cn) in enumerate(CHUNKS):
                ins = fn(toks[0:cn, ci], banks[6][0:cn, ci * 5 * HN:(ci + 1) * 5 * HN]
                         .rearrange("p (j h) -> p j h", j=5), ACT.Copy)
            ins.then_inc(toks_ready, 1)
            fn(glb[:], banks[7][:, 0:3 * HN].rearrange("p (h c) -> p h c", h=HN), ACT.Copy).then_inc(toks_ready, 1)
            nc.scalar.preload_act_table(ACT.Exp)
            for c, (_, cn) in enumerate(CHUNKS):
                act.wait_ge(dcy_used, c + 1)
                fn(cb[c]["dd"][0:cn], cb[c]["dd"][0:cn], ACT.Exp).then_inc(dcy_exp, 1)

            def flipped(c, dst, n):
                cn = CHUNKS[c][1]
                act.wait_ge(ut_done, n + 1)
                heads, src = octet(INV[c][1], cn, cn)[0]
                fn(cb[c][dst][0:cn, heads], src, ACT.Copy).then_inc(u_ready_act, 1)

            for c in range(3):
                flipped(c, "tt", c)
            for lv in range(1, LOG2P):
                now = [c for c in range(3) if (lv, c) in STEP]
                for c in now:
                    cn = CHUNKS[c][1]
                    act.wait_ge(y_done, STEP[lv, c] + 1)
                    _, src = octet((INV[c][0],), cn // 2, cn)[0]
                    fn(cb[c]["yy"][0:cn], src, ACT.Copy).then_inc(y_ready, 1)
                for c in now:
                    flipped(c, "uu", 3 + STEP[lv, c])
            for c, (c0, cn) in enumerate(CHUNKS):
                act.wait_ge(vn_done, c + 1)
                heads, src = octet((0, 1), P, cn)[0]
                fn(vnews[c][0:cn, heads], src, ACT.Copy).then_inc(vnew_act, 1)
                if c < 2:
                    cn1 = CHUNKS[c + 1][1]
                    act.wait_ge(wt_done, c + 1)
                    for heads, src in octet((4, 5), cn1, P):
                        ins = fn(cb[c + 1]["tt"][:, heads], src, ACT.Copy, scale=-1.0)
                    ins.then_inc(wt_ready, 1)
                act.wait_ge(ov_done, c + 1)
                for heads, src in octet((2, 3), cn, P):
                    ins = fn(on[:, heads, c0:c0 + cn], src, ACT.Copy)
                ins.then_inc(ov_taken, 1)
            act.wait_ge(ov_taken, 3)
            fn(sq[:], on[:], ACT.Square).then_inc(onorm_sq, 1)
            act.wait_ge(onorm_done, 1)
            fn(tok[:, 5], banks[4][0:HN, 0:N2], ACT.Sqrt, bias=eps6[0:HN, 0:1], scale=1 / P).then_inc(onorm_std, 1)
            split(on[:], N2, on_used, 8)
            lin("a_out", None)

            def ln(i):
                act.wait_ge(cent_ready, i - LN0 + 1)
                square(i, h[:], N2)
                root(i, N2, 1)

            ln(LN0)
            split(h[:], N2, normed, 4)
            ffn(1, N2, ACT.Silu, PV["conv2_w"] + 2 * KF, None)
            down("down1")
            ln(LN0 + 1)
            split(h[:], N2, normed, 5)
            u0 = UNIT0["b_cx"]

            with act.Fori(0, 4) as it:
                for s in range(SLOTS):
                    act.wait_ge(unit_used, it * 4 + (u0 + s + 1))
                    act.wait_ge(p_used, it * 2 + (s // 2 + 1))
                    fn((abuf if s % 2 == 0 else vbuf)[:, s // 2], banks[s][:, 0:N2], ACT.Copy).then_inc(banks_free, 1)
                    round_unit(it * 4 + (u0 + s + 4), s)
            lin("b_b", None)
            split(ucv[:], N2, banks_free, out_of("b_b"))
            lin("b_out", None)
            ln(LN0 + 2)
            split(h[:], N2, normed, 6)
            ffn(2, N2, ACT.Silu, PV["conv2_w"] + 5 * KF, None)
            down("down2", last=True)
            ln(LN0 + 3)

        @block.vector
        def _(dve):
            v = nc.vector
            dve_n = [0]

            def link(ins):
                dve_n[0] += 1
                ins.then_inc(dve_seq, 1)
                dve.wait_ge(dve_seq, dve_n[0])

            def lanes(ap, k):
                return ap.unsqueeze(1).broadcast_to([ap.shape[0], k, ap.shape[-1]])

            def col(name, i):
                return pv[:, PV[name] + i:PV[name] + i + 1]

            def remainder(i, src, n):
                dve.wait_ge(split_hi, i + 1)
                v.tensor_tensor(a_lo[:, :, 0:n], src, a_hi[:, :, 0:n].bitcast(F32), ALU.subtract) \
                    .then_inc(split_ready, 1)

            def affine(dst, gains, shifts, signal):
                for k in range(KD):
                    if shifts is None:
                        ins = v.tensor_scalar(dst[:, k], dst[:, k], gains(k), None, ALU.mult)
                    else:
                        ins = v.tensor_scalar(dst[:, k], dst[:, k], gains(k), shifts(k), ALU.mult, ALU.add)
                if signal:
                    ins.then_inc(normed, 1)
                return ins

            def scaled(i, dst, src, n):
                c0 = N1 if i == RMS_CTX else 0
                r = rstd[:, c0:c0 + n]
                dve.wait_ge(std_ready, i + 1)
                link(v.reciprocal(r, r))
                link(v.tensor_tensor(dst, src, lanes(r, KD), ALU.mult))

            dve.wait_ge(csil_ready, 2)
            v.memset(junk[:, 0:1], 0.0).then_inc(ada_seq, 1)
            with dve.Fori(0, 4) as it:
                for s in range(2):
                    dve.wait_ge(ada_in[s], it * 16 + 16)
                    for t in range(2):
                        for j, cs in enumerate((csil, csil2)):
                            dve.wait_ge(ada_seq, it * 8 + (4 * s + 2 * t + j + 1))
                            ins = v.scalar_tensor_tensor(junk[:], adaw[:, s, t], 1.0, cs[:], ALU.mult, ALU.mult,
                                                         accum_out=mod[:, j, ds(it * 4 + (2 * s + t), 1)])
                            ins.then_inc(ada_seq, 1)
            dve.wait_ge(ada_seq, 33)
            dve.sem_inc(ada_used, 8)
            dve.wait_ge(small_in, 96)
            for j in range(2):
                ins = v.tensor_tensor(mod[:, j, 0:16], mod[:, j, 0:16], pv[:, PV["b_ada"]:PV["b_ada"] + 16], ALU.add)
            link(ins)
            norm1 = pv[:, PV["norm1_g"]:PV["norm1_g"] + KD]
            for j in range(2):
                ins = v.scalar_tensor_tensor(gain[:, j], mod[:, j, 8:16], 1.0, norm1, ALU.add, ALU.mult)
            link(ins)
            scaled(RMS_CTX, hfull[:, :, N1:], ctxt[:], N1)
            affine(hfull[:, :, N1:], lambda k: gain[:, 1, k:k + 1], lambda k: mod[:, 1, k:k + 1], False)
            scaled(RMS_X, hfull[:, :, 0:N1], x[:], N1)
            affine(hfull[:, :, 0:N1], lambda k: gain[:, 0, k:k + 1], lambda k: mod[:, 0, k:k + 1], True)
            remainder(0, hfull[:], 2 * N1)

            v.memset(reset[:], 1.0).then_inc(ada_done, 1)
            dve.wait_ge(ada_done, 1)
            link(v.memset(reset[:].rearrange("p (c t) -> p c t", t=GC)[:, :, 0:1], 0.0))
            for i in range(2 * HG):
                d, hh = divmod(i, HG)
                dve.wait_ge(z_done, i + 1)
                v.tensor_scalar(la[:, d, hh], banks[4 + i % 4][:, :], col("gla_b2", i), None, ALU.add).then_inc(t_ready, 1)
            dve.wait_ge(log_ready, 1)
            link(v.scalar_tensor_tensor(la[:], la[:], 0.0, ebuf[:], ALU.min, ALU.subtract))
            for d in range(2):
                src = la[:, d].rearrange("p h t -> p (h t)")
                dst = ebuf[:, d].rearrange("p h t -> p (h t)")
                if d:
                    src, dst = src[:, ::-1], dst[:, ::-1]
                v.tensor_tensor_scan(dst, reset[:], src, 0.0, ALU.mult, ALU.add).then_inc(decay_ready, 1)

            with dve.Fori(4, 12) as it:
                for s in range(2):
                    dve.wait_ge(ada_in[s], it * 16 + 16)
                    for t in range(2):
                        ins = v.scalar_tensor_tensor(adaw[:, s, t], adaw[:, s, t], 1.0, csil[:], ALU.mult, ALU.mult,
                                                     accum_out=mod[:, 0, ds(it * 4 + (2 * s + t), 1)])
                    ins.then_inc(ada_used, 1)
            dve.wait_ge(ada_used, 24)
            link(v.tensor_tensor(mod[:, 0, 16:48], mod[:, 0, 16:48], pv[:, PV["b_ada"] + 16:PV["b_ada"] + 48], ALU.add))
            link(v.scalar_tensor_tensor(gain[:, 2], mod[:, 0, 32:40], 1.0, pv[:, PV["norm2_g"]:PV["norm2_g"] + KD],
                                        ALU.add, ALU.mult))

            dve.wait_ge(banks_free, out_of("w_vs"))
            for n in range(2):
                for c in range(2):
                    ins = v.bn_stats(stats[:, n, c], vs[:, n, c * 512:(c + 1) * 512])
                link(ins)
                v.bn_aggr(mv[:, n, 0:2], stats[:, n]).then_inc(vs_var, 1)
            dve.wait_ge(vs_std, 2)
            for n in range(2):
                ins = v.reciprocal(mv[:, n, 3:4], mv[:, n, 2:3])
            link(ins)
            dve.wait_ge(sgu_in, 64)
            for n in range(2):
                link(v.tensor_scalar(vs[:, n], vs[:, n], mv[:, n, 0:1], mv[:, n, 3:4], ALU.subtract, ALU.mult))
                link(v.tensor_tensor(vs[:, n], vs[:, n], rows[:, 0], ALU.mult))
                v.tensor_tensor(vs[:, n], vs[:, n], rows[:, 1], ALU.add).then_inc(vn_ready, 1)
            for n in range(2):
                for half in range(2):
                    dve.wait_ge(sgu_done, 2 * n + half + 1)
                    gs = slice(4 * half, 4 * half + 4)
                    buf = mixed[:]
                    if n or half:
                        dve.wait_ge(gated, 2 * (2 * n + half))
                    link(v.tensor_tensor(buf, quad(banks[4 + 2 * n + half], P),
                                         rows[:, 2].rearrange("p (g t) -> p g t", g=8)[:, gs], ALU.add))
                    v.tensor_tensor(gu[:, gs, n * P:(n + 1) * P], gu[:, gs, n * P:(n + 1) * P], buf, ALU.mult) \
                        .then_inc(gated, 2)
            remainder(1, gu[:], N1)

            def lin(name, take):
                u0 = UNIT0[name]
                with dve.Fori(0, TILES_OF[name] // 4) as it:
                    for s in range(SLOTS):
                        dve.wait_ge(unit_used, it * 4 + (u0 + s + 1))
                        take(it * 4 + s, s)

            def down(name, take):
                u0 = UNIT0[name]
                with dve.Fori(0, 2) as it:
                    for j in range(4):
                        dve.wait_ge(unit_used, it * 12 + (u0 + 3 * j + 3))
                        take(it * 4 + j, j)

            lin("w_br_a", lambda t, s: v.tensor_tensor(ga[:, ds(t, 1)], banks[s][:, 0:N1].unsqueeze(1), ga[:, ds(t, 1)],
                                                       ALU.mult).then_inc(banks_free, 1))

            dve.wait_ge(banks_free, out_of("w_br_a"))
            for d in range(2):
                v.memset(sc[d][:], 0.0)
            v.memset(kmul[:], 1.0)
            v.memset(qmul[:], 1.0).then_inc(ada_done, 1)

            def differences(d):
                flat = ebuf[:, d].rearrange("p h (c t) -> p (h c) t", t=GC)
                last = (flat[:, :, GC - 1:GC] if d == 0 else flat[:, :, 0:1]).broadcast_to([P, HG * 8, GC])
                if d:
                    dve.wait_ge(sc_done, 2)
                    dve.wait_ge(ks_ready, 1)
                v.tensor_tensor(kd[:].rearrange("p h (c t) -> p (h c) t", t=GC), last, flat, ALU.subtract) \
                    .then_inc(diff_ready, 1)

            def per_chunk(ap, n):
                return ap.rearrange("p h c -> p (h c)").unsqueeze(2).broadcast_to([P, HG * n, GC])

            def chunks_of(ap):
                return ap.rearrange("p h (c t) -> p (h c) t", t=GC)

            def operands(d):
                e = (1, 2, 3, 4) if d == 0 else (5, 6, 7, 8)
                dve.wait_ge(exps_ready, e[0])
                v.tensor_tensor(qd[d][:], q1[:], qd[d][:], ALU.mult).then_inc(qk_ready, 1)
                dve.wait_ge(exps_ready, e[1])
                v.tensor_tensor(ki[d][:], k1[:, :, 0:N1], ki[d][:], ALU.mult).then_inc(qk_ready, 1)
                dve.wait_ge(exps_ready, e[2])
                dve.wait_ge(ada_done, 2)
                early, late = slice(d, 4, 2), slice(1 - d, 4, 2)
                v.tensor_copy(qmul[:, d, :, late], dec[:, d, :, early])
                v.tensor_copy(kmul[:, d, :, early], dec[:, d, :, late])
                v.tensor_tensor(bdec[:, d], dec[:, d, :, early], dec[:, d, :, late], ALU.mult)
                c = (4, 5, 6, 7) if d == 0 else (7, 6, 5, 4)
                link(v.tensor_copy(kmul[:, d, :, c[2]], dec[:, d, :, c[3]]))
                for i in (1, 0):
                    link(v.tensor_tensor(kmul[:, d, :, c[i]], kmul[:, d, :, c[i + 1]], dec[:, d, :, c[i + 1]], ALU.mult))
                v.tensor_tensor(chunks_of(qs[d][:]), chunks_of(qd[d][:]), per_chunk(qmul[:, d], 4), ALU.mult)
                dve.wait_ge(exps_ready, e[3])
                v.tensor_tensor(kd[:], kd[:], k1[:], ALU.mult).then_inc(kd_ready, 1)
                dve.wait_ge(kd_ready, d + 1)
                if d:
                    dve.wait_ge(kt_done, 4)
                v.tensor_tensor(chunks_of(ks[:]), chunks_of(kd[:]), per_chunk(kmul[:, d], 8), ALU.mult) \
                    .then_inc(ks_ready, 1)

            def scores(d):
                for blk in range(2):
                    dve.wait_ge(sc_done, 2 * d + blk + 1)
                    for hh in range(HG):
                        ins = v.copy_predicated(sc[d][:, blk, hh], gla_masks[:, d], banks[6 + blk][:, hh * P:(hh + 1) * P])
                    ins.then_inc(sc_ready, 1)

            def second_state(d):
                dve.wait_ge(st0_ready, d + 1)
                dve.wait_ge(up_done, 2 * d + 2)
                for hh in range(HG):
                    ins = v.scalar_tensor_tensor(st1[d][:, hh], st0[d][:, hh], bdec[:, d, hh, d:d + 1],
                                                 banks[2 + hh // 2][:, (hh % 2) * DV:(hh % 2 + 1) * DV], ALU.mult, ALU.add)
                ins.then_inc(st1_ready, 1)

            differences(0)
            operands(0)
            scores(0)
            differences(1)
            second_state(0)
            operands(1)
            scores(1)
            second_state(1)
            of = o1[:].rearrange("p h v t -> p (h v) t")
            for i in range(4):
                blk, pair = divmod(i, 2)
                dve.wait_ge(o_done, i + 1)
                v.tensor_copy(of[:, 4 * pair:4 * pair + 4, blk * P:(blk + 1) * P],
                              banks[4 + i][:, :].rearrange("p (h t) -> p h t", t=P)).then_inc(o_taken, 1)
            for b in range(2):
                hs = slice(2 * b, 2 * b + 2)
                dve.wait_ge(ostd_ready, b + 1)
                link(v.reciprocal(orstd[:, hs], orstd[:, hs]))
                for half in range(2):
                    ins = v.tensor_tensor(o1[:, hs, half], o1[:, hs, half], orstd[:, hs], ALU.mult)
                link(ins)
                for k in range(4 * b, 4 * b + 4):
                    v.scalar_tensor_tensor(of[:, k], of[:, k], col("gla_norm_g", k), sr[:, k], ALU.mult, ALU.mult) \
                        .then_inc(ob_ready, 1)
            dve.wait_ge(ob_ready, 8)
            remainder(2, of, N1)

            def merge(t, s):
                v.tensor_tensor(gb[:, ds(t, 1)], banks[s][:, 0:N1].unsqueeze(1), gb[:, ds(t, 1)], ALU.mult) \
                    .then_inc(banks_free, 1)
                dve.wait_ge(banks_free, t + (TILE0["w_br_b"] + 5))
                v.tensor_tensor(gb[:, ds(t, 1)], gb[:, ds(t, 1)], ga[:, ds(t, 1)], ALU.add).then_inc(merged, 1)

            lin("w_br_b", merge)
            remainder(3, gb[:], N1)

            def residual(j):
                def take(t, s):
                    v.scalar_tensor_tensor(x[:, ds(t, 1)], banks[s][:, 0:N1].unsqueeze(1), mod[:, 0, ds(t + j * KD, 1)],
                                           x[:, ds(t, 1)], ALU.mult, ALU.add).then_inc(banks_free, 1)
                return take

            lin("w_o", residual(2))
            scaled(RMS_F, sq[:, :, 0:N1], x[:], N1)
            affine(sq[:, :, 0:N1], lambda k: gain[:, 2, k:k + 1], lambda k: mod[:, 0, 24 + k:25 + k], True)
            remainder(4, sq[:, :, 0:N1], N1)

            def ffn(i, n, taps):
                t0, j0, nt = TILE0[f"up{i}"], KF * i, len(taps)
                c0 = conv_links[0]
                conv_links[0] += KF * (nt - 1)
                with dve.Fori(0, KF // 2) as it:
                    for m, (w, to, frm) in enumerate(taps):
                        for p in range(2):
                            if m == 0:
                                dve.wait_ge(banks_free, it * 4 + (t0 + 2 * p + 5))
                            else:
                                dve.wait_ge(conv_seq, it * (2 * (nt - 1)) + (c0 + 2 * (m - 1) + p + 1))
                            dst = to(cbuf[:, p, 0:n])
                            v.scalar_tensor_tensor(dst, frm(abuf[:, p, 0:n]), pv[:, ds(it * 2 + (w + p), 1)], dst,
                                                   ALU.mult, ALU.add) \
                                .then_inc(conv_done if m == nt - 1 else conv_seq, 1)
                    for p in range(2):
                        dve.wait_ge(act_done, it * 2 + (j0 + p + 1))
                        v.tensor_tensor(gfull[:, p, 0:n], gbuf[:, p, 0:n], vbuf[:, p, 0:n], ALU.mult).then_inc(glu_done, 1)
                    for p in range(2):
                        dve.wait_ge(glu_done, it * 2 + (j0 + p + 1))
                        v.tensor_copy(g_hi[:, ds(it * 2 + p, 1), 0:n], gfull[:, p:p + 1, 0:n]).then_inc(g_rounded, 1)
                    for p in range(2):
                        dve.wait_ge(g_rounded, it * 2 + (j0 + p + 1))
                        jj = ds(it * 2 + p, 1)
                        v.tensor_tensor(g_lo[:, jj, 0:n], gfull[:, p:p + 1, 0:n], g_hi[:, jj, 0:n].bitcast(F32),
                                        ALU.subtract).then_inc(g_ready, 1)

            conv_links = [0]

            def image_tap(dy, dx):
                rows_, w = N1 // GRID, GRID
                y0, y1 = max(0, 1 - dy), rows_ - max(0, dy - 1)
                x0, x1 = max(0, 1 - dx), w - max(0, dx - 1)

                def view(ap, sy, sx):
                    return ap.rearrange("p (y x) -> p y x", x=w)[:, y0 + sy:y1 + sy, x0 + sx:x1 + sx]

                return (PV["conv1_w"] + (3 * dy + dx) * KF, lambda ap: view(ap, 0, 0),
                        lambda ap: view(ap, dy - 1, dx - 1))

            ffn(0, N1, [image_tap(dy, dx) for dy in range(3) for dx in range(3) if (dy, dx) != (1, 1)])
            down("down0", residual(5))
            scaled(RMS_END, h[:, :, META:], x[:], N1)
            affine(h[:, :, META:], lambda k: col("final_g", k), None, True)
            dve.wait_ge(h_in, 16)
            remainder(5, h[:], N2)

            def causal(w, shift, n=N2):
                return (w, lambda ap: ap[:, shift:n], lambda ap: ap[:, 0:n - shift])

            link(v.memset(tokm[:], 1.0))
            for c0, _ in CHUNKS:
                ins = v.memset(tokm[:, c0:c0 + 1], 0.0)
            link(ins)
            dve.wait_ge(tok_act, 4)
            link(v.scalar_tensor_tensor(tok[:, 5], tok[:, 1], 0.0, tok[:, 5], ALU.max, ALU.add))
            link(v.tensor_scalar(tok[:, 5], tok[:, 5], hb[:, 2:3], -1.0, ALU.mult, ALU.mult))
            link(v.tensor_tensor_scan(tok[:, 1], tokm[:], tok[:, 5], 0.0, ALU.mult, ALU.add))
            for ci, (c0, cn) in enumerate(CHUNKS):
                ins = v.tensor_copy(glast[:, ci:ci + 1], tok[:, 1, c0 + cn - 1:c0 + cn])
            link(ins)
            for ci, (c0, cn) in enumerate(CHUNKS):
                ins = v.tensor_scalar(tok[:, 3, c0:c0 + cn], tok[:, 1, c0:c0 + cn], glast[:, ci:ci + 1], -1.0,
                                      ALU.subtract, ALU.mult)
            ins.then_inc(gcum_ready, 1)
            dve.wait_ge(tok_act, 7)
            link(v.tensor_tensor(tok[:, 4], tok[:, 0], tok[:, 2], ALU.mult))
            t0 = TILE0["a_in"]
            with dve.Fori(0, 6) as it:
                for m in range(3):
                    for s in range(SLOTS):
                        if m == 0:
                            dve.wait_ge(banks_free, it * 4 + (t0 + s + 5))
                        else:
                            dve.wait_ge(conv4_seq, it * 8 + (4 * (m - 1) + s + 1))
                        dst = convc[:, s, 3 - m:N2]
                        v.scalar_tensor_tensor(dst, conva[:, s, 0:N2 - 3 + m],
                                               pv[:, ds(it * 4 + (PV["a_conv"] + 24 * m + s), 1)], dst, ALU.mult, ALU.add) \
                            .then_inc(conv4_done if m == 2 else conv4_seq, 1)
            dve.wait_ge(qstd_ready, 2)
            link(v.reciprocal(tok[:, 6:8], tok[:, 6:8]))
            link(v.tensor_scalar(tok[:, 6], tok[:, 6], 128 ** -0.5, None, ALU.mult))
            for dst, a_, b_ in ((8, 7, 0), (9, 6, 2), (4, 4, 7), (3, 3, 7)):
                ins = v.tensor_tensor(tok[:, dst], tok[:, a_], tok[:, b_], ALU.mult)
            ins.then_inc(tok_ready, 1)
            for i in range(3 * HN):
                j, hh = divmod(i, HN)
                dve.wait_ge(bc_done, i + 1)
                dst, src = ((qg[:, hh], qkv[:, hh]), (kb[:, hh], qkv[:, 8 + hh]), (qkv[:, hh], qkv[:, hh]))[j]
                v.tensor_tensor(dst, src, banks[i % 4][:, 0:N2], ALU.mult).then_inc(bc_used, 1)
            dve.wait_ge(toks_ready, 2)
            n = 0
            for c, (_, cn) in enumerate(CHUNKS):
                B = cb[c]

                def per_token(j, heads, n_):
                    return toks[0:cn, c, j, heads].unsqueeze(2).broadcast_to([cn, heads.stop - heads.start, n_])

                def pair(n_, width):
                    return octet((2 * (n_ % 4), 2 * (n_ % 4) + 1), width, cn)

                dd = B["dd"][0:cn]
                dve.wait_ge(pre_done, n + 1)
                for heads, src in pair(n, cn):
                    ins = v.tensor_tensor(dd[:, heads], src, per_token(1, heads, cn), ALU.subtract)
                ins.then_inc(pre_used, 1)
                dve.wait_ge(pre_used, n + 1)
                v.tensor_tensor(dd, dd, levels[0:cn, LOG2P, 0:cn].unsqueeze(1).broadcast_to([cn, HN, cn]), ALU.add) \
                    .then_inc(dcy_used, 1)
                dve.wait_ge(pre_done, n + 2)
                for heads, src in pair(n + 1, P):
                    if c < 2:
                        v.tensor_tensor(B["kdc"][0:cn, heads], src, per_token(3, heads, P), ALU.mult)
                    ins = v.tensor_tensor(B["kbeg"][0:cn, heads], src, per_token(2, heads, P), ALU.mult)
                ins.then_inc(pre_used, 1)
                dve.wait_ge(pre_done, n + 3)
                for heads, src in pair(n + 2, P):
                    ins = v.tensor_tensor(B["vb"][0:cn, heads], src, per_token(0, heads, P), ALU.mult)
                ins.then_inc(pre_used, 1)
                dve.wait_ge(dcy_exp, c + 1)
                link(v.tensor_tensor(dd, dd, per_token(4, slice(0, HN), cn), ALU.mult))
                dve.wait_ge(pre_done, n + 4)
                for heads, src in pair(n + 3, cn):
                    ins = v.tensor_tensor(B["mt"][0:cn, heads], src, dd[:, heads], ALU.mult)
                ins.then_inc(mt_ready, 1)
                dve.wait_ge(mt_ready, c + 1)
                dve.sem_inc(pre_used, 1)
                dve.wait_ge(pre_done, n + 5)
                for heads, src in pair(n + 4, cn):
                    ins = v.tensor_tensor(B["qkd"][0:cn, heads], src, dd[:, heads], ALU.mult)
                ins.then_inc(pre_used, 1)
                n += 5
            dve.wait_ge(banks_free, out_of("a_in"))
            v.tensor_scalar(sz[:], sz[:], col("a_norm", 0), None, ALU.mult).then_inc(sz_ready, 1)

            def flipped(c, dst, n_):
                if c == 2:
                    return
                cn = CHUNKS[c][1]
                dve.wait_ge(ut_done, n_ + 1)
                heads, src = octet(INV[c][1], cn, cn)[1]
                v.tensor_copy(cb[c][dst][0:cn, heads], src).then_inc(u_ready_dve, 1)

            for c in range(3):
                flipped(c, "tt", c)
            for lv in range(1, LOG2P):
                now = [c for c in range(3) if (lv, c) in STEP]
                for c in now:
                    cn = CHUNKS[c][1]
                    dve.wait_ge(ty_done, STEP[lv, c] + 1)
                    _, src = octet((INV[c][0],), cn // 2, cn)[0]
                    tt = firsts(cb[c]["tt"][0:cn], lv)
                    v.tensor_tensor(tt, tt, src.rearrange("p h (n b) -> p h n b", b=2 ** lv), ALU.subtract) \
                        .then_inc(ty_used, 1)
                for c in now:
                    flipped(c, "uu", 3 + STEP[lv, c])
            for c, (_, cn) in enumerate(CHUNKS):
                dve.wait_ge(vn_done, c + 1)
                heads, src = octet((0, 1), P, cn)[1]
                v.tensor_copy(vnews[c][0:cn, heads], src).then_inc(vnew_dve, 1)
                if c == 2:
                    break
                dve.wait_ge(ov_done, c + 1)
                if c == 0:
                    for heads, src in octet((6, 7), P, P):
                        ins = v.tensor_copy(s2[:, heads], src)
                else:
                    decay = glb[:, :, c:c + 1].broadcast_to([P, HN, P])
                    link(v.tensor_tensor(s2[:], s2[:], decay, ALU.mult))
                    for heads, src in octet((6, 7), P, P):
                        ins = v.tensor_tensor(s2[:, heads], s2[:, heads], src, ALU.add)
                ins.then_inc(s2_ready, 1)
            dve.wait_ge(onorm_sq, 1)
            dve.wait_ge(sz_ready, 1)
            link(v.tensor_tensor(on[:], on[:], sz[:], ALU.mult))
            dve.wait_ge(onorm_std, 1)
            v.reciprocal(tok[:, 5], tok[:, 5]).then_inc(onorm_r, 1)
            for hh in range(HN):
                dve.wait_ge(ob2_done, hh + 1)
                v.tensor_tensor(on[:, hh], on[:, hh], banks[hh % 4][:, 0:N2], ALU.mult).then_inc(on_used, 1)
            dve.wait_ge(on_used, 8)
            remainder(6, on[:], N2)

            def add_to_h(t, s):
                v.scalar_tensor_tensor(h[:, ds(t, 1)], h[:, ds(t, 1)], ALPHA, banks[s][:, 0:N2].unsqueeze(1), ALU.mult,
                                       ALU.add).then_inc(banks_free, 1)

            def ln(i, gains, shifts, first):
                dve.wait_ge(mean_ready, i - LN0 + 1)
                v.tensor_tensor(h[:], h[:], lanes(banks[4][:, 0:N2], KD), ALU.subtract).then_inc(cent_ready, 1)
                dve.wait_ge(cent_ready, i - LN0 + 1)
                scaled(i, h[:], h[:], N2)
                affine(h[:], lambda k: col(gains, first + k), lambda k: col(shifts, first + k), True)

            lin("a_out", add_to_h)
            ln(LN0, "ln_mix_g", "ln_mix_b", 0)
            remainder(7, h[:], N2)
            conv2 = PV["conv2_w"]
            ffn(1, N2, [causal(conv2 + KF, 1), causal(conv2, 2)])
            down("down1", add_to_h)
            ln(LN0 + 1, "ln_ffn_g", "ln_ffn_b", 0)
            remainder(8, h[:], N2)
            t0 = TILE0["b_cx"]
            with dve.Fori(0, 4) as it:
                for p in range(2):
                    dve.wait_ge(banks_free, it * 4 + (t0 + 2 * p + 6))
                    dve.wait_ge(u_seq, it * 6 + (p + 1))
                    v.tensor_tensor(pbuf[:, p], abuf[:, p], vbuf[:, p], ALU.mult).then_inc(p_used, 1)
                for m, shift in enumerate((0, 1, 2)):
                    for p in range(2):
                        w = pv[:, ds(it * 2 + (PV["b_conv"] + 8 * (2 - shift) + p), 1)]
                        dst = ucv[:, ds(it * 2 + p, 1), shift:N2]
                        src = pbuf[:, p:p + 1, 0:N2 - shift]
                        if m == 0:
                            dve.wait_ge(p_used, it * 2 + (p + 3))
                            ins = v.tensor_scalar(dst, src, w, None, ALU.mult)
                        else:
                            dve.wait_ge(u_seq, it * 6 + (2 * (m - 1) + p + 3))
                            ins = v.scalar_tensor_tensor(dst, src, w, dst, ALU.mult, ALU.add)
                        ins.then_inc(u_seq, 1)
            dve.wait_ge(u_seq, 26)
            lin("b_b", lambda t, s: v.tensor_tensor(ucv[:, ds(t, 1)], banks[s][:, 0:N2].unsqueeze(1), ucv[:, ds(t, 1)],
                                                    ALU.mult).then_inc(banks_free, 1))
            remainder(9, ucv[:], N2)
            lin("b_out", add_to_h)
            ln(LN0 + 2, "ln_mix_g", "ln_mix_b", 8)
            remainder(10, h[:], N2)
            conv2 = PV["conv2_w"] + 3 * KF
            ffn(2, N2, [causal(conv2 + KF, 1), causal(conv2, 2)])
            down("down2", add_to_h)
            ln(LN0 + 3, "ln_ffn_g", "ln_ffn_b", 8)

    return nc


def _units(w, cols):
    k, m = w.shape
    t = w.reshape(k // P, P, m // P, P).transpose(2, 1, 0, 3)
    return t[list(cols)]


def _features(v):
    return v.reshape(-1, P).T


def _tokens(t):
    return t.T.reshape(KD, P, -1).transpose(1, 0, 2)


def _layout(i):
    f = np.asarray
    w_in = f(i["w_in"])[0]
    w_main = w_in[:, :7168]
    edge = {"w_u": 0, "w_vs": 8, "w_q": 16, "w_r": 20, "w_ga": 28, "w_gb": 36, "w_k": 44, "w_v": 48}
    tiles = {"w_u": 8, "w_vs": 8, "w_q": 4, "w_r": 8, "w_ga": 8, "w_gb": 8, "w_k": 4, "w_v": 8}
    parts = {n: _units(w_main, range(edge[n], edge[n] + tiles[n])) for n in edge}
    for n in ("w_br_a", "w_br_b", "w_o"):
        parts[n] = _units(f(i[n])[0], range(8))
    pair = [t for j in range(KF) for t in (j, KF + j)]
    parts["up0"] = _units(f(i["ffn_w_up"])[0], pair)
    a_in = f(i["a_w_in_2"])[0]
    parts["a_in"] = _units(a_in[:, :4096], range(32))
    parts["a_out"] = _units(f(i["a_w_out_2"])[0], range(8))
    b_in = f(i["b_w_in_2"])[0]
    parts["b_cx"] = _units(b_in, [t for j in range(8) for t in (8 + j, 16 + j)])
    parts["b_b"] = _units(b_in, range(8))
    parts["b_out"] = _units(f(i["b_w_out_2"])[0], range(8))
    for j in range(2):
        parts[f"up{j + 1}"] = _units(f(i["ffn_w_up_2"])[j], pair)
    d = {name: np.concatenate([parts[n] for n in names]) for name, names in STREAMS if names}
    d["down0"] = _units(f(i["ffn_w_down"])[0], range(8))
    for j in range(2):
        d[f"down{j + 1}"] = _units(f(i["ffn_w_down_2"])[j], range(8))
    d["x"], d["ctx"], d["meta"] = _tokens(f(i["x"])[0]), _tokens(f(i["ctx"])[0]), _tokens(f(i["meta_2"]))
    d["c"], d["c_ctx"] = f(i["c"]).reshape(D), f(i["c_ctx"]).reshape(D)
    d["w_ada"] = f(i["w_ada"])[0].T.reshape(24, 2, P, D).transpose(0, 2, 1, 3)
    d["w_lr"] = w_in[:, 7168:].reshape(KD, P, 2 * RANK).transpose(1, 0, 2)
    d["gla_w2"] = f(i["gla_w2"])[0]
    d["sgu_w"] = f(i["sgu_w"])[0].transpose(2, 0, 1)
    d["sgu_ln_g"], d["sgu_ln_b"] = f(i["sgu_ln_g"]).reshape(D), f(i["sgu_ln_b"]).reshape(D)
    d["sgu_b"] = f(i["sgu_b"]).reshape(D)
    d["w_ba"] = a_in[:, 4096:].reshape(KD, P, 2 * HN).transpose(1, 0, 2)
    d["a_log"], d["dt_bias"] = f(i["a_log_2"]).reshape(HN, 1), f(i["a_dt_bias_2"]).reshape(HN, 1)
    vectors = {"b_ada": i["b_ada"], "norm1_g": i["norm1_g"], "norm2_g": i["norm2_g"], "gla_b2": i["gla_b2"],
               "gla_norm_g": i["gla_norm_g"], "conv1_w": i["ffn_conv_w"], "conv1_b": i["ffn_conv_b"],
               "final_g": i["final_norm_g"], "a_conv": i["a_conv_2"], "a_norm": i["a_norm_2"], "b_conv": i["b_conv_2"],
               "ln_mix_g": i["ln_mix_g_2"], "ln_mix_b": i["ln_mix_b_2"], "conv2_w": i["ffn_conv_2"],
               "ln_ffn_g": i["ln_ffn_g_2"], "ln_ffn_b": i["ln_ffn_b_2"]}
    d["pv"] = np.concatenate([_features(f(vectors[n])) for n, _ in PV_PARTS], axis=1)
    t = np.arange(P)
    d["ident"] = np.eye(P, dtype=np.float32)
    d["averages"] = np.stack([np.full((P, P), 1 / n, np.float32) for n in (D, DV, P, 1)], axis=1)
    masks = []
    for lv in range(LOG2P):
        b = 2 ** lv
        same = (t[:, None] // (2 * b)) == (t[None, :] // (2 * b))
        masks.append(same & ((t[:, None] // b) % 2 == 0) & ((t[None, :] // b) % 2 == 1))
    masks.append(np.where(t[:, None] <= t[None, :], 0.0, -1e30))
    d["levels"] = np.stack(masks, axis=1).astype(np.float32)
    d["gla_masks"] = np.stack([t[:, None] <= t[None, :], t[:, None] >= t[None, :]], axis=1).astype(np.int32)
    d["pick"] = np.repeat(np.eye(HN, dtype=np.float32)[None], P, axis=0)
    d["sel"] = np.repeat(np.eye(HN, dtype=np.float32)[:, :, None], P, axis=2)
    return {n: np.ascontiguousarray(a) for n, a in d.items()}


def kernel(**inputs):
    import concourse.bacc as bacc
    from concourse.bass_utils import run_bass_kernel_spmd

    nc = bacc.Bacc("TRN2", target_bir_lowering=False, num_devices=1)
    arrays = {f"in_{n}": a for n, a in _layout(inputs).items()}
    args = {n[3:]: nc.dram_tensor(n, a.shape, mybir.dt.from_np(a.dtype), kind="ExternalInput").ap()
            for n, a in arrays.items()}
    out = nc.dram_tensor("out_h", (P, KD, N1), F32, kind="ExternalOutput").ap()
    bass_two_blocks(nc, args, out)
    r = run_bass_kernel_spmd(nc, [arrays], core_ids=[0])
    h = np.asarray(r.results[0]["out_h"])
    return np.ascontiguousarray(h.transpose(2, 1, 0).reshape(1, N1, D))
```

```python
from contextlib import ExitStack

import numpy as np

import concourse.bass as bass
from concourse import mybir

F32 = mybir.dt.float32
F32R = mybir.dt.float32r
I32 = mybir.dt.int32
ALU = mybir.AluOpType
ACT = mybir.ActivationFunctionType
ds = bass.ds

P = 128
D = 1024
KD = D // P
N1 = 256
META = 16
N2 = META + N1
FF = 2816
KF = FF // P
HG, DK, DV = 4, 128, 256
RANK = 16
GC = 64
GRID = 64
HN = 8
ALPHA = 4.0 ** 0.25
SLOTS = 4
UB = 8
CHUNKS = [(0, 128), (128, 128), (256, 16)]

PV_PARTS = [("b_ada", 48), ("norm1_g", 8), ("norm2_g", 8), ("gla_b2", 8), ("gla_norm_g", 8),
            ("conv1_w", 9 * KF), ("conv1_b", KF), ("final_g", 8), ("a_conv", 4 * 24), ("a_norm", 1),
            ("b_conv", 3 * 8), ("ln_mix_g", 16), ("ln_mix_b", 16), ("conv2_w", 2 * 3 * KF),
            ("ln_ffn_g", 16), ("ln_ffn_b", 16)]
PV = {}
PV_N = 0
for _name, _n in PV_PARTS:
    PV[_name] = PV_N
    PV_N += _n

LINEARS = [("w_k", 4, 4), ("w_q", 4, 4), ("w_v", 8, 8), ("w_vs", 8, 8), ("w_u", 8, 8), ("w_r", 8, 8),
           ("w_ga", 8, 8), ("w_gb", 8, 8), ("w_br_a", 8, 8), ("w_br_b", 8, 8), ("w_o", 8, 8),
           ("up0", 44, 44), ("down0", 8, 24), ("a_in", 32, 32), ("a_out", 8, 8), ("up1", 44, 44),
           ("down1", 8, 24), ("b_cx", 16, 16), ("b_b", 8, 8), ("b_out", 8, 8), ("up2", 44, 44),
           ("down2", 8, 24)]
UNIT0, TILE0 = {}, {}
_u = _t = 0
for _name, _tiles, _units in LINEARS:
    UNIT0[_name], TILE0[_name] = _u, _t
    _u += _units
    _t += _tiles
UNITS = _u
TILES_OF = {n: t for n, t, _ in LINEARS}
STREAMS = [("s0", ["w_k", "w_q", "w_v", "w_vs", "w_u", "w_r", "w_ga", "w_gb", "w_br_a"]),
           ("s1", ["w_br_b", "w_o", "up0"]), ("down0", None), ("s2", ["a_in", "a_out", "up1"]),
           ("down1", None), ("s3", ["b_cx", "b_b", "b_out", "up2"]), ("down2", None)]
DOWN_SPLIT = [(0, 8), (8, 8), (16, 6)]
LOG2P = 7


def bass_two_blocks(nc, a, out):
    ctx = ExitStack()
    with ctx:
        base = nc.sbuf_base + (-nc.sbuf_base) % 64
        where = [base]

        def at(name, shape, offset, dt=F32):
            return nc.alloc_sbuf_tensor_at(name, shape, dt, offset=offset)

        def sb(name, shape, dt=F32):
            n = 4 * int(np.prod(shape[1:]))
            t = at(name, shape, where[0], dt)
            where[0] += n + (-n) % 32
            return t

        def sem(name):
            return ctx.enter_context(nc.semaphore(name))

        w_raw = sb("w_raw", [P, SLOTS, UB, P])
        w_hi = sb("w_hi", [P, SLOTS, UB, P], F32R)
        w_lo = sb("w_lo", [P, SLOTS, UB, P], F32R)
        area_a = where[0]
        a_hi = sb("a_hi", [P, KD, 2 * N1], F32R)
        a_lo = sb("a_lo", [P, KD, 2 * N1], F32R)
        ident = sb("ident", [P, P])
        averages = sb("averages", [P, 4, P])
        over_d, over_dv, over_dh, ones = (averages[:, i] for i in range(4))
        levels = sb("levels", [P, LOG2P + 1, P])
        gla_masks = sb("gla_masks", [P, 2, P], I32)
        pv = sb("pv", [P, PV_N])
        mod = sb("mod", [P, 2, 48])
        dec = sb("dec", [P, 2, HG, 8])
        kmul = sb("kmul", [P, 2, HG, 8])
        qmul = sb("qmul", [P, 2, HG, 4])
        bdec = sb("bdec", [P, 2, HG, 2])
        gain = sb("gain", [P, 3, KD])
        eps6 = sb("eps6", [P, 2])
        part_sum = sb("part_sum", [P, N2])
        area_c = where[0]
        csil = sb("csil", [P, D])
        c2 = sb("c2", [P, KD, 2])
        stats = sb("stats", [P, 2, 2, 6])
        mv = sb("mv", [P, 2, 4])
        area_x = where[0]
        x = sb("x", [P, KD, N1])
        area_r = where[0]
        rstd = sb("rstd", [P, 2 * N1])
        area_h = where[0]
        h = sb("h", [P, KD, N2])
        area_s = where[0]
        sq = sb("sq", [P, KD, N2])
        arena = where[0]
        assert arena + 86016 <= nc.sbuf_usable_end, (arena, nc.sbuf_usable_end)

        q1 = at("q1", [P, HG, N1], arena)
        k1 = at("k1", [P, HG, 2 * N1], arena + 4096)
        vx = at("vx", [P, 2, D], arena + 12288)
        vc = at("vc", [P, 2, D], arena + 20480)
        ctxt = at("ctxt", [P, KD, N1], arena + 20480)
        sr = at("sr", [P, KD, N1], arena + 28672)
        ga = at("ga", [P, KD, N1], arena + 36864)
        gb = at("gb", [P, KD, N1], arena + 45056)
        hfull = at("hfull", [P, KD, 2 * N1], arena + 53248)
        ebuf = at("ebuf", [P, 2, HG, 2 * N1], arena + 53248)
        la = at("la", [P, 2, HG, 2 * N1], arena + 69632)
        adab = [at(f"adab{i}", [P, KD, 4 * P], arena + o_) for i, o_ in enumerate((69632, 36864))]
        modrow = at("modrow", [2, 2, 4 * P], arena + 4096)
        adaw = [[at(f"adaw{i}{j}", [P, 2, D], o_) for j, o_ in enumerate(pair)] for i, pair in enumerate(
            ((area_h, area_s), (arena + 36864, arena + 45056), (arena + 69632, arena + 77824)))]
        sqx = at("sqx", [P, KD, N2], area_h)
        xr = at("xr", [P, KD, N1], arena + 12288)
        rows = at("rows", [P, 3, D], arena + 69632)
        mixed = at("mixed", [P, 4, P], area_r)
        sguw = at("sguw", [P, 8, P], arena + 69632 + 12288)
        wlr = at("wlr", [P, KD, 96], arena + 28672)
        wlr_hi = at("wlr_hi", [P, KD, 96], arena + 28672 + 3072, F32R)
        wlr_lo = at("wlr_lo", [P, KD, 96], arena, F32R)
        lrs = at("lrs", [96, 2 * N1], arena + 28672 + 6144, F32R)
        w2 = at("w2", [96, 2, HG * DK], arena + 12288)
        w2s = at("w2s", [96, 2, HG * DK], arena + 12288 + 4096, F32R)
        reset = at("reset", [P, HG * 2 * N1], arena + 45056)
        gu = at("gu", [P, KD, N1], area_s)
        vs = at("vs", [P, 2, D], area_h)
        kd = at("kd", [P, HG, 2 * N1], arena + 69632)
        ks = at("ks", [P, HG, 2 * N1], arena + 77824)
        spare_hi = at("spare_hi", [P, KD, 2 * N1], area_a)[:, :, N1:]
        spare_lo = at("spare_lo", [P, KD, 2 * N1], area_a + 16384)[:, :, N1:]
        qd = [at("qd0", [P, HG, N1], arena + 36864), at("qd1", [P, HG, N1], arena + 28672)]
        qs = [at("qs0", [P, HG, N1], arena + 40960), spare_lo[:, 0:HG]]
        ki = [at("ki0", [P, HG, N1], arena + 45056), at("ki1", [P, HG, N1], arena + 32768)]
        sc_full = [at("sc0", [P, 4, N1], arena + 49152), spare_lo[:, HG:]]
        st0, st1 = [], []
        for d in range(2):
            st0.append(at(f"st0{d}", [P, HG, DV], arena + 53248 + 8192 * d))
            st1.append(at(f"st1{d}", [P, HG, DV], arena + 53248 + 8192 * d + 4096))
        o1 = at("o1", [P, HG, 2, N1], arena)
        osq = at("osq", [P, HG, 2, N1], arena + 53248)
        orstd = at("orstd", [P, HG, N1], arena + 61440)

        def sc(d, blk, hh):
            return sc_full[d][:, 2 * blk + hh // 2, (hh % 2) * P:(hh % 2 + 1) * P]

        def kt(blk, hh):
            return spare_hi[:, 2 * blk + hh // 2, (hh % 2) * DK:(hh % 2 + 1) * DK]

        g_hi = at("g_hi", [P, KF, N2], arena, F32R)
        g_lo = at("g_lo", [P, KF, N2], arena + 23936, F32R)
        off = arena + 47872
        abuf = at("abuf", [P, 2, N2], off)
        cbuf = at("cbuf", [P, 2, N2], off + 2176)
        vbuf = at("vbuf", [P, 2, N2], off + 4352)
        gbuf = at("gbuf", [P, 2, N2], off + 6528)
        gfull = at("gfull", [P, 2, N2], off + 8704)
        ucv = at("ucv", [P, KD, N2], arena)
        pbuf = at("pbuf", [P, 2, N2], off + 8704)
        u_hi = at("u_hi", [P, KD, N2], arena + 8704, F32R)
        u_lo = at("u_lo", [P, KD, N2], arena + 17408, F32R)

        qkv = at("qkv", [P, 24, N2], arena)
        ksq = at("ksq", [P, HN, N2], arena + 26112)
        qg = at("qg", [P, HN, N2], arena + 34816)
        sz = at("sz", [P, HN, N2], arena + 43520)
        osq2 = at("osq2", [P, HN, N2], arena)
        convc = at("convc", [P, 4, N2], arena + 43520)
        on = at("on", [P, HN, N2], arena + 52224)
        conva = at("conva", [P, 4, N2], arena + 52224)
        s2 = at("s2", [P, HN, P], arena + 60928)
        sel = at("sel", [HN, HN, P], arena + 65024)
        tok = at("tok", [HN, 10, N2], arena + 69120)
        tokm = at("tokm", [HN, N2], arena + 80000)
        toks = at("toks", [P, 3, 5, HN], arena + 81088)
        glast = at("glast", [HN, 4], arena + 81568)
        glsp = at("glsp", [HN, HN, 4], arena + 82496)
        tok5sp = at("tok5sp", [HN, HN, N2 - N1], arena + 82624)
        glb = at("glb", [P, HN, 3], arena + 81600)
        hb = at("hb", [HN, 4], arena + 81696)
        wba = at("wba", [P, KD, 2 * HN], arena + 81728)
        pick = at("pick", [P, HN, HN], arena + 82240)
        cb = []
        for c, (_, cn) in enumerate(CHUNKS):
            B = {}
            if c < 2:
                places = [(area_s, area_s + 4096, area_a + 8192, arena + 30208),
                          [area_a + 16384 + 4096 * i for i in range(4)]][c]
                for n, o_ in zip(("kbeg", "kdc", "vb", "mt"), places):
                    B[n] = at(f"{n}{c}", [P, HN, P], o_)
                B["uu"] = at(f"uu_{c}", [P, HN, P], (arena + 26112, area_a + 12288)[c])
                B["qkd"] = at(f"qkd{c}", [P, HN, P], area_x + 4096 * c)
                for i, n in enumerate(("tt", "ml0", "ml1")):
                    B[n] = at(f"{n}_{c}", [P, HN, P], arena + 12288 * c + 4096 * i)
                B["dd"] = at(f"dd{c}", [P, HN, P], arena + 52224 + 4096 * c)
                B["yy"] = at(f"yy{c}", [P, HN, P // 2], arena + 52224 + 2048 * c)
            else:
                B["kbeg"] = at("kbeg2", [P, HN, P], area_a)
                B["vb"] = at("vb2", [P, HN, P], area_a + 4096)
                for i, n in enumerate(("mt", "qkd", "tt", "uu", "ml0", "ml1", "dd")):
                    B[n] = at(f"{n}_2", [P, HN, cn], area_c + 512 * i)
                B["yy"] = at("yy2", [P, HN, cn // 2], area_c + 3584)
            cb.append(B)
        vnew2 = at("vnew2", [P, HN, P], area_x)

        banks = [ctx.enter_context(nc.psum_tensor(f"bank{i}", [P, 512], F32)) for i in range(8)]

        def sems(names):
            return [sem(n) for n in names.split()]

        landed = [sem(f"landed{i}") for i in range(SLOTS)]
        hi_ready, lo_ready, unit_used, banks_free = sems("hi_ready lo_ready unit_used banks_free")
        first_in, small_in, w2_in, c_in, ctx_in, x_in, wlr_in = sems("first_in small_in w2_in c_in ctx_in x_in wlr_in")
        sgu_in, h_in, gdn_in, fills = sems("sgu_in h_in gdn_in fills")
        ada_in = sems("ada_in0 ada_in1")
        row_in = sems("row_in0 row_in1 row_in2 row_in3 row_in4 row_in5")
        modrow_ready, mod_flipped = sems("modrow_ready mod_flipped")
        ada_done, mod_taken, gain_ready, row_used, csil_ready, masks_ready = sems(
            "ada_done mod_taken gain_ready row_used csil_ready masks_ready")
        full_ready, xr_ready = sems("full_ready xr_ready")
        act_seq, dve_seq = sems("act_seq dve_seq")
        part_seq, sum_seq, sum_ready, sq_seq, warm = sems("part_seq sum_seq sum_ready sq_seq warm")
        mean_sq, var_ready, mean_out, cent_pool = sems("mean_sq var_ready mean_out cent_pool")
        sq_ready, ms_ready, std_ready, mean_ready, cent_ready, normed = sems(
            "sq_ready ms_ready std_ready mean_ready cent_ready normed")
        split_hi, split_ready = sems("split_hi split_ready")
        w2_ready, w2_split, wlr_ready, wlr_rest, lr_hi, sc_clear = sems("w2_ready w2_split wlr_ready wlr_rest lr_hi sc_clear")
        lr_done, lr_ready, z_done, t_ready, log_ready, decay_ready = sems(
            "lr_done lr_ready z_done t_ready log_ready decay_ready")
        vs_var, vs_std, vn_ready, sgu_done, mixed_used, gated = sems("vs_var vs_std vn_ready sgu_done mixed_used gated")
        diff_ready, exps_ready, kd_ready, ks_ready, qk_ready = sems("diff_ready exps_ready kd_ready ks_ready qk_ready")
        kt_done, kt_ready, sc_done, sc_ready, o_done, o_taken, up_done, st0_ready, st1_ready = sems(
            "kt_done kt_ready sc_done sc_ready o_done o_taken up_done st0_ready st1_ready")
        osq_ready, oms_done, ostd_ready, ob_ready, merged = sems("osq_ready oms_done ostd_ready ob_ready merged")
        conv_seq, conv_done, act_done, glu_done, g_rounded, g_ready = sems(
            "conv_seq conv_done act_done glu_done g_rounded g_ready")
        p_used, u_seq = sems("p_used u_seq")
        conv4_seq, conv4_done, conv4_act = sems("conv4_seq conv4_done conv4_act")
        ba_done, tok_act, gcum_ready, tok_ready, tokx_done, toks_ready = sems(
            "ba_done tok_act gcum_ready tok_ready tokx_done toks_ready")
        qsq_ready, qss_done, qstd_ready, bc_done, bc_used = sems("qsq_ready qss_done qstd_ready bc_done bc_used")
        pre_done, pre_used, dcy_exp, vb_ready, uu_pool, uu_dve = sems(
            "pre_done pre_used dcy_exp vb_ready uu_pool uu_dve")
        ml_ready, y_done, y_ready, ty_done, ty_used, ut_done = sems("ml_ready y_done y_ready ty_done ty_used ut_done")
        u_ready_act, u_ready_dve, vnew_act, vnew_dve = sems("u_ready_act u_ready_dve vnew_act vnew_dve")
        wt_done, wt_ready, vn_done, ov_done, ov_taken, s2_ready = sems(
            "wt_done wt_ready vn_done ov_done ov_taken s2_ready")
        onorm_sq, onorm_done, onorm_ms, onorm_std, onorm_r, ob2_done, on_used, sz_ready = sems(
            "onorm_sq onorm_done onorm_ms onorm_std onorm_r ob2_done on_used sz_ready")
        out_ready, stored = sems("out_ready stored")

        RMS_CTX, RMS_X, RMS_F, RMS_END, LN0 = 0, 1, 2, 3, 4
        LN_SUMS = 18
        S_X, S_GU, S_O, S_MERGED, S_F, S_H, S_ON, S_LN0, S_LN1, S_U, S_LN2 = range(11)
        whole = (a_hi, a_lo)
        half0 = (a_hi[:, :, 0:N1], a_lo[:, :, 0:N1])
        half1 = (a_hi[:, :, N1:], a_lo[:, :, N1:])

        def out_of(name):
            return TILE0[name] + TILES_OF[name] + 4

        CHUNK_ENDS = [(c0, c0 + cn) for c0, cn in CHUNKS]
        STEPS = [(lv, c) for lv in range(1, LOG2P) for c, (_, cn) in enumerate(CHUNKS) if 2 ** lv < cn]
        STEP = {step: i for i, step in enumerate(STEPS)}
        FLIPS = list(range(len(CHUNKS))) + [c for _, c in STEPS]

        G_ROWS, K_TOK, K_K, K_Q, V_TOK = range(5)

        def stage_banks(c, stage):
            b = 4 + 2 * ((5 * c + stage) % 2)
            return (b, b + 1)

        INV = [(0, (1, 2)), (3, (4, 5)), (6, (7,))]

        def firsts(ap, lv):
            return ap.rearrange("p h (n two b) -> p h n two b", two=2, b=2 ** lv)[:, :, :, 0]

        vnews = [cb[0]["ml0"], cb[1]["ml0"], vnew2]

        def octet(bs, cols, rows):
            per = HN // len(bs)
            return [(slice(per * i, per * i + per),
                     banks[b][0:rows, 0:per * cols].rearrange("p (h m) -> p h m", h=per)) for i, b in enumerate(bs)]

        def quad(bank, cols, rows=None):
            return bank[0:rows or cols, :].rearrange("p (h m) -> p h m", h=4)[:, :, 0:cols]

        block = ctx.enter_context(nc.Block())

        @block.sync
        def _(sp):
            def small(dst, src, s):
                sp.dma_start(dst, src).then_inc(s, 16)

            def unit(src, s):
                sp.dma_start(w_raw[:, s], src).then_inc(landed[s], 16)

            def stream_unit(name, i, s):
                unit(a[name][ds(i, 1)].rearrange("o p k m -> (o p) k m"), s)

            small(c2[:], a["c2"], first_in)
            small(ident[:], a["ident"], first_in)
            small(averages[:], a["averages"], first_in)
            small(pv[:], a["pv"], first_in)
            for j in range(4):
                if j >= 2:
                    sp.wait_ge(ada_done, j - 1)
                sp.dma_start(adab[j % 2][:], a["w_ada_first"][j]).then_inc(ada_in[j % 2], 16)
                if j == 0:
                    small(ctxt[:], a["ctx"], ctx_in)
                elif j == 1:
                    small(x[:], a["x"], x_in)
            for s in range(SLOTS):
                stream_unit("s0", s, s)
            small(wlr[:], a["w_lr"], wlr_in)
            small(csil[:], a["c"].partition_broadcast(P), c_in)
            small(gla_masks[:], a["gla_masks"], small_in)

            def ada_rows(pair, ring, s):
                sp.dma_start(adaw[ring][s][:], a["w_ada"][ds(pair, 1)].rearrange("o p t d -> (o p) t d")) \
                    .then_inc(row_in[2 * ring + s], 16)

            u0 = 0
            for name, parts in STREAMS:
                if parts is None:
                    with sp.Fori(0, 2) as it:
                        for j in range(4):
                            for b, (k0, kn) in enumerate(DOWN_SPLIT):
                                n = 3 * j + b
                                sp.wait_ge(lo_ready, it * 12 + (u0 + n - 3))
                                unit_src = a[name][ds(it * 4 + j, 1), :, k0:k0 + kn] \
                                    .rearrange("o p k m -> (o p) k m")
                                sp.dma_start(w_raw[:, n % 4, 0:kn], unit_src).then_inc(landed[n % 4], 16)
                    if name == "down0":
                        sp.wait_ge(split_ready, 8 * S_F + 8)
                        small(h[:, :, 0:META], a["meta"], h_in)
                        small(wba[:], a["w_ba"], gdn_in)
                        small(sel[:], a["sel"], gdn_in)
                        small(pick[:], a["pick"], gdn_in)
                        small(hb[:, 0:1], a["a_log"], gdn_in)
                        small(hb[:, 1:2], a["dt_bias"], gdn_in)
                    u0 += 24
                    continue
                n = sum(TILES_OF[x_] for x_ in parts)
                first = 0
                if u0 == 0:
                    with sp.Fori(1, 2) as it:
                        for s in range(SLOTS):
                            sp.wait_ge(lo_ready, it * 4 + (s - 3))
                            stream_unit(name, it * 4 + s, s)
                    sp.wait_ge(split_ready, 8)
                    for s in range(SLOTS):
                        sp.wait_ge(lo_ready, 5 + s)
                        stream_unit(name, 8 + s, s)
                    for p in range(2):
                        ada_rows(p, 0, p)
                    for s in range(SLOTS):
                        sp.wait_ge(lo_ready, 9 + s)
                        stream_unit(name, 12 + s, s)
                    for p in range(2, 4):
                        sp.wait_ge(row_used, p - 1)
                        ada_rows(p, 0, p % 2)
                    with sp.Fori(4, 8) as it:
                        for s in range(SLOTS):
                            sp.wait_ge(lo_ready, it * 4 + (s - 3))
                            stream_unit(name, it * 4 + s, s)
                    sp.wait_ge(kt_done, 8)
                    small(rows[:, 0], a["sgu_ln_g"].partition_broadcast(P), sgu_in)
                    small(rows[:, 1], a["sgu_ln_b"].partition_broadcast(P), sgu_in)
                    small(rows[:, 2], a["sgu_b"].partition_broadcast(P), sgu_in)
                    small(sguw[:], a["sgu_w"], sgu_in)
                    def four(it):
                        for s in range(SLOTS):
                            sp.wait_ge(lo_ready, 4 * it + s - 3)
                            stream_unit(name, 4 * it + s, s)

                    def two_rows(p, ring, used=True):
                        for s in range(2):
                            if used:
                                sp.wait_ge(row_used, p + s - 1)
                            ada_rows(p + s, ring, s)

                    four(8)
                    small(levels[:], a["levels"], gdn_in)
                    four(9)
                    sp.wait_ge(o_done, 4)
                    two_rows(4, 1, False)
                    four(10)
                    two_rows(6, 1)
                    four(11)
                    sp.wait_ge(gated, 8)
                    two_rows(8, 2, False)
                    for it in (12, 13, 14):
                        four(it)
                        two_rows(2 * it - 14, 2)
                    four(15)
                    first = 16
                if first * 4 < n:
                    with sp.Fori(first, n // 4) as it:
                        for s in range(SLOTS):
                            sp.wait_ge(lo_ready, it * 4 + (u0 + s - 3))
                            stream_unit(name, it * 4 + s, s)
                u0 += n
            for i in range(4):
                sp.wait_ge(out_ready, i + 1)
                sp.dma_start(out[:, 2 * i:2 * i + 2], h[:, 2 * i:2 * i + 2, META:N2]).then_inc(stored, 16)
            sp.wait_ge(stored, 64)

        @block.gpsimd
        def _(pool):
            pool.memset(eps6[:, 0:1], 1e-6).then_inc(fills, 1)
            pool.memset(eps6[:, 1:2], 1e-5).then_inc(fills, 1)
            pool.sem_inc(banks_free, SLOTS)
            pool.sem_inc(u_seq, 2)
            pool.sem_inc(p_used, 2)
            def remainders(u0, u1):
                with pool.Fori(u0 // 4, u1 // 4) as it:
                    for s in range(SLOTS):
                        pool.wait_ge(hi_ready, it * 4 + (s + 1))
                        pool.tensor_tensor(w_lo[:, s], w_raw[:, s], w_hi[:, s].bitcast(F32), ALU.subtract) \
                            .then_inc(lo_ready, 1)

            ahead = UNIT0["a_out"] + SLOTS
            remainders(0, SLOTS)
            pool.wait_ge(split_ready, 8)
            pool.memset(w2[:], 0.0).then_inc(fills, 1)
            pool.wait_ge(fills, 3)
            for i in range(3):
                for d in range(2):
                    r0 = 2 * RANK * i + RANK * d
                    pool.dma_start(w2[r0:r0 + RANK, d], a["gla_w2"][d]).then_inc(w2_in, 16)
            remainders(SLOTS, ahead)
            uu, mt = cb[0]["uu"][:], cb[0]["mt"][:]
            pool.wait_ge(pre_used, K_K + 1)
            pool.tensor_tensor(uu, mt, levels[:, 0].unsqueeze(1).broadcast_to([P, HN, P]), ALU.mult).then_inc(uu_pool, 1)
            pool.wait_ge(uu_pool, 1)
            pool.tensor_tensor(uu, ident[:].unsqueeze(1).broadcast_to([P, HN, P]), uu, ALU.subtract).then_inc(uu_pool, 1)
            pool.wait_ge(pre_used, 12)
            pool.wait_ge(vb_ready, 3)
            for i, (lv, c) in enumerate(STEPS):
                cn = CHUNKS[c][1]
                if lv > 2:
                    pool.wait_ge(y_done, STEP[lv - 2, c] + 1)
                pool.tensor_tensor(cb[c][f"ml{lv % 2}"][0:cn], cb[c]["mt"][0:cn],
                                   levels[0:cn, lv, 0:cn].unsqueeze(1).broadcast_to([cn, HN, cn]), ALU.mult) \
                    .then_inc(ml_ready, 1)

            def centre(i):
                pool.wait_ge(mean_out, i - LN0 + 1)
                for k in range(4, KD):
                    pool.tensor_tensor(h[:, k], h[:, k], part_sum[:], ALU.subtract).then_inc(cent_pool, 1)

            for i, behind in enumerate(("up1", "b_cx", "up2")):
                end = UNIT0[behind] + SLOTS
                remainders(ahead, end)
                centre(LN0 + i)
                ahead = end
            remainders(ahead, UNITS)
            centre(LN0 + 3)

        @block.tensor
        def _(pe):
            mm = nc.tensor.matmul

            def three(dst, pairs):
                n = 0
                last = 3 * len(pairs) - 1
                for (wh, wl), (xh, xl) in pairs:
                    for w_, x_ in ((wh, xh), (wh, xl), (wl, xh)):
                        ins = mm(dst, w_, x_, start=(n == 0), stop=(n == last))
                        n += 1
                return ins

            def lin(name, n, ops, split=None, its=None, tiles=None):
                u0, t0 = UNIT0[name], TILE0[name]

                def tile(it, s):
                    pe.wait_ge(lo_ready, it * 4 + (u0 + s + 1))
                    pe.wait_ge(banks_free, it * 4 + (t0 + s + 1))
                    m = 0
                    for k in range(KD):
                        if s == 0 and split is not None:
                            pe.wait_ge(split_ready, 8 * split + k + 1)
                        for w_, x_ in ((w_hi, ops[0]), (w_hi, ops[1]), (w_lo, ops[0])):
                            ins = mm(banks[s][:, 0:n], w_[:, s, k], x_[:, k, 0:n], start=(m == 0), stop=(m == 3 * KD - 1))
                            m += 1
                    ins.then_inc(unit_used, 1)

                if tiles:
                    for t in range(*tiles):
                        tile(t // SLOTS, t % SLOTS)
                    return
                with pe.Fori(*(its or (0, TILES_OF[name] // 4))) as it:
                    for s in range(SLOTS):
                        tile(it, s)

            def lin_tokens(name, tiles, pair=None):
                u0, t0 = UNIT0[name], TILE0[name]

                def two(it, s):
                    pe.wait_ge(lo_ready, it * 4 + (u0 + s + 2))
                    pe.wait_ge(banks_free, it * 4 + (t0 + s + 2))
                    for t in range(tiles):
                        dst = banks[s + t * 2 // tiles][:, 256 * (t % (tiles // 2)):][:, 0:256] \
                            .rearrange("p (u m) -> p u m", u=2)
                        tk = slice(t * P, t * P + P)
                        n = 0
                        for k in range(KD):
                            wh, wl = w_hi[:, s:s + 2, k], w_lo[:, s:s + 2, k]
                            for x_, w_ in ((a_hi, wh), (a_lo, wh), (a_hi, wl)):
                                ins = mm(dst, x_[:, k, tk], w_, start=(n == 0), stop=(n == 3 * KD - 1))
                                n += 1
                    ins.then_inc(unit_used, 2)

                if pair is not None:
                    two(pair // 2, 2 * (pair % 2))
                    return
                with pe.Fori(0, TILES_OF[name] // 4) as it:
                    for s in (0, 2):
                        two(it, s)

            def down(i, n, its=(0, 2)):
                name = f"down{i}"
                u0, t0 = UNIT0[name], TILE0[name]
                with pe.Fori(*its) as it:
                    for j in range(4):
                        pe.wait_ge(banks_free, it * 4 + (t0 + j + 1))
                        m = 0
                        for b, (k0, kn) in enumerate(DOWN_SPLIT):
                            s = (3 * j + b) % 4
                            pe.wait_ge(lo_ready, it * 12 + (u0 + 3 * j + b + 1))
                            for k in range(kn):
                                if j == 0:
                                    pe.wait_ge(g_ready, KF * i + k0 + k + 1)
                                for w_, x_ in ((w_hi, g_hi), (w_hi, g_lo), (w_lo, g_hi)):
                                    ins = mm(banks[j][:, 0:n], w_[:, s, k], x_[:, k0 + k, 0:n],
                                             start=(m == 0), stop=(m == 3 * KF - 1))
                                    m += 1
                            ins.then_inc(unit_used, 1)

            def rms(i):
                pe.wait_ge(part_seq, 9 * (i - RMS_F) + 9)
                mm(banks[5][:, 0:N1], over_d, part_sum[:, 0:N1], start=True, stop=False)
                for t in (3, 7):
                    pe.wait_ge(sq_ready, 8 * i + t + 1)
                    ins = mm(banks[5][:, 0:N1], over_d, sq[:, t, 0:N1], start=False, stop=(t == 7))
                ins.then_inc(ms_ready, 1)

            def first_mean(i):
                pe.wait_ge(part_seq, LN_SUMS + 7 * (i - LN0) + 1)
                mm(banks[4][:, 0:N2], over_d, part_sum[:], start=True, stop=True).then_inc(mean_ready, 1)

            def ln_norm(i, name):
                pe.wait_ge(part_seq, LN_SUMS + 7 * (i - LN0) + 7)
                mm(banks[4][:, 0:N2], over_d, part_sum[:], start=True, stop=False)
                pe.wait_ge(sq_seq, 6 * (i - LN0) + 6)
                mm(banks[5][:, 0:N2], over_d, sq[:, 0], start=True, stop=False)
                pe.wait_ge(banks_free, TILE0[name] + 7 + 5)
                mm(banks[4][:, 0:N2], over_d, h[:, 7], start=False, stop=True).then_inc(mean_ready, 1)
                pe.wait_ge(sq_ready, 8 * i + 8)
                mm(banks[5][:, 0:N2], over_d, sq[:, 7], start=False, stop=True).then_inc(ms_ready, 1)

            pe.wait_ge(first_in, 64)
            for _ in range(16):
                ins = mm(banks[5][:, 0:P], ident[:], ident[:], start=True, stop=True)
            ins.then_inc(warm, 1)
            pe.wait_ge(csil_ready, 1)
            for j in range(5):
                if j < 4:
                    pe.wait_ge(ada_in[j % 2], 16 * (j // 2) + 16)
                    if j >= 2:
                        pe.wait_ge(modrow_ready, j - 1)
                    for k in range(KD):
                        ins = mm(banks[6 + j % 2][0:2, :], c2[:, k], adab[j % 2][:, k], start=(k == 0), stop=(k == KD - 1))
                    ins.then_inc(ada_done, 1)
                if j >= 1:
                    pe.wait_ge(modrow_ready, j)
                    if j >= 3:
                        pe.wait_ge(mod_taken, j - 2)
                    for i in range(4):
                        ins = nc.tensor.transpose(banks[2 + (j - 1) % 2][:, 2 * i:2 * i + 2],
                                                  modrow[:, (j - 1) % 2, i * P:(i + 1) * P], ident[0:2, 0:2])
                    ins.then_inc(mod_flipped, 1)
                if j < 2:
                    pe.wait_ge(sum_ready, j + 1)
                    pe.wait_ge(warm, 1)
                    mm(banks[4 + j][:, 0:N1], over_d, (sq, sqx)[j][:, 0, 0:N1], start=True, stop=True).then_inc(ms_ready, 1)
            lin("w_k", 2 * N1, whole, S_X, tiles=(0, 4))
            pe.wait_ge(wlr_rest, 1)
            pe.wait_ge(modrow_ready, 4)
            m = 0
            for k in range(KD):
                for w_, x_ in ((wlr_hi, a_hi), (wlr_hi, a_lo), (wlr_lo, a_hi)):
                    ins = mm(banks[6][0:96, :], w_[:, k], x_[:, k], start=(m == 0), stop=(m == 3 * KD - 1))
                    m += 1
            ins.then_inc(lr_done, 1)
            lin("w_q", N1, half0, tiles=(0, 4))
            pe.wait_ge(lr_ready, 1)
            pe.wait_ge(w2_split, 1)
            for i in range(2 * HG):
                d, hh = divmod(i, HG)
                if i >= 4:
                    pe.wait_ge(t_ready, i - 3)
                mm(banks[4 + i % 4][:, :], w2s[:, d, hh * DK:(hh + 1) * DK], lrs[:], start=True, stop=True) \
                    .then_inc(z_done, 1)
            lin_tokens("w_v", 4)

            def scores(d):
                pe.wait_ge(qk_ready, 2 * d + 2)
                pe.wait_ge(kd_ready, d + 1)
                pe.wait_ge(sc_clear, d + 1)
                if d:
                    pe.wait_ge(st0_ready, 1)
                else:
                    pe.wait_ge(t_ready, 8)
                for blk in range(2):
                    e, l = GC * d, GC * (1 - d)
                    tk = slice(blk * P, (blk + 1) * P)
                    for hh in range(HG):
                        mm(banks[6 + blk][:, hh * P:(hh + 1) * P], ki[d][:, hh, tk], qd[d][:, hh, tk],
                           start=True, stop=True)
                        ins = mm(banks[6 + blk][e:e + GC, hh * P + l:hh * P + l + GC],
                                 kd[:, hh, blk * P + e:blk * P + e + GC], qd[d][:, hh, blk * P + l:blk * P + l + GC],
                                 start=True, stop=True)
                    ins.then_inc(sc_done, 1)

            def keys(d, blks):
                pe.wait_ge(ks_ready, d + 1)
                for blk in blks:
                    if blk >= 2:
                        pe.wait_ge(kt_ready, 4 * d + blk - 1)
                    elif d:
                        pe.wait_ge(st1_ready, 1)
                    for hh in range(HG):
                        ins = nc.tensor.transpose(banks[4 + blk % 2][:, hh * DK:(hh + 1) * DK],
                                                  ks[:, hh, blk * P:(blk + 1) * P], ident[:])
                    ins.then_inc(kt_done, 1)

            def states(d):
                pe.wait_ge(kt_ready, 4 * d + 4)
                pe.wait_ge(banks_free, out_of("w_v"))
                pe.wait_ge(sc_ready, 2 * d + 2)
                for hh in range(HG):
                    for blk in range(2):
                        ins = mm(banks[6 + hh // 2][:, (hh % 2) * DV:(hh % 2 + 1) * DV], kt(2 + blk, hh),
                                 vc[:, blk, hh * DV:(hh + 1) * DV], start=(blk == 0), stop=(blk == 1))
                ins.then_inc(up_done, 1)
                for hh in range(HG):
                    ins = mm(banks[4 + hh // 2][:, (hh % 2) * DV:(hh % 2 + 1) * DV], kt(d, hh),
                             vx[:, d, hh * DV:(hh + 1) * DV], start=True, stop=True)
                ins.then_inc(up_done, 1)

            def outputs():
                pe.wait_ge(sc_ready, 4)
                pe.wait_ge(st0_ready, 2)
                pe.wait_ge(st1_ready, 2)
                for blk in range(2):
                    for hh in range(HG):
                        for half in range(2):
                            c0, col = ((hh % 2) * 2 + half) * P, hh * DV + half * P
                            dst = banks[4 + 2 * blk + hh // 2][:, c0:c0 + P]
                            for d in range(2):
                                state = (st0 if blk == d else st1)[d]
                                mm(dst, vx[:, blk, col:col + P], sc(d, blk, hh), start=(d == 0), stop=False)
                                ins = mm(dst, state[:, hh, half * P:(half + 1) * P], qs[d][:, hh, blk * P:(blk + 1) * P],
                                         start=False, stop=(d == 1))
                        if hh % 2:
                            ins.then_inc(o_done, 1)

            pe.wait_ge(small_in, 16)
            scores(0)
            keys(0, (0, 1))
            lin_tokens("w_vs", 2, 0)
            keys(0, (2, 3))
            lin_tokens("w_vs", 2, 1)
            states(0)
            lin_tokens("w_vs", 2, 2)
            lin_tokens("w_vs", 2, 3)
            scores(1)
            keys(1, (0, 1))
            lin("w_u", N1, half0, tiles=(0, 2))
            keys(1, (2, 3))
            lin("w_u", N1, half0, tiles=(2, 4))
            states(1)
            lin("w_u", N1, half0, tiles=(4, 8))
            outputs()
            lin("w_r", N1, half0, tiles=(0, 4))
            pe.wait_ge(sgu_in, 64)
            pe.wait_ge(o_taken, 4)
            for n in range(2):
                pe.wait_ge(vn_ready, n + 1)
                for half in range(2):
                    for g in range(4):
                        gg = 4 * half + g
                        ins = mm(banks[4 + 2 * n + half][:, g * P:(g + 1) * P], vs[:, n, gg * P:(gg + 1) * P],
                                 sguw[:, gg], start=True, stop=True)
                    ins.then_inc(sgu_done, 1)
            lin("w_r", N1, half0, tiles=(4, 8))
            pe.wait_ge(gated, 8)
            for b in range(2):
                pe.wait_ge(osq_ready, b + 1)
                for hh in (2 * b, 2 * b + 1):
                    for half in range(2):
                        ins = mm(banks[4 + b][:, (hh % 2) * N1:(hh % 2 + 1) * N1], over_dv, osq[:, hh, half],
                                 start=(half == 0), stop=(half == 1))
                ins.then_inc(oms_done, 1)
            lin("w_ga", N1, half0)
            lin("w_gb", N1, half0)
            lin("w_br_a", N1, half1, S_GU)
            lin("w_br_b", N1, half0, S_O)
            lin("w_o", N1, half1, S_MERGED)
            rms(RMS_F)
            lin("up0", N1, half0, S_F)
            down(0, N1)
            rms(RMS_END)

            lin("a_in", N2, whole, S_H, its=(0, 6))
            pe.wait_ge(gdn_in, 96)
            for j in range(2):
                for k in range(KD):
                    ins = mm(banks[6 + j][0:HN, 0:N2], wba[:, k, j * HN:(j + 1) * HN], h[:, k],
                             start=(k == 0), stop=(k == KD - 1))
                ins.then_inc(ba_done, 1)
            def head_rows(bank, src, n0, n1, done):
                for hh in range(HN):
                    ins = mm(banks[bank][0:HN, n0:n1], pick[:, hh], src[:, hh, n0:n1], start=(hh == 0), stop=(hh == HN - 1))
                ins.then_inc(done, 1)

            pe.wait_ge(qsq_ready, 1)
            head_rows(4, ksq, 0, N2, qss_done)
            lin("a_in", N2, whole, tiles=(24, 27))
            pe.wait_ge(qsq_ready, 2)
            head_rows(5, sq, 0, N2, qss_done)
            lin("a_in", N2, whole, tiles=(27, 29))
            pe.wait_ge(tok_ready, 1)
            for ci, (c0, cn) in enumerate(CHUNKS):
                for j, r in enumerate((7, 1, 2, 3, 8)):
                    ins = nc.tensor.transpose(banks[6][0:cn, (5 * ci + j) * HN:(5 * ci + j + 1) * HN],
                                              tok[:, r, c0:c0 + cn], ident[0:HN, 0:HN])
            ins.then_inc(tokx_done, 1)
            mm(banks[7][:, 0:4 * HN], ones[0:HN], glsp[:].rearrange("p h c -> p (h c)"), start=True, stop=True) \
                .then_inc(tokx_done, 1)
            pe.wait_ge(qstd_ready, 2)
            for c, (c0, cn) in enumerate(CHUNKS):
                tk = slice(c0, c0 + cn)
                for stage in range(5):
                    if c == 0 and stage in (G_ROWS, K_K, K_Q):
                        t = 29 + (G_ROWS, K_K, K_Q).index(stage)
                        lin("a_in", N2, whole, tiles=(t, t + 1))
                    if c == 0 and stage == K_TOK:
                        pe.wait_ge(toks_ready, 2)
                    if 5 * c + stage >= 2:
                        last_c, last = divmod(5 * c + stage - 2, 5)
                        if last == V_TOK:
                            pe.wait_ge(vb_ready, last_c + 1)
                        else:
                            pe.wait_ge(pre_used, 4 * last_c + last + 1)
                    for heads, dst in octet(stage_banks(c, stage), P if stage in (K_TOK, V_TOK) else cn, cn):
                        for i in range(4):
                            hh = heads.start + i
                            if stage == G_ROWS:
                                ins = mm(dst[:, i], sel[:, hh, 0:cn], tok[:, 1, tk], start=True, stop=True)
                            elif stage in (K_TOK, V_TOK):
                                ins = nc.tensor.transpose(dst[:, i], qkv[:, (8 if stage == K_TOK else 16) + hh, tk], ident[:])
                            else:
                                ins = mm(dst[:, i], qkv[:, 8 + hh, tk], qkv[:, (8 if stage == K_K else 0) + hh, tk],
                                         start=True, stop=True)
                    ins.then_inc(pre_done, 1)
                    if c == 1 and stage < 4:
                        for hh in (2 * stage, 2 * stage + 1):
                            if hh == 0:
                                pe.wait_ge(banks_free, out_of("a_in"))
                            elif hh >= 4:
                                pe.wait_ge(bc_used, hh - 3)
                            mm(banks[hh % 4][:, 0:N2], sel[:, hh], tok[:, 2], start=True, stop=True).then_inc(bc_done, 1)
            pe.wait_ge(pre_used, 12)
            pe.wait_ge(vb_ready, 3)
            pe.wait_ge(bc_used, HN)

            def flip(c, src, dst_sem):
                cn = CHUNKS[c][1]
                for heads, dst in octet(INV[c][1], cn, cn):
                    for i in range(heads.stop - heads.start):
                        ins = nc.tensor.transpose(dst[:, i], cb[c][src][0:cn, heads.start + i], ident[0:cn, 0:cn])
                ins.then_inc(dst_sem, 1)

            def wait_flip(n):
                pe.wait_ge(u_ready_act, n + 1)
                pe.wait_ge(u_ready_dve, sum(c < 2 for c in FLIPS[:n + 1]))

            for c in range(3):
                if c == 0:
                    pe.wait_ge(uu_pool, 2)
                else:
                    pe.wait_ge(uu_dve, 2 * c)
                flip(c, "uu", ut_done)
            for lv in range(1, LOG2P):
                now = [c for c in range(3) if (lv, c) in STEP]
                before = {c: STEP[lv - 1, c] if lv > 1 else None for c in now}
                for c in now:
                    cn, B, i = CHUNKS[c][1], cb[c], STEP[lv, c]
                    pe.wait_ge(ml_ready, i + 1)
                    if lv > 1:
                        pe.wait_ge(ty_used, before[c] + 1)
                    else:
                        wait_flip(c)
                    for heads, dst in octet((INV[c][0],), cn // 2, cn):
                        for hh in range(HN):
                            ins = mm(dst[:, hh].rearrange("p (n b) -> p n b", b=2 ** lv), B[f"ml{lv % 2}"][0:cn, hh],
                                     firsts(B["tt"][0:cn], lv)[:, hh], start=True, stop=True)
                    ins.then_inc(y_done, 1)
                for c in now:
                    cn, B, i = CHUNKS[c][1], cb[c], STEP[lv, c]
                    pe.wait_ge(y_ready, i + 1)
                    if lv > 1:
                        wait_flip(3 + before[c])
                    for heads, dst in octet((INV[c][0],), cn // 2, cn):
                        for hh in range(HN):
                            ins = mm(dst[:, hh], B["uu"][0:cn, hh], B["yy"][0:cn, hh], start=True, stop=True)
                    ins.then_inc(ty_done, 1)
                for c in now:
                    pe.wait_ge(ty_used, STEP[lv, c] + 1)
                    flip(c, "tt", ut_done)
            wait_flip(len(FLIPS) - 1)

            def w_t(c):
                cn, B = CHUNKS[c][1], cb[c]
                if c == 2:
                    pe.wait_ge(wt_ready, 1)
                for heads, dst in octet((4, 5), cn, P):
                    for i in range(4):
                        hh = heads.start + i
                        ins = mm(dst[:, i], B["kbeg"][0:cn, hh], B["uu"][0:cn, hh], start=True, stop=True)
                ins.then_inc(wt_done, 1)

            for c, (c0, cn) in enumerate(CHUNKS):
                B, tk = cb[c], slice(c0, c0 + cn)
                vnew = vnews[c]
                if c:
                    pe.wait_ge(wt_ready, c)
                    if c == 2:
                        pe.wait_ge(onorm_sq, 1)
                        head_rows(4, osq2, *CHUNK_ENDS[0], onorm_done)
                    pe.wait_ge(s2_ready, c)
                for heads, dst in octet((0, 1), P, cn):
                    for i in range(4):
                        hh = heads.start + i
                        ins = mm(dst[:, i], B["uu"][0:cn, hh], B["vb"][0:cn, hh], start=True, stop=(c == 0))
                        if c:
                            ins = mm(dst[:, i], B["tt"][:, hh], s2[:, hh], start=False, stop=True)
                ins.then_inc(vn_done, 1)
                if c < 2:
                    w_t(c + 1)
                if c == 2:
                    pe.wait_ge(onorm_sq, 2)
                    head_rows(4, osq2, *CHUNK_ENDS[1], onorm_done)
                pe.wait_ge(vnew_act, c + 1)
                pe.wait_ge(vnew_dve, c + 1)
                if c:
                    pe.wait_ge(ov_taken, c)
                if c < 2:
                    for heads, dst in octet((6, 7), P, P):
                        for i in range(4):
                            hh = heads.start + i
                            ins = mm(dst[:, i], B["kdc"][0:cn, hh], vnew[0:cn, hh], start=True, stop=True)
                for heads, dst in octet((2, 3), cn, P):
                    for i in range(4):
                        hh = heads.start + i
                        ins = mm(dst[:, i], vnew[0:cn, hh], B["qkd"][0:cn, hh], start=True, stop=(c == 0))
                        if c:
                            ins = mm(dst[:, i], s2[:, hh], qg[:, hh, tk], start=False, stop=True)
                ins.then_inc(ov_done, 1)
            pe.wait_ge(onorm_sq, 3)
            head_rows(5, osq2, N1, N2, onorm_done)
            pe.wait_ge(onorm_r, 1)
            for i in range(4):
                if i >= 2:
                    pe.wait_ge(on_used, i - 1)
                for j in range(2):
                    ins = mm(banks[6 + i % 2][:, j * N1:(j + 1) * N1], sel[:, 2 * i + j], tok[:, 5, 0:N1], start=True, stop=True)
                ins.then_inc(ob2_done, 1)
            pe.wait_ge(onorm_r, 2)
            pe.wait_ge(ov_taken, 3)
            mm(banks[3][:, 0:HN * (N2 - N1)], ones[0:HN], tok5sp[:].rearrange("p h t -> p (h t)"), start=True, stop=True) \
                .then_inc(ob2_done, 1)
            lin("a_out", N2, whole, S_ON, its=(0, 1))
            first_mean(LN0)
            lin("a_out", N2, whole, its=(1, 2))
            ln_norm(LN0, "a_out")
            lin("up1", N2, whole, S_LN0)
            down(1, N2, (0, 1))
            first_mean(LN0 + 1)
            down(1, N2, (1, 2))
            ln_norm(LN0 + 1, "down1")
            lin("b_cx", N2, whole, S_LN1)
            lin("b_b", N2, whole)
            lin("b_out", N2, (u_hi, u_lo), S_U, its=(0, 1))
            first_mean(LN0 + 2)
            lin("b_out", N2, (u_hi, u_lo), its=(1, 2))
            ln_norm(LN0 + 2, "b_out")
            lin("up2", N2, whole, S_LN2)
            down(2, N2, (0, 1))
            first_mean(LN0 + 3)
            down(2, N2, (1, 2))
            ln_norm(LN0 + 3, "down2")

        @block.scalar
        def _(act):
            act_n = [0]

            def link(ins):
                act_n[0] += 1
                ins.then_inc(act_seq, 1)
                act.wait_ge(act_seq, act_n[0])

            def fn(out_, in_, f, **kw):
                return nc.scalar.activation(out_, in_, f, **kw)

            def round_unit(u, s):
                act.wait_ge(landed[s], u * 4 + 16 - 4 * s)
                fn(w_hi[:, s], w_raw[:, s], ACT.Copy).then_inc(hi_ready, 1)

            def lin(name, evac, its=None, after=None):
                u0 = UNIT0[name]
                with act.Fori(*(its or (0, TILES_OF[name] // 4))) as it:
                    for s in range(SLOTS):
                        act.wait_ge(unit_used, it * 4 + (u0 + s + 1))
                        if evac is not None:
                            evac(it * 4 + s, s)
                        round_unit(it * 4 + (u0 + s + 4), s)
                        if after is not None:
                            after(it * 4 + s)

            def down(i, after, its=(0, 2)):
                u0 = UNIT0[f"down{i}"]
                with act.Fori(*its) as it:
                    for j in range(4):
                        for b in range(3):
                            n = 3 * j + b
                            act.wait_ge(unit_used, it * 12 + (u0 + n + 1))
                            round_unit(it * 12 + (u0 + n + 4), n % SLOTS)
                        if after is not None:
                            after(it * 4 + j)

            def down_end(i, after):
                u0 = UNIT0[f"down{i}"]
                for n in range(12, 24):
                    act.wait_ge(unit_used, u0 + n + 1)
                    if u0 + n + 4 < UNITS:
                        round_unit(u0 + n + 4, n % SLOTS)
                    if n % 3 == 2:
                        after(n // 3)

            def split(i, dst, src, ready, count, shift=None):
                for k in range(KD):
                    act.wait_ge(ready, count + k + 1)
                    if shift is None:
                        ins = fn(dst[:, k], src[:, k], ACT.Copy)
                    else:
                        ins = fn(dst[:, k], src[:, k], ACT.Identity, bias=shift(k))
                    ins.then_inc(split_hi, 1)

            def a_of(n):
                return a_hi[:, :, 0:n]

            def column(name, i):
                return pv[:, PV[name] + i:PV[name] + i + 1]

            def square_after(name):
                def after(t):
                    act.wait_ge(banks_free, t + (TILE0[name] + 5))
                    fn(sq[:, ds(t, 1), 0:N1], x[:, ds(t, 1)], ACT.Square).then_inc(sq_ready, 1)
                return after

            def root(i, n, e):
                act.wait_ge(ms_ready, i + 1)
                c0, bank = (N1, 4) if i == RMS_CTX else (0, 5)
                fn(rstd[:, c0:c0 + n], banks[bank][:, 0:n], ACT.Sqrt, bias=eps6[:, e:e + 1]).then_inc(std_ready, 1)

            act.wait_ge(fills, 2)
            act.wait_ge(first_in, 64)
            fn(c2[:], c2[:], ACT.Silu).then_inc(csil_ready, 1)
            nc.scalar.preload_act_table(ACT.Sqrt)
            act.wait_ge(ctx_in, 16)
            for k in range(KD):
                fn(sq[:, k, 0:N1], ctxt[:, k], ACT.Square).then_inc(sq_ready, 1)
            def mod_rows(j):
                act.wait_ge(ada_done, j + 1)
                if j >= 2:
                    act.wait_ge(mod_flipped, j - 1)
                fn(modrow[:, j % 2], banks[6 + j % 2][0:2, :], ACT.Copy).then_inc(modrow_ready, 1)

            def modulated(j):
                for k in (2 * j, 2 * j + 1):
                    act.wait_ge(gain_ready, j + 1)
                    for jj, src in enumerate((xr, ctxt)):
                        ins = fn(a_hi[:, k, jj * N1:(jj + 1) * N1], src[:, k], ACT.Identity, scale=gain[:, jj, k:k + 1],
                                 bias=mod[:, jj, k:k + 1])
                    ins.then_inc(split_hi, 1)

            root(RMS_CTX, N1, 0)
            mod_rows(0)
            act.wait_ge(x_in, 16)
            for k in range(KD):
                fn(sqx[:, k, 0:N1], x[:, k], ACT.Square).then_inc(sq_ready, 1)
            root(RMS_X, N1, 0)
            mod_rows(1)
            act.wait_ge(xr_ready, 2)
            modulated(0)
            mod_rows(2)
            for s in (0, 1):
                round_unit(s, s)
            modulated(1)
            for s in (2, 3):
                round_unit(s, s)
            mod_rows(3)
            modulated(2)
            modulated(3)
            act.wait_ge(wlr_in, 16)
            fn(wlr_hi[:], wlr[:], ACT.Copy).then_inc(wlr_ready, 1)
            lin("w_k", lambda t, s: fn(k1[:, ds(t, 1)], banks[s][:, :].unsqueeze(1), ACT.Copy).then_inc(banks_free, 1))
            def units(name, evac, a_, b_):
                u0 = UNIT0[name]
                for u in range(a_, b_):
                    act.wait_ge(unit_used, u0 + u + 1)
                    evac(u, u % SLOTS)
                    round_unit(u0 + u + 4, u % SLOTS)

            act.wait_ge(lr_done, 1)
            fn(lrs[:], banks[6][0:96, :], ACT.Copy).then_inc(lr_hi, 1)
            act.wait_ge(w2_in, 96)
            fn(w2s[:], w2[:], ACT.Copy).then_inc(w2_ready, 1)
            act.wait_ge(c_in, 16)
            fn(csil[:], csil[:], ACT.Silu).then_inc(csil_ready, 1)
            lin("w_q", lambda t, s: fn(q1[:, ds(t, 1)], banks[s][:, 0:N1].unsqueeze(1), ACT.Copy, scale=DK ** -0.5)
                .then_inc(banks_free, 1))
            act.wait_ge(t_ready, 8)
            link(fn(ebuf[:], la[:], ACT.Abs))
            link(fn(ebuf[:], ebuf[:], ACT.Exp, scale=-1.0))
            fn(ebuf[:], ebuf[:], ACT.Ln, bias=1.0).then_inc(log_ready, 1)

            def evac_v(t, s):
                if s % 2 == 0:
                    return
                for b, dst in ((s - 1, vx), (s, vc)):
                    fn(dst[:, :, (t - 1) * P:(t + 1) * P], banks[b][:, :].rearrange("p (t m) -> p t m", t=2), ACT.Copy) \
                        .then_inc(banks_free, 1)

            def evac_vs(t, s):
                if s % 2 == 0:
                    return
                for b in range(2):
                    fn(vs[:, b, (t - 1) * P:(t + 1) * P], banks[s - 1 + b][:, 0:2 * P], ACT.Gelu).then_inc(banks_free, 1)

            def evac_u(t, s):
                fn(gu[:, t], banks[s][:, 0:N1], ACT.Gelu).then_inc(banks_free, 1)

            def evac_r(t, s):
                fn(sr[:, t], banks[s][:, 0:N1], ACT.Silu).then_inc(banks_free, 1)

            def powers(d):
                fn(qd[d][:], ebuf[:, d, :, 0:N1], ACT.Exp, scale=1 / 16).then_inc(exps_ready, 1)
                fn(ki[d][:], ebuf[:, d, :, 0:N1], ACT.Exp, scale=-1 / 16).then_inc(exps_ready, 1)
                flat = ebuf[:, d].rearrange("p h (c t) -> p h c t", t=GC)
                last = flat[:, :, :, GC - 1] if d == 0 else flat[:, :, :, 0]
                fn(dec[:, d], last, ACT.Exp, scale=1 / 16).then_inc(exps_ready, 1)

            def key_powers(d):
                act.wait_ge(diff_ready, d + 1)
                fn(kd[:], kd[:], ACT.Exp, scale=1 / 16).then_inc(exps_ready, 1)

            def keys(d, blks):
                for blk in blks:
                    act.wait_ge(kt_done, 4 * d + blk + 1)
                    if d and blk == 0:
                        act.wait_ge(up_done, 2)
                    fn(spare_hi[:, 2 * blk:2 * blk + 2], banks[4 + blk % 2][:, :].rearrange("p (h k) -> p h k", h=2),
                       ACT.Copy).then_inc(kt_ready, 1)

            def context_state(d):
                act.wait_ge(up_done, 2 * d + 1)
                act.wait_ge(exps_ready, 8 if d else 7)
                for b in range(2):
                    ins = fn(st0[d][:, 2 * b:2 * b + 2], banks[6 + b][:, :].rearrange("p (h v) -> p h v", h=2), ACT.Copy)
                ins.then_inc(st0_ready, 1)

            nc.scalar.preload_act_table(ACT.Exp)
            units("w_v", evac_v, 0, 4)
            act.wait_ge(decay_ready, 2)
            powers(0)
            key_powers(0)
            powers(1)
            units("w_v", evac_v, 4, 8)
            keys(0, (0, 1))
            nc.scalar.preload_act_table(ACT.Gelu)
            act.wait_ge(row_used, 4)
            units("w_vs", evac_vs, 0, 2)
            keys(0, (2, 3))
            units("w_vs", evac_vs, 2, 4)
            context_state(0)
            units("w_vs", evac_vs, 4, 6)
            key_powers(1)
            nc.scalar.preload_act_table(ACT.Gelu)
            units("w_vs", evac_vs, 6, 8)
            keys(1, (0, 1))
            units("w_u", evac_u, 0, 2)
            keys(1, (2, 3))
            units("w_u", evac_u, 2, 4)
            context_state(1)
            act.wait_ge(vs_var, 2)
            for n in range(2):
                fn(mv[:, n, 2:3], mv[:, n, 1:2], ACT.Sqrt, bias=eps6[:, 0:1]).then_inc(vs_std, 1)
            nc.scalar.preload_act_table(ACT.Gelu)
            units("w_u", evac_u, 4, 8)
            nc.scalar.preload_act_table(ACT.Silu)
            units("w_r", evac_r, 0, 4)
            for b in range(2):
                act.wait_ge(o_taken, 3 + b)
                fn(osq[:, 2 * b:2 * b + 2], o1[:, 2 * b:2 * b + 2], ACT.Square).then_inc(osq_ready, 1)
            units("w_r", evac_r, 4, 8)
            for b in range(2):
                act.wait_ge(oms_done, b + 1)
                fn(orstd[:, 2 * b:2 * b + 2], banks[4 + b][:, :].rearrange("p (h t) -> p h t", h=2), ACT.Sqrt,
                   bias=eps6[:, 0:1]).then_inc(ostd_ready, 1)
            nc.scalar.preload_act_table(ACT.Sigmoid)
            split(S_GU, half1[0], gu, gated, 0)
            act.wait_ge(row_used, 8)
            lin("w_ga", lambda t, s: fn(ga[:, ds(t, 1)], banks[s][:, 0:N1].unsqueeze(1), ACT.Sigmoid).then_inc(banks_free, 1))
            lin("w_gb", lambda t, s: fn(gb[:, ds(t, 1)], banks[s][:, 0:N1].unsqueeze(1), ACT.Sigmoid).then_inc(banks_free, 1))
            split(S_O, half0[0], o1[:].rearrange("p h v t -> p (h v) t"), ob_ready, 0)
            lin("w_br_a", None)

            def round_merged(t):
                act.wait_ge(merged, t + 1)
                fn(half1[0][:, ds(t, 1)], gb[:, ds(t, 1)], ACT.Copy).then_inc(split_hi, 1)

            lin("w_br_b", None, after=round_merged)
            lin("w_o", None, after=square_after("w_o"))
            root(RMS_F, N1, 0)
            split(S_F, half0[0], h[:, :, 0:N1], normed, 0, lambda k: mod[:, 0, 24 + k:25 + k])

            def ffn(i, n, f, w_center, bias):
                name = f"up{i}"
                u0, j0 = UNIT0[name], KF * i
                nc.scalar.preload_act_table(f)

                def activate(j, p):
                    act.wait_ge(conv_done, j + (j0 + p + 1))
                    fn(gbuf[:, p, 0:n], cbuf[:, p, 0:n], f).then_inc(act_done, 1)

                def tiles(it, first):
                    for p in range(2):
                        s = 2 * p
                        u = it * 4 + (u0 + s)
                        act.wait_ge(unit_used, u + 1)
                        if not first:
                            act.wait_ge(act_done, it * 2 + (j0 + p - 1))
                        fn(abuf[:, p, 0:n], banks[s][:, 0:n], ACT.Copy)
                        kw = {"scale": pv[:, ds(it * 2 + (w_center + p), 1)]}
                        if bias is not None:
                            kw["bias"] = pv[:, ds(it * 2 + (bias + p), 1)]
                        fn(cbuf[:, p, 0:n], banks[s][:, 0:n], ACT.Identity, **kw).then_inc(banks_free, 1)
                        round_unit(u + 4, s)
                        act.wait_ge(unit_used, u + 2)
                        if not first:
                            act.wait_ge(glu_done, it * 2 + (j0 + p - 1))
                        fn(vbuf[:, p, 0:n], banks[s + 1][:, 0:n], ACT.Copy).then_inc(banks_free, 1)
                        round_unit(u + 5, s + 1)

                tiles(0, True)
                with act.Fori(1, KF // 2) as it:
                    for p in range(2):
                        activate(it * 2 - 2, p)
                    tiles(it, False)
                for p in range(2):
                    activate(KF - 2, p)

            ffn(0, N1, ACT.Gelu, PV["conv1_w"] + 4 * KF, PV["conv1_b"])
            nc.scalar.preload_act_table(ACT.Sqrt)
            down(0, square_after("down0"))
            root(RMS_END, N1, 0)
            act.wait_ge(h_in, 16)
            split(S_H, a_of(N2), h, normed, 8)
            u0 = UNIT0["a_in"]

            def qkv_tiles(it, first):
                for s in range(SLOTS):
                    act.wait_ge(unit_used, it * 4 + (u0 + s + 1))
                    if not first:
                        act.wait_ge(conv4_act, it * 4 + (s - 3))
                    fn(conva[:, s], banks[s][:, 0:N2], ACT.Copy)
                    fn(convc[:, s], banks[s][:, 0:N2], ACT.Copy, scale=pv[:, ds(it * 4 + (PV["a_conv"] + 3 * 24 + s), 1)]) \
                        .then_inc(banks_free, 1)
                    round_unit(it * 4 + (u0 + s + 4), s)

            def qkv_activate(it):
                for s in range(SLOTS):
                    act.wait_ge(conv4_done, it * 4 + (s + 1))
                    fn(qkv[:, ds(it * 4 + s, 1)], convc[:, s].unsqueeze(1), ACT.Silu).then_inc(conv4_act, 1)

            nc.scalar.preload_act_table(ACT.Silu)
            qkv_tiles(0, True)
            with act.Fori(1, 6) as it:
                qkv_activate(it - 1)
                qkv_tiles(it, False)
            fn(ksq[:], qkv[:, 8:16], ACT.Square).then_inc(qsq_ready, 1)
            qkv_activate(5)
            fn(sq[:], qkv[:, 0:8], ACT.Square).then_inc(qsq_ready, 1)
            act.wait_ge(gdn_in, 96)
            act.wait_ge(ba_done, 2)
            fn(tok[:, 0], banks[6][0:HN, 0:N2], ACT.Sigmoid).then_inc(tok_act, 1)
            fn(tok[:, 1], banks[7][0:HN, 0:N2], ACT.Identity, bias=hb[:, 1:2]).then_inc(tok_act, 1)
            fn(hb[:, 2:3], hb[:, 0:1], ACT.Exp).then_inc(tok_act, 1)
            act.wait_ge(tok_act, 2)
            link(fn(tok[:, 5], tok[:, 1], ACT.Abs))
            link(fn(tok[:, 5], tok[:, 5], ACT.Exp, scale=-1.0))
            fn(tok[:, 5], tok[:, 5], ACT.Ln, bias=1.0).then_inc(tok_act, 1)

            def evac_z(t, s):
                fn(sz[:, t - 24], banks[s][:, 0:N2], ACT.Copy).then_inc(banks_free, 1)

            def length(j):
                act.wait_ge(qss_done, j + 1)
                fn(tok[:, 7 - j], banks[4 + j][0:HN, 0:N2], ACT.Sqrt, bias=eps6[0:HN, 0:1]).then_inc(qstd_ready, 1)

            act.wait_ge(conv4_act, 24)
            length(0)
            units("a_in", evac_z, 24, 25)
            act.wait_ge(gcum_ready, 1)
            fn(tok[:, 2], tok[:, 1], ACT.Exp).then_inc(tok_act, 1)
            fn(tok[:, 3], tok[:, 3], ACT.Exp).then_inc(tok_act, 1)
            fn(glast[:, 0:3], glast[:, 0:3], ACT.Exp).then_inc(tok_act, 1)
            units("a_in", evac_z, 25, 27)
            length(1)
            units("a_in", evac_z, 27, 29)
            act.wait_ge(tokx_done, 2)
            for ci, (c0, cn) in enumerate(CHUNKS):
                ins = fn(toks[0:cn, ci], banks[6][0:cn, ci * 5 * HN:(ci + 1) * 5 * HN]
                         .rearrange("p (j h) -> p j h", j=5), ACT.Copy)
            ins.then_inc(toks_ready, 1)
            fn(glb[:], banks[7][:, 0:4 * HN].rearrange("p (h c) -> p h c", h=HN)[:, :, 0:3], ACT.Copy).then_inc(toks_ready, 1)
            nc.scalar.preload_act_table(ACT.Exp)

            def decays(c):
                cn = CHUNKS[c][1]
                act.wait_ge(pre_used, 4 * c + G_ROWS + 1)
                fn(cb[c]["dd"][0:cn], cb[c]["dd"][0:cn], ACT.Exp).then_inc(dcy_exp, 1)

            def values(c):
                cn = CHUNKS[c][1]
                act.wait_ge(pre_done, 5 * c + V_TOK + 1)
                for heads, src in octet(stage_banks(c, V_TOK), P, cn):
                    for i in range(4):
                        hh = heads.start + i
                        ins = fn(cb[c]["vb"][0:cn, hh], src[:, i], ACT.Identity, scale=toks[0:cn, c, 0, hh:hh + 1])
                ins.then_inc(vb_ready, 1)

            units("a_in", evac_z, 29, 30)
            decays(0)
            units("a_in", evac_z, 30, 32)
            for c in range(3):
                if c:
                    decays(c)
                values(c)
            act.wait_ge(banks_free, out_of("a_in"))
            fn(sz[:], sz[:], ACT.Silu).then_inc(sz_ready, 1)

            def flipped(c, dst, n):
                cn = CHUNKS[c][1]
                act.wait_ge(ut_done, n + 1)
                heads, src = octet(INV[c][1], cn, cn)[0]
                fn(cb[c][dst][0:cn, heads], src, ACT.Copy).then_inc(u_ready_act, 1)

            for c in range(3):
                flipped(c, "tt", c)
            for lv in range(1, LOG2P):
                now = [c for c in range(3) if (lv, c) in STEP]
                for c in now:
                    cn = CHUNKS[c][1]
                    act.wait_ge(y_done, STEP[lv, c] + 1)
                    _, src = octet((INV[c][0],), cn // 2, cn)[0]
                    fn(cb[c]["yy"][0:cn], src, ACT.Copy).then_inc(y_ready, 1)
                for c in now:
                    flipped(c, "uu", 3 + STEP[lv, c])
            def norm_root(j, tk):
                act.wait_ge(onorm_ms, j + 1)
                fn(tok[:, 5, tk], tok[:, 5, tk], ACT.Sqrt, bias=eps6[0:HN, 0:1], scale=1 / P).then_inc(onorm_std, 1)

            nc.scalar.preload_act_table(ACT.Sqrt)
            for c, (c0, cn) in enumerate(CHUNKS):
                act.wait_ge(vn_done, c + 1)
                heads, src = octet((0, 1), P, cn)[0]
                fn(vnews[c][0:cn, heads], src, ACT.Copy).then_inc(vnew_act, 1)
                if c < 2:
                    cn1 = CHUNKS[c + 1][1]
                    act.wait_ge(wt_done, c + 1)
                    for heads, src in octet((4, 5), cn1, P):
                        ins = fn(cb[c + 1]["tt"][:, heads], src, ACT.Copy, scale=-1.0)
                    ins.then_inc(wt_ready, 1)
                if c == 2:
                    norm_root(0, slice(0, N1))
                act.wait_ge(ov_done, c + 1)
                for heads, src in octet((2, 3), cn, P):
                    ins = fn(on[:, heads, c0:c0 + cn], src, ACT.Copy)
                ins.then_inc(ov_taken, 1)
                act.wait_ge(ov_taken, c + 1)
                fn(osq2[:, :, c0:c0 + cn], on[:, :, c0:c0 + cn], ACT.Square).then_inc(onorm_sq, 1)
            norm_root(1, slice(N1, N2))
            act.wait_ge(on_used, 5)
            for k in range(KD):
                fn(a_hi[:, k, 0:N2], on[:, k], ACT.Copy).then_inc(split_hi, 1)

            def square_shifted(i):
                for k in range(4):
                    act.wait_ge(cent_ready, 8 * (i - LN0) + k + 1)
                    fn(sq[:, k], h[:, k], ACT.Square).then_inc(sq_ready, 1)

            def square_h(name):
                def after(t):
                    act.wait_ge(banks_free, t + (TILE0[name] + 5))
                    fn(sq[:, ds(t, 1)], h[:, ds(t, 1)], ACT.Square).then_inc(sq_ready, 1)
                return after

            def deviation(i):
                act.wait_ge(mean_ready, 2 * (i - LN0) + 2)
                fn(rstd[:, 0:N2], banks[4][:, 0:N2], ACT.Square).then_inc(mean_sq, 1)
                fn(part_sum[:], banks[4][:, 0:N2], ACT.Copy).then_inc(mean_out, 1)
                act.wait_ge(var_ready, i - LN0 + 1)
                fn(rstd[:, 0:N2], rstd[:, 0:N2], ACT.Sqrt, bias=eps6[:, 1:2]).then_inc(std_ready, 1)

            lin("a_out", None, (0, 1))
            square_shifted(LN0)
            lin("a_out", None, (1, 2), square_h("a_out"))
            deviation(LN0)
            split(S_LN0, a_of(N2), h, normed, 16, lambda k: column("ln_mix_b", k))
            ffn(1, N2, ACT.Silu, PV["conv2_w"] + 2 * KF, None)
            nc.scalar.preload_act_table(ACT.Sqrt)
            down(1, None, (0, 1))
            square_shifted(LN0 + 1)
            down(1, square_h("down1"), (1, 2))
            deviation(LN0 + 1)
            split(S_LN1, a_of(N2), h, normed, 24, lambda k: column("ln_ffn_b", k))
            u0 = UNIT0["b_cx"]

            with act.Fori(0, 4) as it:
                for s in range(SLOTS):
                    act.wait_ge(unit_used, it * 4 + (u0 + s + 1))
                    act.wait_ge(p_used, it * 2 + (s // 2 + 1))
                    fn((abuf if s % 2 == 0 else vbuf)[:, s // 2], banks[s][:, 0:N2], ACT.Copy).then_inc(banks_free, 1)
                    round_unit(it * 4 + (u0 + s + 4), s)

            def round_u(t):
                act.wait_ge(banks_free, t + (TILE0["b_b"] + 5))
                fn(u_hi[:, ds(t, 1)], ucv[:, ds(t, 1)], ACT.Copy).then_inc(split_hi, 1)

            lin("b_b", None, after=round_u)
            nc.scalar.preload_act_table(ACT.Sqrt)
            lin("b_out", None, (0, 1))
            square_shifted(LN0 + 2)
            lin("b_out", None, (1, 2), square_h("b_out"))
            deviation(LN0 + 2)
            split(S_LN2, a_of(N2), h, normed, 32, lambda k: column("ln_mix_b", 8 + k))
            ffn(2, N2, ACT.Silu, PV["conv2_w"] + 5 * KF, None)
            nc.scalar.preload_act_table(ACT.Sqrt)
            down(2, None, (0, 1))
            square_shifted(LN0 + 3)
            down_end(2, square_h("down2"))
            deviation(LN0 + 3)
            for k in range(KD):
                act.wait_ge(normed, 40 + k + 1)
                ins = fn(h[:, k], h[:, k], ACT.Identity, bias=column("ln_ffn_b", 8 + k))
                if k % 2:
                    ins.then_inc(out_ready, 1)

        @block.vector
        def _(dve):
            v = nc.vector
            dve_n = [0]

            def link(ins):
                dve_n[0] += 1
                ins.then_inc(dve_seq, 1)
                dve.wait_ge(dve_seq, dve_n[0])

            def lanes(ap, k):
                return ap.unsqueeze(1).broadcast_to([ap.shape[0], k, ap.shape[-1]])

            def col(name, i):
                return pv[:, PV[name] + i:PV[name] + i + 1]

            def remainder(i, k, ops, src, shift=None):
                dve.wait_ge(split_hi, k + (8 * i + 1))
                tile = ds(k, 1)
                hi, lo = ops[0][:, tile].bitcast(F32), ops[1][:, tile]
                if shift is None:
                    ins = v.tensor_tensor(lo, src, hi, ALU.subtract)
                else:
                    ins = v.scalar_tensor_tensor(lo, src, shift, hi, ALU.add, ALU.subtract)
                ins.then_inc(split_ready, 1)

            def whole_of(n):
                return (a_hi[:, :, 0:n], a_lo[:, :, 0:n])

            def inverse(i, n):
                dve.wait_ge(std_ready, i + 1)
                link(v.reciprocal(rstd[:, 0:n], rstd[:, 0:n]))

            def normalise(i, y, n, ops, of, shift=None, gain=None):
                for k in range(KD + 1):
                    if k < KD:
                        if gain is None:
                            ins = v.tensor_tensor(y[:, k], y[:, k], rstd[:, 0:n], ALU.mult)
                        else:
                            ins = v.scalar_tensor_tensor(y[:, k], y[:, k], gain(k), rstd[:, 0:n], ALU.mult, ALU.mult)
                        ins.then_inc(normed, 1)
                    if k:
                        remainder(i, k - 1, ops, of[:, k - 1:k], shift and shift(k - 1))

            def sum_squares(i, squares):
                for k in range(1, KD):
                    dve.wait_ge(sq_ready, 8 * i + k + 1)
                    if k > 1:
                        dve.wait_ge(sum_seq, 6 * i + k - 1)
                    ins = v.tensor_tensor(squares[:, 0], squares[:, 0], squares[:, k], ALU.add)
                    ins.then_inc(sum_seq if k < KD - 1 else sum_ready, 1)

            def one_over(i, c):
                dve.wait_ge(std_ready, i + 1)
                link(v.reciprocal(c, c))

            r_ctx, r_x = rstd[:, N1:2 * N1], rstd[:, 0:N1]
            sum_squares(RMS_CTX, sq[:, :, 0:N1])
            one_over(RMS_CTX, r_ctx)
            sum_squares(RMS_X, sqx[:, :, 0:N1])
            v.tensor_tensor(ctxt[:], ctxt[:], lanes(r_ctx, KD), ALU.mult).then_inc(xr_ready, 1)
            one_over(RMS_X, r_x)
            v.tensor_tensor(xr[:], x[:], lanes(r_x, KD), ALU.mult).then_inc(xr_ready, 1)
            dve.wait_ge(first_in, 64)
            dve.wait_ge(xr_ready, 2)
            b_ada = pv[:, PV["b_ada"]:PV["b_ada"] + 16].rearrange("p (s k) -> p s k", s=2)
            for j in range(4):
                dve.wait_ge(mod_flipped, j + 1)
                for part in range(2):
                    ins = v.tensor_tensor(mod[:, :, 8 * part + 2 * j:8 * part + 2 * j + 2].rearrange("p j k -> p k j"),
                                          banks[2 + j % 2][:, 4 * part:4 * part + 4].rearrange("p (k j) -> p k j", j=2),
                                          b_ada[:, part, 2 * j:2 * j + 2].unsqueeze(2).broadcast_to([P, 2, 2]), ALU.add)
                ins.then_inc(mod_taken, 1)
                dve.wait_ge(mod_taken, j + 1)
                v.scalar_tensor_tensor(gain[:, 0:2, 2 * j:2 * j + 2], mod[:, :, 8 + 2 * j:10 + 2 * j], 1.0,
                                       lanes(pv[:, PV["norm1_g"] + 2 * j:PV["norm1_g"] + 2 * j + 2], 2), ALU.add, ALU.mult) \
                    .then_inc(gain_ready, 1)
                dve.wait_ge(gain_ready, j + 1)
                for k in (2 * j, 2 * j + 1):
                    for jj, src in enumerate((xr, ctxt)):
                        ins = v.tensor_scalar(hfull[:, k, jj * N1:(jj + 1) * N1], src[:, k], gain[:, jj, k:k + 1],
                                              mod[:, jj, k:k + 1], ALU.mult, ALU.add)
                    ins.then_inc(full_ready, 1)
                for k in (2 * j, 2 * j + 1):
                    dve.wait_ge(full_ready, k + 1)
                    remainder(S_X, k, whole, hfull[:, k:k + 1])

            dve.wait_ge(wlr_ready, 1)
            v.tensor_tensor(wlr_lo[:], wlr[:], wlr_hi[:].bitcast(F32), ALU.subtract).then_inc(wlr_rest, 1)
            mid, last = slice(2 * RANK, 4 * RANK), slice(4 * RANK, 6 * RANK)
            dve.wait_ge(lr_hi, 1)
            v.tensor_tensor(lrs[mid], banks[6][mid, :], lrs[mid].bitcast(F32), ALU.subtract).then_inc(lr_ready, 1)
            dve.wait_ge(w2_ready, 1)
            v.tensor_tensor(w2s[last], w2[last], w2s[last].bitcast(F32), ALU.subtract).then_inc(w2_split, 1)
            link(v.memset(reset[:], 1.0))
            link(v.memset(reset[:].rearrange("p (c t) -> p c t", t=GC)[:, :, 0:1], 0.0))
            for i in range(2 * HG):
                d, hh = divmod(i, HG)
                dve.wait_ge(z_done, i + 1)
                v.tensor_scalar(la[:, d, hh], banks[4 + i % 4][:, :], col("gla_b2", i), None, ALU.add).then_inc(t_ready, 1)
            dve.wait_ge(log_ready, 1)
            link(v.scalar_tensor_tensor(la[:], la[:], 0.0, ebuf[:], ALU.min, ALU.subtract))
            for d in range(2):
                src = la[:, d].rearrange("p h t -> p (h t)")
                dst = ebuf[:, d].rearrange("p h t -> p (h t)")
                if d:
                    src, dst = src[:, ::-1], dst[:, ::-1]
                v.tensor_tensor_scan(dst, reset[:], src, 0.0, ALU.mult, ALU.add).then_inc(decay_ready, 1)

            def modulations(p0, p1, ring):
                with dve.Fori(p0 // 2, p1 // 2) as it:
                    for s in range(2):
                        dve.wait_ge(row_in[2 * ring + s], it * 16 + (16 - 8 * p0))
                        for t in range(2):
                            ins = v.scalar_tensor_tensor(adaw[ring][s][:, t], adaw[ring][s][:, t], 1.0, csil[:], ALU.mult,
                                                         ALU.mult, accum_out=mod[:, 0, ds(it * 4 + (2 * s + t + 16), 1)])
                        ins.then_inc(row_used, 1)

            dve.wait_ge(decay_ready, 2)
            v.memset(kmul[:], 1.0)
            v.memset(qmul[:], 1.0).then_inc(masks_ready, 1)
            v.memset(sc_full[0][:], 0.0).then_inc(sc_clear, 1)
            def differences(d):
                flat = ebuf[:, d].rearrange("p h (c t) -> p (h c) t", t=GC)
                last = (flat[:, :, GC - 1:GC] if d == 0 else flat[:, :, 0:1]).broadcast_to([P, HG * 8, GC])
                if d:
                    dve.wait_ge(sc_done, 2)
                    dve.wait_ge(ks_ready, 1)
                v.tensor_tensor(kd[:].rearrange("p h (c t) -> p (h c) t", t=GC), last, flat, ALU.subtract) \
                    .then_inc(diff_ready, 1)

            def per_chunk(ap, n):
                return ap.rearrange("p h c -> p (h c)").unsqueeze(2).broadcast_to([P, HG * n, GC])

            def by_chunk(ap):
                return ap[:, :, :].rearrange("p h (c t) -> p h c t", t=GC)

            def chunks_of(ap):
                return ap.rearrange("p h (c t) -> p (h c) t", t=GC)

            def operands(d):
                e = (1, 2, 3, 4) if d == 0 else (5, 6, 7, 8)
                dve.wait_ge(exps_ready, e[0])
                v.tensor_tensor(qd[d][:], q1[:], qd[d][:], ALU.mult).then_inc(qk_ready, 1)
                dve.wait_ge(exps_ready, e[1])
                v.tensor_tensor(ki[d][:], k1[:, :, 0:N1], ki[d][:], ALU.mult).then_inc(qk_ready, 1)
                dve.wait_ge(exps_ready, e[2])
                dve.wait_ge(masks_ready, 1)
                early, late = slice(d, 4, 2), slice(1 - d, 4, 2)
                v.tensor_copy(qmul[:, d, :, late], dec[:, d, :, early])
                v.tensor_copy(kmul[:, d, :, early], dec[:, d, :, late])
                v.tensor_tensor(bdec[:, d], dec[:, d, :, early], dec[:, d, :, late], ALU.mult)
                c = (4, 5, 6, 7) if d == 0 else (7, 6, 5, 4)
                link(v.tensor_copy(kmul[:, d, :, c[2]], dec[:, d, :, c[3]]))
                for i in (1, 0):
                    link(v.tensor_tensor(kmul[:, d, :, c[i]], kmul[:, d, :, c[i + 1]], dec[:, d, :, c[i + 1]], ALU.mult))
                v.tensor_tensor(by_chunk(qs[d]), by_chunk(qd[d]), qmul[:, d].unsqueeze(3).broadcast_to([P, HG, 4, GC]), ALU.mult)
                dve.wait_ge(exps_ready, e[3])
                v.tensor_tensor(kd[:], kd[:], k1[:], ALU.mult).then_inc(kd_ready, 1)
                dve.wait_ge(kd_ready, d + 1)
                if d:
                    dve.wait_ge(kt_done, 4)
                v.tensor_tensor(chunks_of(ks[:]), chunks_of(kd[:]), per_chunk(kmul[:, d], 8), ALU.mult) \
                    .then_inc(ks_ready, 1)

            def scores(d):
                for blk in range(2):
                    dve.wait_ge(sc_done, 2 * d + blk + 1)
                    for hh in range(HG):
                        ins = v.copy_predicated(sc(d, blk, hh), gla_masks[:, d], banks[6 + blk][:, hh * P:(hh + 1) * P])
                    ins.then_inc(sc_ready, 1)

            def second_state(d):
                dve.wait_ge(st0_ready, d + 1)
                dve.wait_ge(up_done, 2 * d + 2)
                for hh in range(HG):
                    ins = v.scalar_tensor_tensor(st1[d][:, hh], st0[d][:, hh], bdec[:, d, hh, d:d + 1],
                                                 banks[4 + hh // 2][:, (hh % 2) * DV:(hh % 2 + 1) * DV], ALU.mult, ALU.add)
                ins.then_inc(st1_ready, 1)

            def layer_norm_stats():
                dve.wait_ge(banks_free, out_of("w_vs"))
                for n in range(2):
                    for c in range(2):
                        ins = v.bn_stats(stats[:, n, c], vs[:, n, c * 512:(c + 1) * 512])
                    link(ins)
                    v.bn_aggr(mv[:, n, 0:2], stats[:, n]).then_inc(vs_var, 1)

            differences(0)
            dve.wait_ge(csil_ready, 2)
            modulations(0, 4, 0)
            operands(0)
            dve.wait_ge(banks_free, out_of("w_v"))
            v.memset(sc_full[1], 0.0).then_inc(sc_clear, 1)
            scores(0)
            differences(1)
            second_state(0)
            operands(1)
            layer_norm_stats()
            scores(1)
            second_state(1)
            of = o1[:].rearrange("p h v t -> p (h v) t")
            dve.wait_ge(vs_std, 2)
            for n in range(2):
                ins = v.reciprocal(mv[:, n, 3:4], mv[:, n, 2:3])
            link(ins)
            dve.wait_ge(sgu_in, 64)
            for n in range(2):
                link(v.tensor_scalar(vs[:, n], vs[:, n], mv[:, n, 0:1], mv[:, n, 3:4], ALU.subtract, ALU.mult))
                link(v.tensor_tensor(vs[:, n], vs[:, n], rows[:, 0], ALU.mult))
                v.tensor_tensor(vs[:, n], vs[:, n], rows[:, 1], ALU.add).then_inc(vn_ready, 1)
            dve.wait_ge(ks_ready, 2)
            for i in range(4):
                blk, pair = divmod(i, 2)
                dve.wait_ge(o_done, i + 1)
                v.tensor_copy(of[:, 4 * pair:4 * pair + 4, blk * P:(blk + 1) * P],
                              banks[4 + i][:, :].rearrange("p (h t) -> p h t", t=P)).then_inc(o_taken, 1)
            dve.wait_ge(banks_free, out_of("w_u"))
            for n in range(2):
                for half in range(2):
                    dve.wait_ge(sgu_done, 2 * n + half + 1)
                    gs = slice(4 * half, 4 * half + 4)
                    buf = mixed[:]
                    if n or half:
                        dve.wait_ge(mixed_used, 2 * n + half)
                    link(v.tensor_tensor(buf, quad(banks[4 + 2 * n + half], P),
                                         rows[:, 2].rearrange("p (g t) -> p g t", g=8)[:, gs], ALU.add))
                    v.tensor_tensor(gu[:, gs, n * P:(n + 1) * P], gu[:, gs, n * P:(n + 1) * P], buf, ALU.mult) \
                        .then_inc(mixed_used, 1)
            dve.wait_ge(mixed_used, 4)
            dve.sem_inc(gated, 8)
            modulations(4, 8, 1)
            for k in range(KD):
                remainder(S_GU, k, half1, gu[:, k:k + 1])
            dve.wait_ge(banks_free, out_of("w_r"))
            for b in range(2):
                hs = slice(2 * b, 2 * b + 2)
                dve.wait_ge(ostd_ready, b + 1)
                link(v.reciprocal(orstd[:, hs], orstd[:, hs]))
                for half in range(2):
                    ins = v.tensor_tensor(o1[:, hs, half], o1[:, hs, half], orstd[:, hs], ALU.mult)
                link(ins)
                for k in range(4 * b, 4 * b + 4):
                    v.scalar_tensor_tensor(of[:, k], of[:, k], col("gla_norm_g", k), sr[:, k], ALU.mult, ALU.mult) \
                        .then_inc(ob_ready, 1)
            modulations(8, 16, 2)
            dve.wait_ge(row_used, 16)
            link(v.tensor_tensor(mod[:, 0, 16:48], mod[:, 0, 16:48], pv[:, PV["b_ada"] + 16:PV["b_ada"] + 48], ALU.add))
            link(v.scalar_tensor_tensor(gain[:, 2], mod[:, 0, 32:40], 1.0, pv[:, PV["norm2_g"]:PV["norm2_g"] + KD],
                                        ALU.add, ALU.mult))

            def begin_sum():
                v.memset(part_sum[:], 0.0).then_inc(part_seq, 1)

            def add_to_sum(q, t, s, src):
                if s < 3:
                    dve.wait_ge(part_seq, t + (9 * q + 1))
                    part = part_sum[:, 0:src.shape[-1]].unsqueeze(1)
                    v.tensor_tensor(part, part, src, ALU.add).then_inc(part_seq, 2 if s == 2 else 1)

            def lin(name, take):
                u0 = UNIT0[name]
                with dve.Fori(0, TILES_OF[name] // 4) as it:
                    for s in range(SLOTS):
                        dve.wait_ge(unit_used, it * 4 + (u0 + s + 1))
                        take(it * 4 + s, s)

            def down(name, take):
                u0 = UNIT0[name]
                with dve.Fori(0, 2) as it:
                    for j in range(4):
                        dve.wait_ge(unit_used, it * 12 + (u0 + 3 * j + 3))
                        take(it * 4 + j, j)

            for k in range(KD):
                remainder(S_O, k, half0, of[:, k:k + 1])
            lin("w_br_a", lambda t, s: v.tensor_tensor(ga[:, ds(t, 1)], banks[s][:, 0:N1].unsqueeze(1), ga[:, ds(t, 1)],
                                                       ALU.mult).then_inc(banks_free, 1))

            def merge(t, s):
                v.tensor_tensor(gb[:, ds(t, 1)], banks[s][:, 0:N1].unsqueeze(1), gb[:, ds(t, 1)], ALU.mult) \
                    .then_inc(banks_free, 1)
                dve.wait_ge(banks_free, t + (TILE0["w_br_b"] + 5))
                v.tensor_tensor(gb[:, ds(t, 1)], gb[:, ds(t, 1)], ga[:, ds(t, 1)], ALU.add).then_inc(merged, 1)
                remainder(S_MERGED, t, half1, gb[:, ds(t, 1)])

            lin("w_br_b", merge)

            def residual(i, name, j, dst, gains):
                def take(t, s):
                    v.scalar_tensor_tensor(x[:, ds(t, 1)], banks[s][:, 0:N1].unsqueeze(1), mod[:, 0, ds(t + j * KD, 1)],
                                           x[:, ds(t, 1)], ALU.mult, ALU.add).then_inc(banks_free, 1)
                    dve.wait_ge(banks_free, t + (TILE0[name] + 5))
                    v.tensor_scalar(dst[:, ds(t, 1)], x[:, ds(t, 1)], gains[:, ds(t, 1)], None, ALU.mult)
                    if s < 3:
                        dve.wait_ge(sq_ready, t + (8 * i + 1))
                        add_to_sum(i - RMS_F, t, s, sq[:, ds(t, 1), 0:N1])

                begin_sum()
                return take

            hx = h[:, :, 0:N1]
            lin("w_o", residual(RMS_F, "w_o", 2, hx, gain[:, 2]))
            inverse(RMS_F, N1)
            normalise(S_F, hx, N1, half0, hx, lambda k: mod[:, 0, 24 + k:25 + k])

            def ffn(i, n, taps):
                t0, j0, nt = TILE0[f"up{i}"], KF * i, len(taps)
                c0 = conv_links[0]
                conv_links[0] += KF * (nt - 1)
                with dve.Fori(0, KF // 2) as it:
                    for m, (w, to, frm) in enumerate(taps):
                        for p in range(2):
                            if m == 0:
                                dve.wait_ge(banks_free, it * 4 + (t0 + 2 * p + 5))
                            else:
                                dve.wait_ge(conv_seq, it * (2 * (nt - 1)) + (c0 + 2 * (m - 1) + p + 1))
                            dst = to(cbuf[:, p, 0:n])
                            v.scalar_tensor_tensor(dst, frm(abuf[:, p, 0:n]), pv[:, ds(it * 2 + (w + p), 1)], dst,
                                                   ALU.mult, ALU.add) \
                                .then_inc(conv_done if m == nt - 1 else conv_seq, 1)
                    for p in range(2):
                        dve.wait_ge(act_done, it * 2 + (j0 + p + 1))
                        v.tensor_tensor(gfull[:, p, 0:n], gbuf[:, p, 0:n], vbuf[:, p, 0:n], ALU.mult).then_inc(glu_done, 1)
                    for p in range(2):
                        dve.wait_ge(glu_done, it * 2 + (j0 + p + 1))
                        v.tensor_copy(g_hi[:, ds(it * 2 + p, 1), 0:n], gfull[:, p:p + 1, 0:n]).then_inc(g_rounded, 1)
                    for p in range(2):
                        dve.wait_ge(g_rounded, it * 2 + (j0 + p + 1))
                        jj = ds(it * 2 + p, 1)
                        v.tensor_tensor(g_lo[:, jj, 0:n], gfull[:, p:p + 1, 0:n], g_hi[:, jj, 0:n].bitcast(F32),
                                        ALU.subtract).then_inc(g_ready, 1)

            conv_links = [0]

            def image_tap(dy, dx):
                rows_, w = N1 // GRID, GRID
                y0, y1 = max(0, 1 - dy), rows_ - max(0, dy - 1)
                x0, x1 = max(0, 1 - dx), w - max(0, dx - 1)

                def view(ap, sy, sx):
                    return ap.rearrange("p (y x) -> p y x", x=w)[:, y0 + sy:y1 + sy, x0 + sx:x1 + sx]

                return (PV["conv1_w"] + (3 * dy + dx) * KF, lambda ap: view(ap, 0, 0),
                        lambda ap: view(ap, dy - 1, dx - 1))

            ffn(0, N1, [image_tap(dy, dx) for dy in range(3) for dx in range(3) if (dy, dx) != (1, 1)])
            hx = h[:, :, META:]
            down("down0", residual(RMS_END, "down0", 5, hx, pv[:, PV["final_g"]:PV["final_g"] + KD]))
            inverse(RMS_END, N1)
            dve.wait_ge(h_in, 16)
            normalise(S_H, hx, N1, whole_of(N2), h)

            def causal(w, shift, n=N2):
                return (w, lambda ap: ap[:, shift:n], lambda ap: ap[:, 0:n - shift])

            t0 = TILE0["a_in"]
            with dve.Fori(0, 6) as it:
                for m in range(3):
                    for s in range(SLOTS):
                        if m == 0:
                            dve.wait_ge(banks_free, it * 4 + (t0 + s + 5))
                        else:
                            dve.wait_ge(conv4_seq, it * 8 + (4 * (m - 1) + s + 1))
                        dst = convc[:, s, 3 - m:N2]
                        v.scalar_tensor_tensor(dst, conva[:, s, 0:N2 - 3 + m],
                                               pv[:, ds(it * 4 + (PV["a_conv"] + 24 * m + s), 1)], dst, ALU.mult, ALU.add) \
                            .then_inc(conv4_done if m == 2 else conv4_seq, 1)
            link(v.memset(tokm[:], 1.0))
            v.memset(glast[:, 3:4], 0.0)
            for c0, _ in CHUNKS:
                ins = v.memset(tokm[:, c0:c0 + 1], 0.0)
            link(ins)
            dve.wait_ge(tok_act, 4)
            link(v.scalar_tensor_tensor(tok[:, 5], tok[:, 1], 0.0, tok[:, 5], ALU.max, ALU.add))
            link(v.tensor_scalar(tok[:, 5], tok[:, 5], hb[:, 2:3], -1.0, ALU.mult, ALU.mult))
            link(v.tensor_tensor_scan(tok[:, 1], tokm[:], tok[:, 5], 0.0, ALU.mult, ALU.add))
            for ci, (c0, cn) in enumerate(CHUNKS):
                ins = v.tensor_copy(glast[:, ci:ci + 1], tok[:, 1, c0 + cn - 1:c0 + cn])
            link(ins)
            for ci, (c0, cn) in enumerate(CHUNKS):
                ins = v.tensor_scalar(tok[:, 3, c0:c0 + cn], tok[:, 1, c0:c0 + cn], glast[:, ci:ci + 1], -1.0,
                                      ALU.subtract, ALU.mult)
            ins.then_inc(gcum_ready, 1)
            dve.wait_ge(tok_act, 7)
            dve.wait_ge(qstd_ready, 1)
            link(v.reciprocal(tok[:, 8], tok[:, 7]))
            link(v.tensor_tensor(tok[:, 8], tok[:, 8], tok[:, 8], ALU.mult))
            link(v.tensor_tensor(tok[:, 8], tok[:, 8], tok[:, 0], ALU.mult))
            v.tensor_tensor(glsp[:], glast[:].unsqueeze(1).broadcast_to([HN, HN, 4]),
                            ident[0:HN, 0:HN].unsqueeze(2).broadcast_to([HN, HN, 4]), ALU.mult)
            v.tensor_tensor(tok[:, 3], tok[:, 3], tok[:, 8], ALU.mult).then_inc(tok_ready, 1)
            dve.wait_ge(conv4_act, 24)

            def gated_queries(h0):
                for hh in (h0, h0 + 1):
                    dve.wait_ge(bc_done, hh + 1)
                    v.tensor_tensor(qg[:, hh], qkv[:, hh], banks[hh % 4][:, 0:N2], ALU.mult).then_inc(bc_used, 1)

            dve.wait_ge(toks_ready, 2)
            for c, (_, cn) in enumerate(CHUNKS):
                B = cb[c]
                dd = B["dd"][0:cn]

                def staged(stage, width):
                    dve.wait_ge(pre_done, 5 * c + stage + 1)
                    return octet(stage_banks(c, stage), width, cn)

                def each_head(stage):
                    return [(h0.start + i, src[:, i]) for h0, src in staged(stage, cn) for i in range(4)]

                def per_token(j, hh):
                    return toks[0:cn, c, j, hh:hh + 1]

                def per_tokens(j, heads, n_):
                    return toks[0:cn, c, j, heads].unsqueeze(2).broadcast_to([cn, heads.stop - heads.start, n_])

                for hh, src in each_head(G_ROWS):
                    ins = v.scalar_tensor_tensor(dd[:, hh], src, per_token(1, hh), levels[0:cn, LOG2P, 0:cn],
                                                 ALU.subtract, ALU.add)
                ins.then_inc(pre_used, 1)
                if c == 1:
                    gated_queries(0)
                for heads, src in staged(K_TOK, P):
                    if c < 2:
                        v.tensor_tensor(B["kdc"][0:cn, heads], src, per_tokens(3, heads, P), ALU.mult)
                    ins = v.tensor_tensor(B["kbeg"][0:cn, heads], src, per_tokens(2, heads, P), ALU.mult)
                ins.then_inc(pre_used, 1)
                if c == 1:
                    gated_queries(2)
                dve.wait_ge(dcy_exp, c + 1)
                for stage, dst in ((K_K, "mt"), (K_Q, "qkd")):
                    for hh, src in each_head(stage):
                        ins = v.scalar_tensor_tensor(B[dst][0:cn, hh], src, per_token(4, hh), dd[:, hh], ALU.mult, ALU.mult)
                    ins.then_inc(pre_used, 1)
                    if c == 1:
                        gated_queries(4 if stage == K_K else 6)
            for c in (1, 2):
                cn = CHUNKS[c][1]
                uu, mt = cb[c]["uu"][0:cn], cb[c]["mt"][0:cn]
                dve.wait_ge(pre_used, 4 * c + K_K + 1)
                v.tensor_tensor(uu, mt, levels[0:cn, 0, 0:cn].unsqueeze(1).broadcast_to([cn, HN, cn]), ALU.mult) \
                    .then_inc(uu_dve, 1)
                dve.wait_ge(uu_dve, 2 * c - 1)
                v.tensor_tensor(uu, ident[0:cn, 0:cn].unsqueeze(1).broadcast_to([cn, HN, cn]), uu, ALU.subtract) \
                    .then_inc(uu_dve, 1)
            dve.wait_ge(qstd_ready, 2)
            link(v.reciprocal(tok[:, 6], tok[:, 6]))
            link(v.tensor_scalar(tok[:, 6], tok[:, 6], 128 ** -0.5, None, ALU.mult))
            link(v.tensor_tensor(tok[:, 9], tok[:, 6], tok[:, 6], ALU.mult))

            def flipped(c, dst, n_):
                if c == 2:
                    return
                cn = CHUNKS[c][1]
                dve.wait_ge(ut_done, n_ + 1)
                heads, src = octet(INV[c][1], cn, cn)[1]
                v.tensor_copy(cb[c][dst][0:cn, heads], src).then_inc(u_ready_dve, 1)

            for c in range(3):
                flipped(c, "tt", c)
            for lv in range(1, LOG2P):
                now = [c for c in range(3) if (lv, c) in STEP]
                for c in now:
                    cn = CHUNKS[c][1]
                    dve.wait_ge(ty_done, STEP[lv, c] + 1)
                    _, src = octet((INV[c][0],), cn // 2, cn)[0]
                    tt = firsts(cb[c]["tt"][0:cn], lv)
                    v.tensor_tensor(tt, tt, src.rearrange("p h (n b) -> p h n b", b=2 ** lv), ALU.subtract) \
                        .then_inc(ty_used, 1)
                for c in now:
                    flipped(c, "uu", 3 + STEP[lv, c])
            def gated_outputs(chunks, tk):
                dve.wait_ge(onorm_sq, chunks)
                dve.wait_ge(sz_ready, 1)
                link(v.scalar_tensor_tensor(on[:, :, tk], on[:, :, tk], col("a_norm", 0), sz[:, :, tk], ALU.mult, ALU.mult))

            for c, (_, cn) in enumerate(CHUNKS):
                dve.wait_ge(vn_done, c + 1)
                heads, src = octet((0, 1), P, cn)[1]
                v.tensor_copy(vnews[c][0:cn, heads], src).then_inc(vnew_dve, 1)
                if c == 2:
                    break
                dve.wait_ge(ov_done, c + 1)
                if c == 0:
                    for heads, src in octet((6, 7), P, P):
                        ins = v.tensor_copy(s2[:, heads], src)
                else:
                    decay = glb[:, :, c:c + 1].broadcast_to([P, HN, P])
                    link(v.tensor_tensor(s2[:], s2[:], decay, ALU.mult))
                    for heads, src in octet((6, 7), P, P):
                        ins = v.tensor_tensor(s2[:, heads], s2[:, heads], src, ALU.add)
                ins.then_inc(s2_ready, 1)
                if c == 1:
                    gated_outputs(2, slice(0, N1))
            def factor(j, tk):
                dve.wait_ge(onorm_done, j + 2)
                v.tensor_tensor(tok[:, 5, tk], banks[4 + j][0:HN, tk], tok[:, 9, tk], ALU.mult).then_inc(onorm_ms, 1)
                dve.wait_ge(onorm_std, j + 1)
                link(v.reciprocal(tok[:, 5, tk], tok[:, 5, tk]))
                last = v.tensor_tensor(tok[:, 5, tk], tok[:, 5, tk], tok[:, 6, tk], ALU.mult)
                if j:
                    link(last)
                    last = v.tensor_tensor(tok5sp[:], tok[:, 5, tk].unsqueeze(1).broadcast_to([HN, HN, N2 - N1]),
                                           ident[0:HN, 0:HN].unsqueeze(2).broadcast_to([HN, HN, N2 - N1]), ALU.mult)
                last.then_inc(onorm_r, 1)

            factor(0, slice(0, N1))
            factor(1, slice(N1, N2))
            gated_outputs(3, slice(N1, N2))
            for i in range(4):
                dve.wait_ge(ob2_done, i + 1)
                two = on[:, 2 * i:2 * i + 2, 0:N1]
                v.tensor_tensor(two, two, banks[6 + i % 2][:, :].rearrange("p (h t) -> p h t", h=2), ALU.mult) \
                    .then_inc(on_used, 1)
            dve.wait_ge(ob2_done, 5)
            v.tensor_tensor(on[:, :, N1:], on[:, :, N1:], banks[3][:, 0:HN * 16].rearrange("p (h t) -> p h t", h=HN),
                            ALU.mult).then_inc(on_used, 1)
            for k in range(KD):
                remainder(S_ON, k, whole_of(N2), on[:, k:k + 1])

            def add_to_h(i, name, units):
                j, u0, t0 = i - LN0, UNIT0[name], TILE0[name]
                first, q = LN_SUMS + 7 * j, banks[4][:, 0:N2]

                def add(t):
                    dve.wait_ge(unit_used, u0 + units * (t + 1))
                    v.scalar_tensor_tensor(h[:, t], h[:, t], ALPHA, banks[t % SLOTS][:, 0:N2], ALU.mult, ALU.add) \
                        .then_inc(banks_free, 1)

                add(0)
                add(1)
                dve.wait_ge(banks_free, t0 + 1 + 5)
                v.tensor_tensor(part_sum[:], h[:, 0], h[:, 1], ALU.add).then_inc(part_seq, 1)
                add(2)
                add(3)
                dve.wait_ge(banks_free, t0 + 3 + 5)
                dve.wait_ge(mean_ready, 2 * j + 1)
                for k in range(KD):
                    v.scalar_tensor_tensor(h[:, k], q, -4.0 if k < 4 else -4.0 / ALPHA, h[:, k], ALU.mult, ALU.add) \
                        .then_inc(cent_ready, 1)
                dve.wait_ge(cent_ready, 8 * j + 8)
                v.tensor_tensor(part_sum[:], h[:, 0], h[:, 1], ALU.add).then_inc(part_seq, 1)
                for t in range(2, 8):
                    dve.wait_ge(sq_ready, 8 * i + t)
                    if t > 2:
                        dve.wait_ge(sq_seq, 6 * j + t - 2)
                    v.tensor_tensor(sq[:, 0], sq[:, 0], sq[:, t - 1], ALU.add).then_inc(sq_seq, 1)
                    if t >= 4:
                        add(t)
                    if t < 7:
                        dve.wait_ge(banks_free, t0 + t + 5)
                        dve.wait_ge(part_seq, first + t)
                        v.tensor_tensor(part_sum[:], part_sum[:], h[:, t], ALU.add).then_inc(part_seq, 1)

            def ln(i, split, gains, shifts, first):
                j = i - LN0
                dve.wait_ge(ms_ready, i + 1)
                dve.wait_ge(mean_sq, j + 1)
                v.tensor_tensor(rstd[:, 0:N2], banks[5][:, 0:N2], rstd[:, 0:N2], ALU.subtract).then_inc(var_ready, 1)
                dve.wait_ge(mean_out, j + 1)
                for k in range(4):
                    ins = v.tensor_tensor(h[:, k], h[:, k], part_sum[:], ALU.subtract)
                link(ins)
                inverse(i, N2)

                def gained(k):
                    if k >= 4:
                        dve.wait_ge(cent_pool, 4 * j + k - 3)
                    return col(gains, first + k)

                if split is None:
                    for k in range(KD):
                        v.scalar_tensor_tensor(h[:, k], h[:, k], gained(k), rstd[:, 0:N2], ALU.mult, ALU.mult) \
                            .then_inc(normed, 1)
                    return
                normalise(split, h, N2, whole_of(N2), h, lambda k: col(shifts, first + k), gained)
                for k in range(KD):
                    ins = v.tensor_scalar(h[:, k], h[:, k], col(shifts, first + k), None, ALU.add)
                link(ins)

            add_to_h(LN0, "a_out", 1)
            ln(LN0, S_LN0, "ln_mix_g", "ln_mix_b", 0)
            conv2 = PV["conv2_w"]
            ffn(1, N2, [causal(conv2 + KF, 1), causal(conv2, 2)])
            add_to_h(LN0 + 1, "down1", 3)
            ln(LN0 + 1, S_LN1, "ln_ffn_g", "ln_ffn_b", 0)
            t0 = TILE0["b_cx"]
            with dve.Fori(0, 4) as it:
                for p in range(2):
                    dve.wait_ge(banks_free, it * 4 + (t0 + 2 * p + 6))
                    dve.wait_ge(u_seq, it * 6 + (p + 1))
                    v.tensor_tensor(pbuf[:, p], abuf[:, p], vbuf[:, p], ALU.mult).then_inc(p_used, 1)
                for m, shift in enumerate((0, 1, 2)):
                    for p in range(2):
                        w = pv[:, ds(it * 2 + (PV["b_conv"] + 8 * (2 - shift) + p), 1)]
                        dst = ucv[:, ds(it * 2 + p, 1), shift:N2]
                        src = pbuf[:, p:p + 1, 0:N2 - shift]
                        if m == 0:
                            dve.wait_ge(p_used, it * 2 + (p + 3))
                            ins = v.tensor_scalar(dst, src, w, None, ALU.mult)
                        else:
                            dve.wait_ge(u_seq, it * 6 + (2 * (m - 1) + p + 3))
                            ins = v.scalar_tensor_tensor(dst, src, w, dst, ALU.mult, ALU.add)
                        ins.then_inc(u_seq, 1)
            dve.wait_ge(u_seq, 26)

            def gate(t, s):
                v.tensor_tensor(ucv[:, ds(t, 1)], banks[s][:, 0:N2].unsqueeze(1), ucv[:, ds(t, 1)], ALU.mult) \
                    .then_inc(banks_free, 1)
                remainder(S_U, t, (u_hi, u_lo), ucv[:, ds(t, 1)])

            lin("b_b", gate)
            add_to_h(LN0 + 2, "b_out", 1)
            ln(LN0 + 2, S_LN2, "ln_mix_g", "ln_mix_b", 8)
            conv2 = PV["conv2_w"] + 3 * KF
            ffn(2, N2, [causal(conv2 + KF, 1), causal(conv2, 2)])
            add_to_h(LN0 + 3, "down2", 3)
            ln(LN0 + 3, None, "ln_ffn_g", "ln_ffn_b", 8)

    return nc


def _units(w, cols):
    k, m = w.shape
    t = w.reshape(k // P, P, m // P, P).transpose(2, 1, 0, 3)
    return t[list(cols)]


def _features(v):
    return v.reshape(-1, P).T


def _tokens(t):
    return t.T.reshape(KD, P, -1).transpose(1, 0, 2)


def _layout(i):
    f = np.asarray
    w_in = f(i["w_in"])[0]
    w_main = w_in[:, :7168]
    edge = {"w_u": 0, "w_vs": 8, "w_q": 16, "w_r": 20, "w_ga": 28, "w_gb": 36, "w_k": 44, "w_v": 48}
    tiles = {"w_u": 8, "w_vs": 8, "w_q": 4, "w_r": 8, "w_ga": 8, "w_gb": 8, "w_k": 4, "w_v": 8}
    parts = {n: _units(w_main, range(edge[n], edge[n] + tiles[n])) for n in edge}
    for n in ("w_br_a", "w_br_b", "w_o"):
        parts[n] = _units(f(i[n])[0], range(8))
    pair = [t for j in range(KF) for t in (j, KF + j)]
    parts["up0"] = _units(f(i["ffn_w_up"])[0], pair)
    a_in = f(i["a_w_in_2"])[0]
    parts["a_in"] = _units(a_in[:, :4096], range(32))
    parts["a_out"] = _units(f(i["a_w_out_2"])[0], range(8))
    b_in = f(i["b_w_in_2"])[0]
    parts["b_cx"] = _units(b_in, [t for j in range(8) for t in (8 + j, 16 + j)])
    parts["b_b"] = _units(b_in, range(8))
    parts["b_out"] = _units(f(i["b_w_out_2"])[0], range(8))
    for j in range(2):
        parts[f"up{j + 1}"] = _units(f(i["ffn_w_up_2"])[j], pair)
    d = {name: np.concatenate([parts[n] for n in names]) for name, names in STREAMS if names}
    d["down0"] = _units(f(i["ffn_w_down"])[0], range(8))
    for j in range(2):
        d[f"down{j + 1}"] = _units(f(i["ffn_w_down_2"])[j], range(8))
    d["x"], d["ctx"], d["meta"] = _tokens(f(i["x"])[0]), _tokens(f(i["ctx"])[0]), _tokens(f(i["meta_2"]))
    d["c"] = f(i["c"]).reshape(D)
    d["c2"] = np.stack([_features(f(i["c"])), _features(f(i["c_ctx"]))], axis=2)
    w_ada = f(i["w_ada"])[0]
    d["w_ada_first"] = w_ada[:, :2 * D].reshape(KD, P, 2, 4, 2 * P).transpose(3, 1, 0, 2, 4) \
        .reshape(4, P, KD, 4 * P)
    d["w_ada"] = w_ada[:, 2 * D:].T.reshape(16, 2, P, D).transpose(0, 2, 1, 3)
    d["w_lr"] = np.concatenate([w_in[:, 7168:].reshape(KD, P, 2 * RANK).transpose(1, 0, 2)] * 3, axis=2)
    d["gla_w2"] = f(i["gla_w2"])[0]
    d["sgu_w"] = f(i["sgu_w"])[0].transpose(2, 0, 1)
    d["sgu_ln_g"], d["sgu_ln_b"] = f(i["sgu_ln_g"]).reshape(D), f(i["sgu_ln_b"]).reshape(D)
    d["sgu_b"] = f(i["sgu_b"]).reshape(D)
    d["w_ba"] = a_in[:, 4096:].reshape(KD, P, 2 * HN).transpose(1, 0, 2)
    d["a_log"], d["dt_bias"] = f(i["a_log_2"]).reshape(HN, 1), f(i["a_dt_bias_2"]).reshape(HN, 1)
    vectors = {"b_ada": i["b_ada"], "norm1_g": i["norm1_g"], "norm2_g": i["norm2_g"], "gla_b2": i["gla_b2"],
               "gla_norm_g": i["gla_norm_g"], "conv1_w": i["ffn_conv_w"], "conv1_b": i["ffn_conv_b"],
               "final_g": i["final_norm_g"], "a_conv": i["a_conv_2"], "a_norm": i["a_norm_2"], "b_conv": i["b_conv_2"],
               "ln_mix_g": i["ln_mix_g_2"], "ln_mix_b": i["ln_mix_b_2"], "conv2_w": i["ffn_conv_2"],
               "ln_ffn_g": i["ln_ffn_g_2"], "ln_ffn_b": i["ln_ffn_b_2"]}
    d["pv"] = np.concatenate([_features(f(vectors[n])) for n, _ in PV_PARTS], axis=1)
    t = np.arange(P)
    d["ident"] = np.eye(P, dtype=np.float32)
    d["averages"] = np.stack([np.full((P, P), 1 / n, np.float32) for n in (D, DV, P, 1)], axis=1)
    masks = []
    for lv in range(LOG2P):
        b = 2 ** lv
        same = (t[:, None] // (2 * b)) == (t[None, :] // (2 * b))
        masks.append(same & ((t[:, None] // b) % 2 == 0) & ((t[None, :] // b) % 2 == 1))
    masks.append(np.where(t[:, None] <= t[None, :], 0.0, -1e30))
    d["levels"] = np.stack(masks, axis=1).astype(np.float32)
    d["gla_masks"] = np.stack([t[:, None] <= t[None, :], t[:, None] >= t[None, :]], axis=1).astype(np.int32)
    d["pick"] = np.repeat(np.eye(HN, dtype=np.float32)[None], P, axis=0)
    d["sel"] = np.repeat(np.eye(HN, dtype=np.float32)[:, :, None], P, axis=2)
    return {n: np.ascontiguousarray(a) for n, a in d.items()}


def kernel(**inputs):
    import concourse.bacc as bacc
    from concourse.bass_utils import run_bass_kernel_spmd

    nc = bacc.Bacc("TRN2", target_bir_lowering=False, num_devices=1)
    arrays = {f"in_{n}": a for n, a in _layout(inputs).items()}
    args = {n[3:]: nc.dram_tensor(n, a.shape, mybir.dt.from_np(a.dtype), kind="ExternalInput").ap()
            for n, a in arrays.items()}
    out = nc.dram_tensor("out_h", (P, KD, N1), F32, kind="ExternalOutput").ap()
    bass_two_blocks(nc, args, out)
    r = run_bass_kernel_spmd(nc, [arrays], core_ids=[0])
    h = np.asarray(r.results[0]["out_h"])
    return np.ascontiguousarray(h.transpose(2, 1, 0).reshape(1, N1, D))
```
